# Optimizing a Trainium2 kernel written in Bass

```python
import math
import jax, jax.numpy as jnp
from jax import lax
import numpy as np
import jax
import jax.numpy as jnp

D_MODEL = 1024
BATCH = 1
SEQ = 256
DEPTH = 2

GRID_W = 64
CTX_LEN = 256
ROPE_BASE = 10000.0
LN_EPS = 1e-5
DEEPNORM_ALPHA = (2 * DEPTH) ** 0.25
DEEPNORM_BETA = (8 * DEPTH) ** -0.25
N_EVEN = (DEPTH + 1) // 2
N_ODD = DEPTH // 2
H_A = 4
DK_A = D_MODEL // 8
DV_A = D_MODEL // 8
CHUNK_A = 128
RET_EXP_FWD = 5.0
RET_EXP_BWD = 5.5
H_B = 4
DK_B = D_MODEL // 16
DV_B = D_MODEL // 8
GLA_RANK = 16
GLA_TAU = 16.0
CHUNK_B = 64
AB_SPLITS = (H_A * DK_A, H_A * DK_A, H_A * DV_A, H_A * DV_A,
             H_B * DK_B, H_B * DK_B, H_B * DV_B, H_B * DV_B, GLA_RANK, GLA_RANK)
AB_IN = sum(AB_SPLITS)
AB_OUT = H_A * DV_A + H_B * DV_B
H_C = 8
DH_C = D_MODEL // 16
DV_C = 2 * DH_C
Q_BLOCK = 128
C_SPLITS = (H_C * 2 * DH_C, H_C * 2 * DH_C, H_C * DV_C)
C_IN = sum(C_SPLITS)
C_OUT = H_C * DV_C
LAMBDA_STD = 0.1
N_GROUPS = 4
EXPERTS_PER_GROUP = 8
N_EXPERTS = N_GROUPS * EXPERTS_PER_GROUP
TOP_K_EXPERT = 2
D_EXPERT = D_MODEL // 2
MOE_BLOCK = 128


def layer_norm(x, g, b):
    xf = x.astype(jnp.float32)
    mu = jnp.mean(xf, axis=-1, keepdims=True)
    var = jnp.mean(jnp.square(xf - mu), axis=-1, keepdims=True)
    return ((xf - mu) * lax.rsqrt(var + LN_EPS) * g + b).astype(x.dtype)

def head_norm(o, center):
    of = o.astype(jnp.float32)
    if center:
        of = of - jnp.mean(of, axis=-1, keepdims=True)
    return of * lax.rsqrt(jnp.mean(jnp.square(of), axis=-1, keepdims=True) + LN_EPS)

def split_sizes(t, sizes):
    cuts = [int(s) for s in np.cumsum(sizes)[:-1]]
    return jnp.split(t, cuts, axis=-1)

def axial_rope(rows, head_dim):
    row = jnp.repeat(jnp.arange(rows, dtype=jnp.float32), GRID_W)
    col = jnp.tile(jnp.arange(GRID_W, dtype=jnp.float32), rows)
    quarter = head_dim // 4
    inv = ROPE_BASE ** (-jnp.arange(quarter, dtype=jnp.float32) / quarter)
    ang_r = row[:, None] * inv
    ang_c = col[:, None] * inv
    ang = jnp.concatenate([ang_r, ang_r, ang_c, ang_c], axis=-1)
    return jnp.cos(ang), jnp.sin(ang)

def rope(x, cos, sin):
    a, b, c, d = jnp.split(x, 4, axis=-1)
    rot = jnp.concatenate([-b, a, -d, c], axis=-1)
    return (x * cos + rot * sin).astype(x.dtype)

def chunk_scan(q, k, v, log_a, s0, chunk, inclusive):
    bn, h, t, dk = q.shape
    dv = v.shape[-1]
    n = t // chunk

    def to_chunks(z):
        return jnp.moveaxis(z.reshape(bn, h, n, chunk, z.shape[-1]), 2, 0)

    mask = jnp.tril(jnp.ones((chunk, chunk), dtype=bool), 0 if inclusive else -1)

    def step(s, inp):
        qi, ki, vi, li = inp
        b = jnp.cumsum(li, axis=-2)
        bq = b if inclusive else b - li
        btot = b[..., -1:, :]
        qd = qi * jnp.exp(bq)
        kd = ki * jnp.exp(-b)
        att = jnp.where(mask, jnp.einsum('bhid,bhjd->bhij', qd, kd), 0.0)
        o = jnp.einsum('bhij,bhje->bhie', att, vi) + jnp.einsum('bhid,bhde->bhie', qd, s)
        kt = ki * jnp.exp(btot - b)
        s = jnp.exp(btot)[..., 0, :, None] * s + jnp.einsum('bhjd,bhje->bhde', kt, vi)
        return s, o

    s_fin, o = lax.scan(step, s0, (to_chunks(q), to_chunks(k), to_chunks(v), to_chunks(log_a)))
    return jnp.moveaxis(o, 0, 2).reshape(bn, h, t, dv), s_fin

def bidir_scan(q, k, v, la_f, la_b, s0_f, s0_b, chunk):
    q, k, v = (z.astype(jnp.float32) for z in (q, k, v))
    o_f, s_f = chunk_scan(q, k, v, la_f, s0_f, chunk, True)
    flip = lambda z: jnp.flip(z, axis=2)
    o_b, s_b = chunk_scan(flip(q), flip(k), flip(v), flip(la_b), s0_b, chunk, False)
    return o_f + flip(o_b), s_f, s_b

def ret_logdecay(exp0, like):
    gam = jnp.log1p(-jnp.exp2(-(exp0 + jnp.arange(H_A, dtype=jnp.float32))))
    return jnp.broadcast_to(gam[None, :, None, None], like.shape)

def ab_heads(z, w_in, w_lr_f, b_lr_f, w_lr_b, b_lr_b, cs):
    bn, t, _ = z.shape
    qa, ka, va, ga, qb, kb, vb, gb, lr_f, lr_b = split_sizes(z @ w_in, AB_SPLITS)
    qa = qa.reshape(bn, t, H_A, DK_A)
    ka = ka.reshape(bn, t, H_A, DK_A)
    if cs is not None:
        qa = rope(qa, *cs)
        ka = rope(ka, *cs)
    qa = qa * (DK_A ** -0.5)
    va = va.reshape(bn, t, H_A, DV_A)
    qb = qb.reshape(bn, t, H_B, DK_B) * (DK_B ** -0.5)
    kb = kb.reshape(bn, t, H_B, DK_B)
    vb = vb.reshape(bn, t, H_B, DV_B)

    def gla_logdecay(lr, w, b):
        g = (lr @ w + b).astype(jnp.float32)
        return (jax.nn.log_sigmoid(g) / GLA_TAU).reshape(bn, t, H_B, DK_B)

    la_f = gla_logdecay(lr_f, w_lr_f, b_lr_f)
    la_b = gla_logdecay(lr_b, w_lr_b, b_lr_b)
    bhtd = lambda u: jnp.swapaxes(u, 1, 2)
    return (bhtd(qa), bhtd(ka), bhtd(va), ga, bhtd(qb), bhtd(kb), bhtd(vb), gb, bhtd(la_f), bhtd(la_b))

def mixer_ab(ux, uc, w_in, w_lr_f, b_lr_f, w_lr_b, b_lr_b, gn_a, gn_b, w_out, cs, need_ctx):
    fx = ab_heads(ux, w_in, w_lr_f, b_lr_f, w_lr_b, b_lr_b, cs)
    fc = ab_heads(uc, w_in, w_lr_f, b_lr_f, w_lr_b, b_lr_b, None)
    bn = ux.shape[0]
    za = jnp.zeros((bn, H_A, DK_A, DV_A), jnp.float32)
    zb = jnp.zeros((bn, H_B, DK_B, DV_B), jnp.float32)

    def mix(f, st):
        qa, ka, va, ga, qb, kb, vb, gb, laf, lab = f
        oa, saf, sab = bidir_scan(qa, ka, va, ret_logdecay(RET_EXP_FWD, qa),
                                  ret_logdecay(RET_EXP_BWD, qa), st[0], st[1], CHUNK_A)
        ob, sbf, sbb = bidir_scan(qb, kb, vb, laf, lab, st[2], st[3], CHUNK_B)
        return (oa, ga, ob, gb), (saf, sab, sbf, sbb)

    out_c, st_c = mix(fc, (za, za, zb, zb))
    out_x, _ = mix(fx, st_c)

    def merge(oa, ga, ob, gb):
        b_, _, t_, _ = oa.shape
        ya = jnp.swapaxes(head_norm(oa, True), 1, 2).reshape(b_, t_, H_A * DV_A) * gn_a
        yb = jnp.swapaxes(head_norm(ob, False), 1, 2).reshape(b_, t_, H_B * DV_B) * gn_b
        y = jnp.concatenate([jax.nn.silu(ga.astype(jnp.float32)) * ya,
                             jax.nn.silu(gb.astype(jnp.float32)) * yb], axis=-1)
        return y.astype(ux.dtype) @ w_out

    yx = merge(*out_x)
    yc = merge(*out_c) if need_ctx else None
    return yx, yc

def c_heads(z, w_qkv, cs):
    bn, t, _ = z.shape
    q, k, v = split_sizes(z @ w_qkv, C_SPLITS)
    q = q.reshape(bn, t, H_C, 2, DH_C)
    k = k.reshape(bn, t, H_C, 2, DH_C)
    if cs is not None:
        q = rope(q, *cs)
        k = rope(k, *cs)
    return q * (DH_C ** -0.5), k, v.reshape(bn, t, H_C, DV_C)

def diff_attend(q, k, v, lam):
    s = jnp.einsum('bqhcd,bkhcd->bchqk', q, k).astype(jnp.float32)
    p = jax.nn.softmax(s, axis=-1)
    a = p[:, 0] - lam[:, None, None] * p[:, 1]
    return jnp.einsum('bhqk,bkhe->bqhe', a.astype(v.dtype), v)

def mixer_c(ux, uc, w_qkv, lq1, lk1, lq2, lk2, subln_g, w_out, lam_init, cs, need_ctx):
    qx, kx, vx = c_heads(ux, w_qkv, cs)
    qc, kc, vc = c_heads(uc, w_qkv, None)
    lam = (jnp.exp(jnp.sum(lq1 * lk1, axis=-1)) - jnp.exp(jnp.sum(lq2 * lk2, axis=-1))).astype(jnp.float32) + lam_init
    k_all = jnp.concatenate([kc, kx], axis=1)
    v_all = jnp.concatenate([vc, vx], axis=1)
    bn, t = qx.shape[:2]
    qb = jnp.moveaxis(qx.reshape(bn, t // Q_BLOCK, Q_BLOCK, H_C, 2, DH_C), 1, 0)
    ox = lax.map(lambda qi: diff_attend(qi, k_all, v_all, lam), qb)
    ox = jnp.moveaxis(ox, 0, 1).reshape(bn, t, H_C, DV_C)

    def finish(o):
        b_, t_ = o.shape[:2]
        y = head_norm(o, False).reshape(b_, t_, C_OUT) * subln_g * (1.0 - lam_init)
        return y.astype(ux.dtype) @ w_out

    yx = finish(ox)
    yc = finish(diff_attend(qc, kc, vc, lam)) if need_ctx else None
    return yx, yc

def hier_moe(z, w_grp, b_grp, w_rexp, b_rexp, w_gate, w_up, w_down):
    n, d = z.shape
    zf = z.astype(jnp.float32)
    g_logits = zf @ w_grp.astype(jnp.float32) + b_grp
    g_prob = jax.nn.softmax(g_logits, axis=-1)
    grp = jnp.argmax(g_logits, axis=-1).astype(jnp.int32)
    g_oh = jax.nn.one_hot(grp, N_GROUPS, dtype=jnp.float32)
    g_w = jnp.sum(g_prob * g_oh, axis=-1)
    e_logits = (zf @ w_rexp.astype(jnp.float32) + b_rexp).reshape(n, N_GROUPS, EXPERTS_PER_GROUP)
    e_sel = jnp.einsum('nge,ng->ne', e_logits, g_oh)
    top_v, top_i = lax.top_k(e_sel, TOP_K_EXPERT)
    comb = g_w[:, None] * jax.nn.softmax(top_v, axis=-1)
    eid = grp[:, None] * EXPERTS_PER_GROUP + top_i.astype(jnp.int32)
    na = n * TOP_K_EXPERT
    e_flat = eid.reshape(-1)
    t_flat = jnp.repeat(jnp.arange(n, dtype=jnp.int32), TOP_K_EXPERT)
    w_flat = comb.reshape(-1)
    order = jnp.argsort(e_flat)
    e_sorted = e_flat[order]
    counts = jnp.bincount(e_flat, length=N_EXPERTS)
    padded = (counts + MOE_BLOCK - 1) // MOE_BLOCK * MOE_BLOCK
    pad_end = jnp.cumsum(padded)
    pad_start = pad_end - padded
    raw_start = jnp.cumsum(counts) - counts
    dest = pad_start[e_sorted] + jnp.arange(na) - raw_start[e_sorted]
    p_rows = -(-na // MOE_BLOCK) * MOE_BLOCK + N_EXPERTS * MOE_BLOCK
    n_blocks = p_rows // MOE_BLOCK
    row_tok = jnp.full((p_rows,), n, jnp.int32).at[dest].set(t_flat[order])
    row_w = jnp.zeros((p_rows,), jnp.float32).at[dest].set(w_flat[order])
    blk_exp = jnp.minimum(jnp.searchsorted(pad_end, jnp.arange(n_blocks) * MOE_BLOCK, side='right'),
                          N_EXPERTS - 1)
    z_pad = jnp.concatenate([z, jnp.zeros((1, d), z.dtype)], axis=0)
    xs = z_pad[row_tok].reshape(n_blocks, MOE_BLOCK, d)

    def run(args):
        xb, e = args
        h = jax.nn.silu(xb @ w_gate[e]) * (xb @ w_up[e])
        return h @ w_down[e]

    ys = lax.map(run, (xs, blk_exp)).reshape(p_rows, d)
    out = jnp.zeros((n + 1, d), z.dtype).at[row_tok].add(ys * row_w[:, None].astype(z.dtype))
    return out[:n]

def first_inputs(seed: int = 0) -> dict:
    key = jax.random.key(seed)
    ks = iter(jax.random.split(key, 40))
    nrm = lambda shape, scale: jax.random.normal(next(ks), shape, jnp.float32) * scale
    gain = lambda shape: 1.0 + nrm(shape, 0.05)
    d = D_MODEL
    return {
        'x': nrm((BATCH, SEQ, d), 1.0),
        'c': nrm((BATCH, d), 1.0),
        'ctx': nrm((BATCH, CTX_LEN, d), 1.0),
        'c_ctx': nrm((d,), 1.0),
        'ada_w': nrm((DEPTH, d, 6 * d), 0.5 * d ** -0.5),
        'ada_b': nrm((DEPTH, 6 * d), 0.01),
        'ln1_g': gain((DEPTH, d)),
        'ln1_b': nrm((DEPTH, d), 0.01),
        'ln2_g': gain((DEPTH, d)),
        'ln2_b': nrm((DEPTH, d), 0.01),
        'ab_w_in': nrm((N_EVEN, d, AB_IN), d ** -0.5),
        'ab_w_lr_f': nrm((N_EVEN, GLA_RANK, H_B * DK_B), GLA_RANK ** -0.5),
        'ab_b_lr_f': nrm((N_EVEN, H_B * DK_B), 0.01),
        'ab_w_lr_b': nrm((N_EVEN, GLA_RANK, H_B * DK_B), GLA_RANK ** -0.5),
        'ab_b_lr_b': nrm((N_EVEN, H_B * DK_B), 0.01),
        'ab_gn_a': gain((N_EVEN, H_A * DV_A)),
        'ab_gn_b': gain((N_EVEN, H_B * DV_B)),
        'ab_w_out': nrm((N_EVEN, AB_OUT, d), DEEPNORM_BETA * AB_OUT ** -0.5),
        'c_w_qkv': nrm((N_ODD, d, C_IN), d ** -0.5),
        'c_lq1': nrm((N_ODD, H_C, DH_C), LAMBDA_STD),
        'c_lk1': nrm((N_ODD, H_C, DH_C), LAMBDA_STD),
        'c_lq2': nrm((N_ODD, H_C, DH_C), LAMBDA_STD),
        'c_lk2': nrm((N_ODD, H_C, DH_C), LAMBDA_STD),
        'c_subln_g': gain((N_ODD, C_OUT)),
        'c_w_out': nrm((N_ODD, C_OUT, d), DEEPNORM_BETA * C_OUT ** -0.5),
        'moe_w_grp': nrm((DEPTH, d, N_GROUPS), d ** -0.5),
        'moe_b_grp': nrm((DEPTH, N_GROUPS), 0.01),
        'moe_w_rexp': nrm((DEPTH, d, N_EXPERTS), d ** -0.5),
        'moe_b_rexp': nrm((DEPTH, N_EXPERTS), 0.01),
        'moe_w_gate': nrm((DEPTH, N_EXPERTS, d, D_EXPERT), d ** -0.5),
        'moe_w_up': nrm((DEPTH, N_EXPERTS, d, D_EXPERT), d ** -0.5),
        'moe_w_down': nrm((DEPTH, N_EXPERTS, D_EXPERT, d), DEEPNORM_BETA * D_EXPERT ** -0.5),
    }

def first_block(x, c, ctx, c_ctx, ada_w, ada_b, ln1_g, ln1_b, ln2_g, ln2_b,
              ab_w_in, ab_w_lr_f, ab_b_lr_f, ab_w_lr_b, ab_b_lr_b, ab_gn_a, ab_gn_b, ab_w_out,
              c_w_qkv, c_lq1, c_lk1, c_lq2, c_lk2, c_subln_g, c_w_out,
              moe_w_grp, moe_b_grp, moe_w_rexp, moe_b_rexp, moe_w_gate, moe_w_up, moe_w_down):
    bn, t, d = x.shape
    n_ctx = ctx.shape[1]
    rows = t // GRID_W
    cos_a, sin_a = axial_rope(rows, DK_A)
    cs_a = (cos_a[:, None, :], sin_a[:, None, :])
    cos_c, sin_c = axial_rope(rows, DH_C)
    cs_c = (cos_c[:, None, None, :], sin_c[:, None, None, :])
    sc = jax.nn.silu(c)
    scc = jax.nn.silu(c_ctx)
    for l in range(DEPTH):
        last = l == DEPTH - 1
        i = l // 2
        sh1x, s1x, g1x, sh2x, s2x, g2x = jnp.split(sc @ ada_w[l] + ada_b[l], 6, axis=-1)
        sh1c, s1c, g1c, sh2c, s2c, g2c = jnp.split(scc @ ada_w[l] + ada_b[l], 6, axis=-1)
        ux = x * (1.0 + s1x[:, None, :]) + sh1x[:, None, :]
        uc = ctx * (1.0 + s1c) + sh1c
        if l % 2 == 0:
            yx, yc = mixer_ab(ux, uc, ab_w_in[i], ab_w_lr_f[i], ab_b_lr_f[i], ab_w_lr_b[i], ab_b_lr_b[i],
                              ab_gn_a[i], ab_gn_b[i], ab_w_out[i], cs_a, not last)
        else:
            lam_init = 0.8 - 0.6 * math.exp(-0.3 * l)
            yx, yc = mixer_c(ux, uc, c_w_qkv[i], c_lq1[i], c_lk1[i], c_lq2[i], c_lk2[i], c_subln_g[i],
                             c_w_out[i], lam_init, cs_c, not last)
        x = layer_norm(DEEPNORM_ALPHA * x + g1x[:, None, :] * yx, ln1_g[l], ln1_b[l])
        if not last:
            ctx = layer_norm(DEEPNORM_ALPHA * ctx + g1c * yc, ln1_g[l], ln1_b[l])
        ux = x * (1.0 + s2x[:, None, :]) + sh2x[:, None, :]
        tok = ux.reshape(bn * t, d)
        if not last:
            uc = ctx * (1.0 + s2c) + sh2c
            tok = jnp.concatenate([tok, uc.reshape(bn * n_ctx, d)], axis=0)
        y = hier_moe(tok, moe_w_grp[l], moe_b_grp[l], moe_w_rexp[l], moe_b_rexp[l],
                     moe_w_gate[l], moe_w_up[l], moe_w_down[l])
        x = layer_norm(DEEPNORM_ALPHA * x + g2x[:, None, :] * y[:bn * t].reshape(bn, t, d), ln2_g[l], ln2_b[l])
        if not last:
            ctx = layer_norm(DEEPNORM_ALPHA * ctx + g2c * y[bn * t:].reshape(bn, n_ctx, d), ln2_g[l], ln2_b[l])
    return x


N_EVEN_2 = (DEPTH + 1) // 2
N_ODD_2 = DEPTH // 2
EPS = 1e-6

MLA_HEADS = 8
QK_NOPE = 64
QK_ROPE = 32
QK_HEAD = QK_NOPE + QK_ROPE
V_HEAD = 64
Q_LORA = 384
KV_LORA = 256

FNET_GROUPS = 4
FNET_GROUP_W = 128
FNET_W = FNET_GROUPS * FNET_GROUP_W

CONF_GROUPS = 4
CONF_W = 512
CONF_WIDTH = 31
SC_W = 512
SC_WIDTH = 3

D_FF = -(-8 * D_MODEL // (3 * 256)) * 256

EVEN_KV_END = Q_LORA + KV_LORA + QK_ROPE
EVEN_IN = EVEN_KV_END + FNET_W
EVEN_MIX = MLA_HEADS * V_HEAD + FNET_W
ODD_IN = 2 * CONF_W + 3 * SC_W
ODD_MIX = CONF_W + SC_W


def rms_norm(x, g):
    xf = x.astype(jnp.float32)
    y = xf * lax.rsqrt(jnp.mean(jnp.square(xf), axis=-1, keepdims=True) + EPS)
    return (y * g.astype(jnp.float32)).astype(x.dtype)

def group_layer_norm(x, g, b, groups):
    bsz, n, w = x.shape
    xf = x.astype(jnp.float32).reshape(bsz, n, groups, w // groups)
    mu = jnp.mean(xf, axis=-1, keepdims=True)
    var = jnp.mean(jnp.square(xf - mu), axis=-1, keepdims=True)
    y = ((xf - mu) * lax.rsqrt(var + EPS)).reshape(bsz, n, w)
    return (y * g.astype(jnp.float32) + b.astype(jnp.float32)).astype(x.dtype)

def modulate(h, shift, scale):
    return h * (1.0 + scale) + shift

def ada_mod(cvec, w, b):
    return jnp.split(jax.nn.silu(cvec) @ w + b, 6, axis=-1)

def axial_rope_tables(n):
    rows = n // GRID_W
    row = jnp.broadcast_to(jnp.arange(rows, dtype=jnp.float32)[:, None], (rows, GRID_W)).reshape(n)
    col = jnp.broadcast_to(jnp.arange(GRID_W, dtype=jnp.float32)[None, :], (rows, GRID_W)).reshape(n)
    per_axis = QK_ROPE // 4
    inv_freq = ROPE_BASE ** (-jnp.arange(per_axis, dtype=jnp.float32) / per_axis)
    ang = jnp.concatenate([row[:, None] * inv_freq, col[:, None] * inv_freq], axis=-1)
    return jnp.cos(ang), jnp.sin(ang)

def rope_tail(t, rope):
    if rope is None:
        return t
    cos, sin = rope
    half = QK_ROPE // 2
    r = t[..., QK_NOPE:].astype(jnp.float32)
    r1, r2 = r[..., :half], r[..., half:]
    rot = jnp.concatenate([r1 * cos - r2 * sin, r2 * cos + r1 * sin], axis=-1).astype(t.dtype)
    return jnp.concatenate([t[..., :QK_NOPE], rot], axis=-1)

def mla_queries(cq, q_ln_g, w_uq, q_norm_g, rope):
    q = jnp.einsum('bsr,rhd->bshd', rms_norm(cq, q_ln_g), w_uq)
    return rope_tail(rms_norm(q, q_norm_g), rope)

def mla_keys_values(ckv, kr, kv_ln_g, w_uk, w_uv, k_norm_g, rope):
    ckv = rms_norm(ckv, kv_ln_g)
    k_nope = jnp.einsum('bsr,rhd->bshd', ckv, w_uk)
    v = jnp.einsum('bsr,rhd->bshd', ckv, w_uv)
    k_rope = jnp.broadcast_to(kr[:, :, None, :], k_nope.shape[:-1] + (QK_ROPE,))
    k = rope_tail(rms_norm(jnp.concatenate([k_nope, k_rope], axis=-1), k_norm_g), rope)
    return k, v

def latent_attention(q, k, v, k_ctx, v_ctx):
    bsz, n, heads, dq = q.shape
    kt = jnp.concatenate([k_ctx, k], axis=1).transpose(0, 2, 1, 3)
    vt = jnp.concatenate([v_ctx, v], axis=1).transpose(0, 2, 1, 3)
    qb = q.reshape(bsz, n // Q_BLOCK, Q_BLOCK, heads, dq).transpose(1, 0, 2, 3, 4)
    scale = dq ** -0.5

    def block(qi):
        s = jnp.einsum('bqhd,bhkd->bhqk', qi, kt).astype(jnp.float32) * scale
        p = jax.nn.softmax(s, axis=-1).astype(vt.dtype)
        return jnp.einsum('bhqk,bhkd->bqhd', p, vt)

    o = lax.map(block, qb)
    return o.transpose(1, 0, 2, 3, 4).reshape(bsz, n, heads * V_HEAD)

def context_attention(q, k, v):
    bsz, n, heads, dq = q.shape
    s = jnp.einsum('bqhd,bkhd->bhqk', q, k).astype(jnp.float32) * (dq ** -0.5)
    p = jax.nn.softmax(s, axis=-1).astype(v.dtype)
    return jnp.einsum('bhqk,bkhd->bqhd', p, v).reshape(bsz, n, heads * V_HEAD)

def fourier_mix(u):
    bsz, n, _ = u.shape
    ug = u.astype(jnp.float32).reshape(bsz, n, FNET_GROUPS, FNET_GROUP_W)
    y = jnp.fft.fft2(ug, axes=(1, 3), norm='ortho').real
    return y.reshape(bsz, n, FNET_W).astype(u.dtype)

def depthwise_conv(u, w):
    width, ch = w.shape
    pad = (width - 1) // 2
    return lax.conv_general_dilated(
        u, w[:, None, :].astype(u.dtype), window_strides=(1,), padding=[(pad, pad)],
        dimension_numbers=('NWC', 'WIO', 'NWC'), feature_group_count=ch)

def odd_mixer(u, conf_dw, conf_dw_b, conf_ln_g, conf_ln_b, sc_dw):
    a, gate, sb, scc, sx = jnp.split(
        u, [CONF_W, 2 * CONF_W, 2 * CONF_W + SC_W, 2 * CONF_W + 2 * SC_W], axis=-1)
    conf = a * jax.nn.sigmoid(gate)
    conf = depthwise_conv(conf, conf_dw) + conf_dw_b
    conf = jax.nn.silu(group_layer_norm(conf, conf_ln_g, conf_ln_b, CONF_GROUPS))
    sc = sb * depthwise_conv(scc * sx, sc_dw)
    return jnp.concatenate([conf, sc], axis=-1)

def swiglu(h, w1, w3, w2):
    return (jax.nn.silu(h @ w1) * (h @ w3)) @ w2

def second_inputs(seed: int = 0) -> dict:
    key = jax.random.key(seed)
    keys = iter(jax.random.split(key, 40))

    def normal(shape, scale):
        return jax.random.normal(next(keys), shape, jnp.float32) * scale

    def gain(shape):
        return 1.0 + 0.05 * jax.random.normal(next(keys), shape, jnp.float32)

    E, O, L, D = N_EVEN_2, N_ODD_2, DEPTH, D_MODEL
    return {
        'x': normal((BATCH, SEQ, D), 1.0),
        'c': normal((BATCH, D), 1.0),
        'ctx': normal((BATCH, CTX_LEN, D), 1.0),
        'c_ctx': normal((D,), 1.0),
        'ada_w': normal((L, D, 6 * D), 0.5 * D ** -0.5),
        'ada_b': normal((L, 6 * D), 0.02),
        'norm1_g': gain((L, D)),
        'norm2_g': gain((L, D)),
        'ffn_w1': normal((L, D, D_FF), D ** -0.5),
        'ffn_w3': normal((L, D, D_FF), D ** -0.5),
        'ffn_w2': normal((L, D_FF, D), D_FF ** -0.5),
        'a_w_in': normal((E, D, EVEN_IN), D ** -0.5),
        'a_q_ln_g': gain((E, Q_LORA)),
        'a_kv_ln_g': gain((E, KV_LORA)),
        'a_w_uq': normal((E, Q_LORA, MLA_HEADS, QK_HEAD), Q_LORA ** -0.5),
        'a_w_uk': normal((E, KV_LORA, MLA_HEADS, QK_NOPE), KV_LORA ** -0.5),
        'a_w_uv': normal((E, KV_LORA, MLA_HEADS, V_HEAD), KV_LORA ** -0.5),
        'a_q_norm_g': gain((E, QK_HEAD)),
        'a_k_norm_g': gain((E, QK_HEAD)),
        'a_w_out': normal((E, EVEN_MIX, D), EVEN_MIX ** -0.5),
        'b_w_in': normal((O, D, ODD_IN), D ** -0.5),
        'b_conf_dw': normal((O, CONF_WIDTH, CONF_W), CONF_WIDTH ** -0.5),
        'b_conf_dw_b': normal((O, CONF_W), 0.02),
        'b_conf_ln_g': gain((O, CONF_W)),
        'b_conf_ln_b': normal((O, CONF_W), 0.02),
        'b_sc_dw': normal((O, SC_WIDTH, SC_W), SC_WIDTH ** -0.5),
        'b_w_out': normal((O, ODD_MIX, D), ODD_MIX ** -0.5),
    }

def second_block(x, c, ctx, c_ctx, ada_w, ada_b, norm1_g, norm2_g, ffn_w1, ffn_w3, ffn_w2,
              a_w_in, a_q_ln_g, a_kv_ln_g, a_w_uq, a_w_uk, a_w_uv, a_q_norm_g, a_k_norm_g, a_w_out,
              b_w_in, b_conf_dw, b_conf_dw_b, b_conf_ln_g, b_conf_ln_b, b_sc_dw, b_w_out):
    n = x.shape[1]
    cos, sin = axial_rope_tables(n)
    rope = (cos[:, None, :], sin[:, None, :])
    for i in range(DEPTH):
        ctx_needed = any(l % 2 == 0 for l in range(i + 1, DEPTH))
        j = i // 2
        sh1, sc1, g1, sh2, sc2, g2 = [t[:, None, :] for t in ada_mod(c, ada_w[i], ada_b[i])]
        h = modulate(rms_norm(x, norm1_g[i]), sh1, sc1)
        if i % 2 == 0 or ctx_needed:
            csh1, csc1, cg1, csh2, csc2, cg2 = ada_mod(c_ctx, ada_w[i], ada_b[i])
            hc = modulate(rms_norm(ctx, norm1_g[i]), csh1, csc1)
        if i % 2 == 0:
            w_in = a_w_in[j]
            u = h @ w_in
            ukc = hc @ w_in[:, Q_LORA:EVEN_KV_END]
            k_c, v_c = mla_keys_values(ukc[..., :KV_LORA], ukc[..., KV_LORA:], a_kv_ln_g[j],
                                       a_w_uk[j], a_w_uv[j], a_k_norm_g[j], None)
            k, v = mla_keys_values(u[..., Q_LORA:Q_LORA + KV_LORA], u[..., Q_LORA + KV_LORA:EVEN_KV_END],
                                   a_kv_ln_g[j], a_w_uk[j], a_w_uv[j], a_k_norm_g[j], rope)
            q = mla_queries(u[..., :Q_LORA], a_q_ln_g[j], a_w_uq[j], a_q_norm_g[j], rope)
            o = jnp.concatenate([latent_attention(q, k, v, k_c, v_c), fourier_mix(u[..., EVEN_KV_END:])], axis=-1)
            mix = o @ a_w_out[j]
            if ctx_needed:
                q_c = mla_queries(hc @ w_in[:, :Q_LORA], a_q_ln_g[j], a_w_uq[j], a_q_norm_g[j], None)
                oc = jnp.concatenate([context_attention(q_c, k_c, v_c),
                                      fourier_mix(hc @ w_in[:, EVEN_KV_END:])], axis=-1)
                mix_c = oc @ a_w_out[j]
        else:
            mix = odd_mixer(h @ b_w_in[j], b_conf_dw[j], b_conf_dw_b[j], b_conf_ln_g[j],
                            b_conf_ln_b[j], b_sc_dw[j]) @ b_w_out[j]
            if ctx_needed:
                mix_c = odd_mixer(hc @ b_w_in[j], b_conf_dw[j], b_conf_dw_b[j], b_conf_ln_g[j],
                                  b_conf_ln_b[j], b_sc_dw[j]) @ b_w_out[j]
        x = x + g1 * mix
        x = x + g2 * swiglu(modulate(rms_norm(x, norm2_g[i]), sh2, sc2), ffn_w1[i], ffn_w3[i], ffn_w2[i])
        if ctx_needed:
            ctx = ctx + cg1 * mix_c
            ctx = ctx + cg2 * swiglu(modulate(rms_norm(ctx, norm2_g[i]), csh2, csc2),
                                     ffn_w1[i], ffn_w3[i], ffn_w2[i])
    return x


def setup_inputs(seed=0):
    out = dict(first_inputs(seed))
    for name, value in second_inputs(seed + 1).items():
        if name != "x":
            out[name + "_2"] = value
    return out


def reference(
    x, c, ctx, c_ctx, ada_w, ada_b, ln1_g, ln1_b, ln2_g, ln2_b, ab_w_in, ab_w_lr_f, ab_b_lr_f,
    ab_w_lr_b, ab_b_lr_b, ab_gn_a, ab_gn_b, ab_w_out, c_w_qkv, c_lq1, c_lk1, c_lq2, c_lk2,
    c_subln_g, c_w_out, moe_w_grp, moe_b_grp, moe_w_rexp, moe_b_rexp, moe_w_gate, moe_w_up,
    moe_w_down, c_2, ctx_2, c_ctx_2, ada_w_2, ada_b_2, norm1_g_2, norm2_g_2, ffn_w1_2, ffn_w3_2,
    ffn_w2_2, a_w_in_2, a_q_ln_g_2, a_kv_ln_g_2, a_w_uq_2, a_w_uk_2, a_w_uv_2, a_q_norm_g_2,
    a_k_norm_g_2, a_w_out_2, b_w_in_2, b_conf_dw_2, b_conf_dw_b_2, b_conf_ln_g_2, b_conf_ln_b_2,
    b_sc_dw_2, b_w_out_2,
):
    x = first_block(
        x, c, ctx, c_ctx, ada_w, ada_b, ln1_g, ln1_b, ln2_g, ln2_b, ab_w_in, ab_w_lr_f,
        ab_b_lr_f, ab_w_lr_b, ab_b_lr_b, ab_gn_a, ab_gn_b, ab_w_out, c_w_qkv, c_lq1, c_lk1,
        c_lq2, c_lk2, c_subln_g, c_w_out, moe_w_grp, moe_b_grp, moe_w_rexp, moe_b_rexp,
        moe_w_gate, moe_w_up, moe_w_down,
    )
    return second_block(
        x, c_2, ctx_2, c_ctx_2, ada_w_2, ada_b_2, norm1_g_2, norm2_g_2, ffn_w1_2, ffn_w3_2,
        ffn_w2_2, a_w_in_2, a_q_ln_g_2, a_kv_ln_g_2, a_w_uq_2, a_w_uk_2, a_w_uv_2, a_q_norm_g_2,
        a_k_norm_g_2, a_w_out_2, b_w_in_2, b_conf_dw_2, b_conf_dw_b_2, b_conf_ln_g_2,
        b_conf_ln_b_2, b_sc_dw_2, b_w_out_2,
    )


_drawn_inputs = setup_inputs


def setup_inputs(seed=0):
    import zlib

    import numpy as np

    out = dict(_drawn_inputs(seed))
    spreads = {}
    factors = {'ada_b': 7.418,
     'ln1_b': 3.44,
     'ln2_b': 3.356,
     'ab_w_lr_f': 7.678,
     'ab_b_lr_f': 24.279,
     'ab_w_lr_b': 6.684,
     'ab_b_lr_b': 8.0,
     'ab_gn_a': 8.0,
     'ab_gn_b': 8.0,
     'c_lq1': 7.359,
     'c_lk1': 6.981,
     'c_lq2': 8.0,
     'c_lk2': 6.637,
     'c_subln_g': 8.0,
     'moe_b_grp': 8.0,
     'moe_b_rexp': 8.0,
     'ctx_2': 4.907,
     'a_q_ln_g_2': 8.0,
     'a_kv_ln_g_2': 8.0,
     'a_w_uq_2': 2.962,
     'a_w_uk_2': 3.304,
     'a_q_norm_g_2': 8.0,
     'a_k_norm_g_2': 8.0,
     'b_conf_dw_b_2': 8.0,
     'b_conf_ln_g_2': 42.873,
     'b_conf_ln_b_2': 119.047,
     'norm2_g_2': 5.653}
    for name, (base, spread) in spreads.items():
        noise = np.random.default_rng([zlib.crc32(name.encode()), seed]).standard_normal(out[name].shape)
        drawn = base * np.exp(spread * noise) if base else spread * noise
        out[name] = jnp.asarray(drawn.astype(out[name].dtype))
    for name, factor in factors.items():
        out[name] = (out[name] * factor).astype(out[name].dtype)
    return out
```

```python
from contextlib import ExitStack
import math

import numpy as np

import concourse.bass as bass
from concourse import mybir
from concourse.alu_op_type import AluOpType as ALU

F32 = mybir.dt.float32
I32 = mybir.dt.int32
U32 = mybir.dt.uint32
ACT = mybir.ActivationFunctionType
AX_X = mybir.AxisListType.X

P = 128
D = 1024
KT = D // P
SEQ = 256
T = 2 * SEQ
R = 6
SLOT = 2048
ARENA = 24192
OVW = 15872
ALPHA = 4.0 ** 0.25
LN_EPS = 1e-5
RMS_EPS = 1e-6
NG, EPG = 4, 8
NE = NG * EPG
DE = 512
S = 64
D_FF = 2816
LAM_INIT = 0.8 - 0.6 * math.exp(-0.3)


def rope_tables(head, quarter):
    tok = np.arange(SEQ)
    inv = 10000.0 ** (-np.arange(quarter, dtype=np.float64) / quarter)
    row, col = (tok // 64)[:, None] * inv, (tok % 64)[:, None] * inv
    ang = np.concatenate([row, row, col, col], 1)
    sign = np.tile(np.repeat([-1.0, 1.0], quarter), 2)
    return np.concatenate([np.cos(ang), np.sin(ang) * sign], 1).astype(np.float32)


def mla_rope_tables():
    tok = np.arange(SEQ)
    inv = 10000.0 ** (-np.arange(8, dtype=np.float64) / 8)
    ang = np.concatenate([(tok // 64)[:, None] * inv, (tok % 64)[:, None] * inv], 1)
    c, s = np.cos(ang), np.sin(ang)
    return np.concatenate([c, c, -s, s], 1).astype(np.float32)


def retention_tables():
    i, j = np.arange(SEQ)[None, :], np.arange(SEQ)[:, None]
    out = np.zeros((P, 4, 2, 2, SEQ), np.float64)
    for h in range(4):
        gf, gb = np.log1p(-2.0 ** -(5.0 + h)), np.log1p(-2.0 ** -(5.5 + h))
        within = np.where(i >= j, np.exp(gf * (i - j)), np.exp(gb * (j - i - 1)))
        across = np.exp(gf * (SEQ + i - j)) + np.exp(gb * (SEQ - 1 - i + j))
        for n, m in enumerate((within, across)):
            out[:, h, n] = m.reshape(2, P, SEQ).transpose(1, 0, 2)
    return (out * P ** -0.5).astype(np.float32).reshape(P, -1)


def gla_tables():
    j, i = np.arange(P)[:, None], np.arange(P)[None, :]
    same = (j // 64) == (i // 64)
    sums = [(same & m) / 16.0 for m in (j <= i, j > i, j >= i, j > i, j < i)]
    masks = [same & m for m in (j <= i, j <= i, j > i, j > i)]
    return np.concatenate(sums + masks, 1).astype(np.float32)


def fourier_tables():
    n = np.arange(SEQ)
    a = 2 * np.pi * np.outer(n, n) / SEQ
    tokens = np.concatenate([np.cos(a), np.sin(a)], 1)
    c = np.arange(P)
    b = 2 * np.pi * np.outer(c, c) / P
    chans = np.concatenate([np.cos(b), -np.sin(b)], 1) / math.sqrt(SEQ * P)
    return (tokens.astype(np.float32).reshape(2, P, T).transpose(1, 0, 2).reshape(P, -1).copy(),
            chans.astype(np.float32))


def misc_tables():
    j, i = np.arange(P)[:, None], np.arange(P)[None, :]
    return np.concatenate([np.eye(P), (j < i) * 1.0, np.ones((P, P)), np.tile(np.arange(P), (P, 1)),
                           np.full((P, P), 1.0 / P)], 1).astype(np.float32)


def constants():
    dft_tok, dft_ch = fourier_tables()
    return {"k_misc": misc_tables(), "k_rope_a": rope_tables(128, 32), "k_rope_c": rope_tables(64, 16),
            "k_rope_m": mla_rope_tables(), "k_ret": retention_tables(), "k_gla": gla_tables(),
            "k_dft_tok": dft_tok, "k_dft_ch": dft_ch}


class Count:

    def __init__(self, sem):
        self.sem, self.base, self.total = sem, 0, 0

    def up(self, times=1):
        self.total += times
        return self.sem

    def at(self, k):
        return self.base + k


def dims(ap, *free):
    return bass.AP(tensor=ap.tensor, offset=ap.offset, ap=[list(ap.ap[0])] + [list(f) for f in free])


def rows_to_all(ap_row, n):
    return bass.AP(tensor=ap_row.tensor, offset=ap_row.offset, ap=[[0, P], [1, n]])


def build_program(nc, I, out, debug=None):
    ctx = ExitStack()
    with ctx:
        Program(nc, ctx, I, out, debug).run()


class Program:
    def __init__(self, nc, ctx, I, out, debug):
        self.nc, self.I, self.out, self.debug = nc, I, out, debug

        def sb(name, n, dt=F32, p=P):
            return ctx.enter_context(nc.sbuf_tensor(name, [p, n], dt))

        self.counts = []

        def count(name):
            c = Count(ctx.enter_context(nc.semaphore(name)))
            self.counts.append(c)
            return c

        self.bank = [ctx.enter_context(nc.psum_tensor(f"bank{i}", [P, 512], F32)) for i in range(8)]
        self.ring = sb("ring", R * SLOT)
        self.xres = sb("xres", 4 * D)
        self.mod = sb("mod", 6 * D)
        self.actT = sb("actT", KT * T)
        self.misc = sb("misc", 5 * P)
        self.scx = sb("scx", KT * P)
        self.cols = sb("cols", 64)
        self.stat = sb("stat", 512)
        self.pw = sb("pw", 64)
        self.arena = sb("arena", ARENA)
        self.ident = self.misc[:, 0:P]
        self.before = self.misc[:, P:2 * P]
        self.ones = self.misc[:, 2 * P:3 * P]
        self.iota = self.misc[:, 3 * P:4 * P]
        self.mean_of = self.misc[:, 4 * P:5 * P]

        self.loaded = [ctx.enter_context(nc.semaphore(f"loaded{i}")) for i in range(R)]
        self.freed = {}
        self.weights_used = count("weights_used")
        self.pe_done = count("pe_done")
        self.act_done = count("act_done")
        self.dve_done = count("dve_done")
        self.pool_done = count("pool_done")
        self.params_in = count("params_in")
        self.dve_chain = count("dve_chain")
        self.act_chain = count("act_chain")
        self.pool_chain = count("pool_chain")
        self.sem = {n: count(n) for n in (
            "gateup_done", "silu_done", "h_ready", "gather_done", "xs_ready", "down_done", "pick_ready",
            "weigh_ready", "turned", "turn_out", "ys_ready", "sum_done", "added", "exp_done", "max_done",
            "score_done", "mix_done", "aT_ready", "o_out", "o_done", "stored", "ov_loaded")}
        self.ov = [([ctx.enter_context(nc.semaphore(f"ov{l}_weights{j}")) for j in range(6)],
                    *(ctx.enter_context(nc.semaphore(f"ov{l}_{n}")) for n in ("pe", "act", "dve"))) for l in range(2)]
        self.W = []
        self.sent = 0
        self.used = 0

    def stage(self):
        for c in self.counts:
            c.base = c.total
        return self.nc.Block(no_gpsimd_drain=True)

    def linker(self, eng, chain):
        def link(ins):
            ins.then_inc(chain.up(), 1)
            eng.wait_ge(chain.sem, chain.total)
        return link

    def plan(self, src, k, n):
        self.W.append((src, k, n))

    def plan_linear(self, w, n0, n1, width=512, ks=4):
        kt = w.shape[0] // P
        for c in range(n0, n1, width):
            e = min(c + width, n1)
            for k in range(0, kt, ks):
                kk = min(ks, kt - k)
                self.plan(w[k * P:(k + kk) * P, c:e].rearrange("(k p) n -> p k n", p=P), kk, e - c)

    def slot(self, i):
        _, k, n = self.W[i]
        s = i % R
        return self.ring[:, s * SLOT:s * SLOT + k * n].rearrange("p (k n) -> p k n", k=k)

    def feed(self, sp, upto):
        while self.sent < min(upto, len(self.W)):
            i = self.sent
            if i >= R:
                sem, value = self.freed[i - R]
                sp.wait_ge(sem, value)
            sp.dma_start(self.slot(i), self.W[i][0]).then_inc(self.loaded[i % R], 16)
            self.sent += 1

    def arrived(self, pe, i):
        pe.wait_ge(self.loaded[i % R], 16 * (i // R + 1))

    def frees(self, w, c):
        self.freed[w] = (c.sem, c.total)

    def load_params(self, pool, pairs):
        for dst, src in pairs:
            pool.dma_start(dst, src, allow_slow_non_contiguous=True).then_inc(self.params_in.up(16), 16)

    def A(self, off, n):
        assert off + n <= ARENA, (off, n)
        return self.arena[:, off:off + n]

    def st_linear(self, lhsT, chunks, dest, add=None, params=None):
        nc = self.nc
        first = self.used
        groups = []
        for ci, (ns, tiles, _) in enumerate(chunks):
            for n, m in enumerate(tiles):
                groups.append((ci, m, 4 * (ci % 2) + n, add is None and len(groups) % 2 == 0))

        def out_of(g):
            c = self.act_done if groups[g][3] else self.dve_done
            return c.sem, c.at(sum(x[3] == groups[g][3] for x in groups[:g + 1]))

        with self.stage() as block:
            @block.tensor
            def _(pe):
                g0 = 0
                for ci, (ns, tiles, ncols) in enumerate(chunks):
                    kts = sum(self.W[self.used + j][1] for j in range(ns))
                    kt = 0
                    for j in range(ns):
                        self.arrived(pe, self.used)
                        sl, kk = self.slot(self.used), self.W[self.used][1]
                        for n, m in enumerate(tiles):
                            bank = groups[g0 + n][2]
                            earlier = [q for q in range(g0) if groups[q][2] == bank]
                            if j == 0 and earlier:
                                pe.wait_ge(*out_of(earlier[-1]))
                            for k in range(kk):
                                mm = nc.tensor.matmul(self.bank[bank][:, 0:ncols], lhsT(m, kt + k), sl[:, k, 0:ncols],
                                                      start=(kt + k == 0), stop=(kt + k == kts - 1))
                            if j == ns - 1:
                                mm.then_inc(self.pe_done.up(), 1)
                        if j == ns - 1:
                            self.frees(self.used, self.pe_done)
                        else:
                            mm.then_inc(self.weights_used.up(), 1)
                            self.frees(self.used, self.weights_used)
                        kt += kk
                        self.used += 1
                    g0 += len(tiles)

            @block.sync
            def _(sp):
                self.feed(sp, self.used + R)

            if params:
                @block.gpsimd
                def _(pool):
                    self.load_params(pool, params)

            @block.scalar
            def _(act):
                for g, (ci, m, bank, on_act) in enumerate(groups):
                    if on_act:
                        act.wait_ge(self.pe_done.sem, self.pe_done.at(g + 1))
                        nc.scalar.activation(dest(ci, m), self.bank[bank][:, 0:chunks[ci][2]],
                                             ACT.Copy).then_inc(self.act_done.up(), 1)

            @block.vector
            def _(dve):
                if params:
                    dve.wait_ge(self.params_in.sem, self.params_in.at(16 * len(params)))
                for g, (ci, m, bank, on_act) in enumerate(groups):
                    if not on_act:
                        dve.wait_ge(self.pe_done.sem, self.pe_done.at(g + 1))
                        src = self.bank[bank][:, 0:chunks[ci][2]]
                        if add is None:
                            nc.vector.tensor_copy(dest(ci, m), src).then_inc(self.dve_done.up(), 1)
                        else:
                            nc.vector.tensor_tensor(dest(ci, m), src, add(ci, m), ALU.add).then_inc(self.dve_done.up(), 1)

    def st_transpose(self, src, nt, put, prep=None, nb=KT, bw=P, scale=1.0):
        nc = self.nc
        G = -(-nb // 4)
        groups = [(t, g, 4 if 4 * g + 4 <= nb else nb - 4 * g) for t in range(nt) for g in range(G)]
        assert len(groups) <= 8
        with self.stage() as block:
            def taken(eng, n):
                eng.wait_ge(self.pe_done.sem, self.pe_done.at(n + 1))
                t, g, k = groups[n]
                return put(t, g), dims(self.bank[n][0:bw, :], [P, k], [1, P])

            @block.vector
            def _(dve):
                link = self.linker(dve, self.dve_chain)
                if prep:
                    for t in range(nt):
                        prep(link, t).then_inc(self.dve_done.up(), 1)
                for n in range(1, len(groups), 2):
                    dst, bank = taken(dve, n)
                    nc.vector.tensor_scalar(dst, bank, scale, None, ALU.mult)

            @block.scalar
            def _(act):
                for n in range(0, len(groups), 2):
                    dst, bank = taken(act, n)
                    nc.scalar.activation(dst, bank, ACT.Copy, scale=scale)

            @block.tensor
            def _(pe):
                for n, (t, g, blocks) in enumerate(groups):
                    if prep and g == 0:
                        pe.wait_ge(self.dve_done.sem, self.dve_done.at(t + 1))
                    for q in range(blocks):
                        k = 4 * g + q
                        mm = nc.tensor.transpose(self.bank[n][0:bw, q * P:(q + 1) * P],
                                                 src(t)[:, k * bw:(k + 1) * bw], self.ident)
                    mm.then_inc(self.pe_done.up(), 1)

    def put_mixed(self, t, half):
        return dims(self.actT[:, 4 * half * T + 64 * t:], [T, 4], [SEQ, 2], [1, 64])

    def put_pure(self, t, half):
        return dims(self.actT[:, 4 * half * T + P * t:], [T, 4], [1, P])

    def put_for_mixed(self, t, half):
        return dims(self.actT[:, 4 * half * T + (t % 2) * SEQ + 64 * (t // 2):], [T, 4], [P, 2], [1, 64])

    def x_tile(self, t):
        return self.xres[:, t * D:(t + 1) * D]

    def mod_row(self, i):
        return self.mod[:, i * D:(i + 1) * D]

    def modulated(self, dst, i_shift):
        nc = self.nc

        def prep(link, t):
            link(nc.vector.scalar_tensor_tensor(dst(t), self.mod_row(i_shift + 1), 1.0, self.x_tile(t), ALU.add, ALU.mult))
            return nc.vector.tensor_tensor(dst(t), dst(t), self.mod_row(i_shift), ALU.add)
        return prep

    def rstd(self, pool, n, waits):
        pool.wait_ge(self.dve_done.sem, waits)
        self.nc.gpsimd.tensor_tensor(self.stat[:, 0:n], self.stat[:, 0:n], self.pw[:, 0:n],
                                     ALU.pow).then_inc(self.pool_done.up(), 1)

    def moments(self, link, views, n, eps, centred):
        nc = self.nc
        k = len(views(0))
        for i in range(n):
            for j, v in enumerate(views(i)):
                ins = nc.vector.bn_stats(self.stat[:, 192 + 6 * (k * i + j):198 + 6 * (k * i + j)], v)
        link(ins)
        for i in range(n):
            ins = nc.vector.bn_aggr(self.stat[:, 64 + 2 * i:66 + 2 * i],
                                    self.stat[:, 192 + 6 * k * i:192 + 6 * k * (i + 1)])
        link(ins)
        mean, var = dims(self.stat[:, 64:], [2, n]), dims(self.stat[:, 65:], [2, n])
        if centred:
            return nc.vector.tensor_scalar(self.stat[:, 0:n], var, 1.0, eps, ALU.mult, ALU.add)
        link(nc.vector.tensor_tensor(self.stat[:, 0:n], mean, mean, ALU.mult))
        return nc.vector.scalar_tensor_tensor(self.stat[:, 0:n], self.stat[:, 0:n], eps, var, ALU.add, ALU.add)

    def mean_at(self, i):
        return self.stat[:, 64 + 2 * i:65 + 2 * i]

    def st_add_norm(self, y, nt, i_gate, g_row, b_row, buf, finish=None):
        nc = self.nc
        with self.stage() as block:
            @block.gpsimd
            def _(pool):
                self.load_params(pool, [(buf[:, 0:D], rows_to_all(g_row, D)), (buf[:, D:2 * D], rows_to_all(b_row, D))])
                self.rstd(pool, nt, self.dve_done.at(1))

            @block.vector
            def _(dve):
                link = self.linker(dve, self.dve_chain)
                for t in range(nt):
                    ins = nc.vector.tensor_tensor(y(t), y(t), self.mod_row(i_gate), ALU.mult)
                link(ins)
                for t in range(nt):
                    ins = nc.vector.scalar_tensor_tensor(self.x_tile(t), self.x_tile(t), ALPHA, y(t), ALU.mult, ALU.add)
                link(ins)
                self.moments(link, lambda t: [self.x_tile(t)[:, 0:512], self.x_tile(t)[:, 512:D]], nt, LN_EPS,
                             True).then_inc(self.dve_done.up(), 1)
                dve.wait_ge(self.pool_done.sem, self.pool_done.at(1))
                for t in range(nt):
                    ins = nc.vector.tensor_scalar(self.x_tile(t), self.x_tile(t), self.mean_at(t), self.stat[:, t:t + 1],
                                                  ALU.subtract, ALU.mult)
                link(ins)
                dve.wait_ge(self.params_in.sem, self.params_in.at(32))
                for t in range(nt):
                    ins = nc.vector.tensor_tensor(self.x_tile(t), self.x_tile(t), buf[:, 0:D], ALU.mult)
                link(ins)
                for t in range(nt):
                    nc.vector.tensor_tensor(self.x_tile(t), self.x_tile(t), buf[:, D:2 * D], ALU.add)

    def st_ada(self, n_chunks, cvecs, bias_row, first=0):
        nc = self.nc
        with self.stage() as block:
            @block.vector
            def _(dve):
                for half, v in enumerate(cvecs):
                    ins = nc.vector.tensor_copy(dims(self.scx[:, 64 * half:], [P, KT], [1, 64]),
                                                dims(self.cols[:, 8 * v:], [1, KT], [0, 64]))
                ins.then_inc(self.dve_done.up(), 1)
        lo, n = first * 512, n_chunks * 512
        self.st_linear(lambda m, k: self.scx[:, k * P:(k + 1) * P], [(2, [0], 512)] * n_chunks,
                       lambda c, m: self.mod[:, lo + c * 512:lo + (c + 1) * 512],
                       lambda c, m: self.mod[:, lo + c * 512:lo + (c + 1) * 512],
                       [(self.mod[:, lo:lo + n], rows_to_all(bias_row[lo:lo + n], n))])

    def st_setup(self):
        nc, I = self.nc, self.I
        vecs = [I["c"], I["c_ctx"], I["c_2"], I["c_ctx_2"]]
        with self.stage() as block:
            @block.sync
            def _(sp):
                self.feed(sp, R)

            @block.gpsimd
            def _(pool):
                nc.gpsimd.memset(self.pw[:, :], -0.5)
                for v, src in enumerate(vecs):
                    flat = bass.AP(tensor=src.tensor, offset=src.offset, ap=[[1, P], [P, KT]])
                    self.load_params(pool, [(self.cols[:, 8 * v:8 * v + 8], flat)])
                pool.wait_ge(self.params_in.sem, self.params_in.at(64))
                self.load_params(pool, [(self.misc[:, :], I["k_misc"])] +
                    [(self.xres[64 * s:64 * s + 64, :].rearrange("p (t d) -> p t d", t=4),
                      I[n][0].rearrange("(t p) d -> p t d", p=64)) for s, n in enumerate(("x", "ctx"))])
                pool.wait_ge(self.params_in.sem, self.params_in.at(112))

            @block.scalar
            def _(act):
                act.wait_ge(self.params_in.sem, self.params_in.at(64))
                nc.scalar.activation(self.stat[:, 0:32], self.cols[:, 0:32], ACT.Silu).then_inc(self.act_done.up(), 1)
                act.wait_ge(self.act_done.sem, self.act_done.at(1))
                nc.scalar.activation(self.cols[:, 0:32], self.stat[:, 0:32], ACT.Copy)

    def rope(self, link, view, n, step, width, quarter, cos, sin, tmp):
        nc, m = self.nc, width // quarter // 2
        t1, t2 = tmp[:, 0:n * width], tmp[:, n * width:2 * n * width]
        nc.vector.tensor_tensor(dims(t1, [width, n], [1, width]), dims(view, [step, n], [1, width]),
                                dims(cos, [0, n], [1, width]), ALU.mult)
        for k in range(2):
            part = lambda ap, s, off: dims(ap[:, off * quarter:], [s, n], [2 * quarter, m], [1, quarter])
            ins = nc.vector.tensor_tensor(part(t2, width, k), part(view, step, 1 - k), part(sin, 0, k), ALU.mult)
        link(ins)
        return nc.vector.tensor_tensor(dims(view, [step, n], [1, width]), dims(t1, [width, n], [1, width]),
                                       dims(t2, [width, n], [1, width]), ALU.add)

    def mixer_ab(self):
        nc, I = self.nc, self.I
        O, VA, G, QKB, VB, LRT, QBT, XX = 0, 4096, 6144, 10240, 12288, 14336, 14848, 16896
        A = self.A
        w_in, w_out = I["ab_w_in"][0], I["ab_w_out"][0]

        def O_t(t):
            return A(O + t * D, D)

        self.st_transpose(O_t, 4, self.put_mixed, self.modulated(O_t, 0))

        def dest(c, t):
            off = [O + t * D, O + t * D + 512, VA + t * 512, G + t * D, QKB + t * 512, VB + t * 512,
                   G + t * D + 512][c]
            return A(off, 512)
        self.st_linear(lambda m, k: self.actT[:, k * T + m * P:k * T + m * P + P],
                       [(2, [0, 1, 2, 3], 512)] * 7, dest)

        rope_at = XX + 4096
        with self.stage() as block:
            @block.gpsimd
            def _(pool):
                self.load_params(pool, [(A(rope_at, 512).rearrange("p (t n) -> p t n", t=2),
                                         I["k_rope_a"].rearrange("(t p) n -> p t n", p=P))])

            @block.tensor
            def _(pe):
                self.arrived(pe, self.used)
                sl = self.slot(self.used)
                for k in range(KT):
                    mm = nc.tensor.matmul(self.bank[0][0:32, :], sl[:, k, :], self.actT[:, k * T:(k + 1) * T],
                                          start=(k == 0), stop=(k == KT - 1))
                mm.then_inc(self.pe_done.up(), 1)
                self.frees(self.used, self.pe_done)
                self.used += 1
                for t in range(4):
                    for q in range(4):
                        mm = nc.tensor.transpose(self.bank[1 + t][:, q * P:(q + 1) * P],
                                                 A(QKB + t * 512 + q * P, P), self.ident)
                    mm.then_inc(self.pe_done.up(), 1)

            @block.sync
            def _(sp):
                self.feed(sp, self.used + R)

            @block.scalar
            def _(act):
                act.wait_ge(self.pe_done.sem, self.pe_done.at(1))
                nc.scalar.activation(self.arena[0:32, LRT:LRT + 512], self.bank[0][0:32, :], ACT.Copy)
                for t in range(4):
                    act.wait_ge(self.pe_done.sem, self.pe_done.at(2 + t))
                    nc.scalar.activation(dims(A(QBT + t * P, 1), [T, 4], [1, P]), self.bank[1 + t][:, :], ACT.Copy)

            @block.vector
            def _(dve):
                link = self.linker(dve, self.dve_chain)
                dve.wait_ge(self.params_in.sem, self.params_in.at(16))
                for t in range(2):
                    link(self.rope(link, O_t(t), 8, P, P, 32, A(rope_at + 256 * t, P), A(rope_at + 256 * t + P, P),
                                   A(rope_at + 512, 2048)))

        QAT = XX
        TAB = [QKB, QKB + 1024, XX + 4096, XX + 5120]
        self.st_transpose(O_t, 4, lambda t, half: dims(A(QAT + half * 2048 + t * P, 1), [T, 4], [1, P]))

        with self.stage() as block:
            @block.gpsimd
            def _(pool):
                self.load_params(pool, [(A(TAB[2 * i], 2048), I["k_ret"][:, 2048 * i:2048 * (i + 1)]) for i in range(2)])

            def score(h):
                b = 3 * (h % 2)
                for n, (k0, q0) in enumerate(((0, 0), (SEQ, SEQ), (SEQ, 0))):
                    for j in range(2):
                        mm = nc.tensor.matmul(self.bank[b + n][:, j * SEQ:(j + 1) * SEQ],
                                              A(QAT + 2048 + h * T + k0 + j * P, P), A(QAT + h * T + q0, SEQ),
                                              start=True, stop=True)
                mm.then_inc(self.pe_done.up(), 1)

            def att(h, n, j, t):
                off = 1536 * (h % 2) + 512 * n + SEQ * j + P * t
                return self.actT[:, off:off + P]

            @block.tensor
            def _(pe):
                score(0)
                for h in range(4):
                    if h < 3:
                        if h >= 1:
                            pe.wait_ge(self.dve_done.sem, self.dve_done.at(h))
                        score(h + 1)
                    pe.wait_ge(self.dve_done.sem, self.dve_done.at(h + 1))
                    if h >= 2:
                        pe.wait_ge(self.act_done.sem, self.act_done.at(h - 1))
                    for t in range(4):
                        parts = [(0, 0, t, 0), (0, 1, t, 1), (2, 0, t, 2), (2, 1, t, 3)] if t < 2 else \
                                [(1, 0, t - 2, 2), (1, 1, t - 2, 3)]
                        for i, (n, j, tq, v) in enumerate(parts):
                            mm = nc.tensor.matmul(self.bank[6 + h % 2][:, t * P:(t + 1) * P], att(h, n, j, tq),
                                                  A(VA + v * 512 + h * P, P), start=(i == 0), stop=(i == len(parts) - 1))
                    mm.then_inc(self.sem["mix_done"].up(), 1)

            @block.vector
            def _(dve):
                dve.wait_ge(self.params_in.sem, self.params_in.at(32))
                for h in range(4):
                    dve.wait_ge(self.pe_done.sem, self.pe_done.at(h + 1))
                    if h >= 2:
                        dve.wait_ge(self.sem["mix_done"].sem, self.sem["mix_done"].at(h - 1))
                    for n in range(3):
                        off = 1536 * (h % 2) + 512 * n
                        ins = nc.vector.tensor_tensor(self.actT[:, off:off + 512], self.bank[3 * (h % 2) + n][:, :],
                                                      A(TAB[h] + (512 if n == 2 else 0), 512), ALU.mult)
                    ins.then_inc(self.dve_done.up(), 1)

            @block.scalar
            def _(act):
                for h in range(4):
                    act.wait_ge(self.sem["mix_done"].sem, self.sem["mix_done"].at(h + 1))
                    nc.scalar.activation(dims(A(O + h * P, 1), [D, 4], [1, P]), self.bank[6 + h % 2][:, :],
                                         ACT.Copy).then_inc(self.act_done.up(), 1)

        LA, GT = XX, XX + 2048
        QD, KD, KTT, KTOK = XX + 3200, XX + 4224, XX + 5248, XX + 6272
        wlr, blr = (lambda r, c0, c1: self.actT[r, 2048 + c0:2048 + c1]), self.actT[:, 2560:3072]
        with self.stage() as block:
            @block.gpsimd
            def _(pool):
                nc.gpsimd.memset(wlr(slice(0, 32), 0, 512), 0.0).then_inc(self.pool_done.up(), 1)
                pool.wait_ge(self.pool_done.sem, self.pool_done.at(1))
                self.load_params(pool, [
                    (wlr(slice(0, 16), 0, 256), I["ab_w_lr_f"][0]), (wlr(slice(16, 32), 256, 512), I["ab_w_lr_b"][0]),
                    (blr[:, 0:256], rows_to_all(I["ab_b_lr_f"][0], 256)), (blr[:, 256:512], rows_to_all(I["ab_b_lr_b"][0], 256)),
                    (A(GT, 1152), I["k_gla"])])

            @block.tensor
            def _(pe):
                pe.wait_ge(self.params_in.sem, self.params_in.at(80))
                for t in range(4):
                    nc.tensor.matmul(self.bank[t][:, :], self.arena[0:32, LRT + t * P:LRT + (t + 1) * P],
                                     wlr(slice(0, 32), 0, 512), start=True, stop=True).then_inc(self.pe_done.up(), 1)

            @block.vector
            def _(dve):
                link = self.linker(dve, self.dve_chain)
                dve.wait_ge(self.params_in.sem, self.params_in.at(80))
                for t in range(4):
                    dve.wait_ge(self.pe_done.sem, self.pe_done.at(t + 1))
                    ins = nc.vector.tensor_tensor(A(LA + 512 * t, 512), self.bank[t][:, :], blr, ALU.add)
                link(ins)
                nc.vector.scalar_tensor_tensor(self.actT[:, 0:2048], A(LA, 2048), -1.0, A(LA, 2048), ALU.mult,
                                               ALU.max).then_inc(self.dve_done.up(), 1)
                dve.wait_ge(self.act_done.sem, self.act_done.at(2))
                nc.vector.scalar_tensor_tensor(A(LA, 2048), A(LA, 2048), 0.0, self.actT[:, 0:2048], ALU.min, ALU.subtract)

            @block.scalar
            def _(act):
                act.wait_ge(self.dve_done.sem, self.dve_done.at(1))
                nc.scalar.activation(self.actT[:, 0:2048], self.actT[:, 0:2048], ACT.Exp, scale=-1.0).then_inc(self.act_done.up(), 1)
                act.wait_ge(self.act_done.sem, self.act_done.at(1))
                nc.scalar.activation(self.actT[:, 0:2048], self.actT[:, 0:2048], ACT.Ln, bias=1.0).then_inc(self.act_done.up(), 1)

        ST, ATT, EB = 0, 2048, 3072
        for pair in range(2):
            self.gla_pair(pair, dict(O=O, VB=VB, QBT=QBT, LA=LA, GT=GT, QD=QD, KD=KD, KTT=KTT, KTOK=KTOK,
                                     ST=ST, ATT=ATT, EB=EB))

        GN = XX
        with self.stage() as block:
            @block.gpsimd
            def _(pool):
                self.load_params(pool, [(A(GN, 512), rows_to_all(I["ab_gn_a"][0], 512)), (A(GN + 512, 512), rows_to_all(I["ab_gn_b"][0], 512))])
                self.rstd(pool, 32, self.dve_done.at(1))

            @block.scalar
            def _(act):
                nc.scalar.activation(A(XX + 1024, 4096), A(G, 4096), ACT.Silu).then_inc(self.act_done.up(), 1)

            @block.vector
            def _(dve):
                link = self.linker(dve, self.dve_chain)
                link(self.moments(link, lambda i: [A(O + i * P, P)], 32, LN_EPS, True))
                mean_b = dims(self.stat[:, 64 + 8:], [16, 4], [2, 4])
                sq, var_b = dims(self.stat[:, 160:], [4, 4], [1, 4]), dims(self.stat[:, 4:], [8, 4], [1, 4])
                link(nc.vector.tensor_tensor(sq, mean_b, mean_b, ALU.mult))
                nc.vector.tensor_tensor(var_b, var_b, sq, ALU.add)
                link(nc.vector.memset(mean_b, 0.0))
                nc.vector.memset(self.stat[:, 180:181], 0.0).then_inc(self.dve_done.up(), 1)
                dve.wait_ge(self.pool_done.sem, self.pool_done.at(1))
                for i in range(32):
                    ins = nc.vector.tensor_scalar(A(O + i * P, P), A(O + i * P, P), self.mean_at(i), self.stat[:, i:i + 1],
                                                  ALU.subtract, ALU.mult)
                link(ins)
                dve.wait_ge(self.params_in.sem, self.params_in.at(32))
                for t in range(4):
                    ins = nc.vector.tensor_tensor(O_t(t), O_t(t), A(GN, D), ALU.mult)
                link(ins)
                dve.wait_ge(self.act_done.sem, self.act_done.at(1))
                nc.vector.tensor_tensor(A(O, 4096), A(O, 4096), A(XX + 1024, 4096), ALU.mult)

        self.st_transpose(O_t, 4, self.put_for_mixed)
        self.st_linear(lambda m, k: self.actT[:, k * T + m * P:k * T + m * P + P],
                       [(2, [0, 1, 2, 3], 512)] * 2, lambda c, t: A(O + t * D + 512 * c, 512))
        self.st_add_norm(O_t, 4, 2, I["ln1_g"][0], I["ln1_b"][0], A(4096, 2048))

    def gla_pair(self, pair, at):
        nc, A = self.nc, self.A
        QT, KTb = at["QBT"] + pair * T, at["QBT"] + 2 * T + pair * T
        LA, GT, QD, KD, KTT, KTOK = at["LA"], at["GT"], at["QD"], at["KD"], at["KTT"], at["KTOK"]
        actT = self.actT
        states = lambda d, c: actT[:, at["ST"] + (d * 8 + c) * P:at["ST"] + (d * 8 + c + 1) * P]
        order = [[4, 5, 6, 7, 0, 1, 2, 3], [7, 6, 5, 4, 3, 2, 1, 0]]
        E = KTOK
        with self.stage() as block:
            @block.tensor
            def _(pe):
                for b in range(5):
                    d = 0 if b < 2 else 1
                    for t in range(4):
                        mm = nc.tensor.matmul(self.bank[b][:, t * P:(t + 1) * P],
                                              A(LA + t * 512 + d * 256 + pair * P, P), A(GT + b * P, P), start=True, stop=True)
                    mm.then_inc(self.pe_done.up(), 1)
                for d in range(2):
                    pe.wait_ge(self.dve_done.sem, self.dve_done.at(3 * d + 3))
                    for t in range(4):
                        mm = nc.tensor.transpose(self.bank[5 + d][:, t * P:(t + 1) * P], A(KTT + d * T + t * P, P), self.ident)
                    mm.then_inc(self.pe_done.up(), 1)

            jobs = [(0, 1.0), (0, -1.0), (1, 1.0), (3, 1.0), (2, -1.0), (4, 1.0)]

            @block.scalar
            def _(act):
                for n, (b, sign) in enumerate(jobs):
                    act.wait_ge(self.pe_done.sem, self.pe_done.at(b + 1))
                    if n >= 2:
                        act.wait_ge(self.dve_done.sem, self.dve_done.at(n - 1))
                    nc.scalar.activation(A(E + 512 * (n % 2), 512), self.bank[b][:, :], ACT.Exp, scale=sign).then_inc(self.act_done.up(), 1)
                nc.scalar.activation(actT[:, at["EB"]:at["EB"] + 8], dims(self.bank[0][:, 63:], [64, 8]), ACT.Exp)
                nc.scalar.activation(actT[:, at["EB"] + 8:at["EB"] + 16], dims(self.bank[2][:, 0:], [64, 8]), ACT.Exp)
                for d in range(2):
                    act.wait_ge(self.pe_done.sem, self.pe_done.at(6 + d))
                    act.wait_ge(self.dve_done.sem, self.dve_done.at(6))
                    nc.scalar.activation(A(KTOK + d * T, T), self.bank[5 + d][:, :], ACT.Copy)

            @block.vector
            def _(dve):
                for n in range(6):
                    dve.wait_ge(self.act_done.sem, self.act_done.at(n + 1))
                    d, what = n // 3, n % 3
                    dst, src = ((QD, QT), (KD, KTb), (KTT, KTb))[what]
                    nc.vector.scalar_tensor_tensor(A(dst + d * T, T), A(E + 512 * (n % 2), 512), 0.125 if what == 0 else 1.0,
                                                   A(src, T), ALU.mult, ALU.mult).then_inc(self.dve_done.up(), 1)
                if pair == 0:
                    nc.vector.memset(actT[:, at["ATT"]:at["ATT"] + 1024], 0.0)

        with self.stage() as block:
            @block.tensor
            def _(pe):
                for d in range(2):
                    for n in range(7):
                        c = order[d][n]
                        t, half = c // 2, c % 2
                        for h in range(2):
                            rows = slice(64 * half, 64 * half + 64)
                            mm = nc.tensor.matmul(
                                self.bank[4 + 2 * d + half][64 * h:64 * h + 64, t * P:(t + 1) * P],
                                self.arena[rows, KTOK + d * T + t * P + 64 * h:KTOK + d * T + t * P + 64 * h + 64],
                                self.arena[rows, at["VB"] + t * 512 + (2 * pair + h) * P:at["VB"] + t * 512 + (2 * pair + h + 1) * P],
                                start=True, stop=True)
                mm.then_inc(self.pe_done.up(), 1)
                for h in range(2):
                    for d in range(2):
                        for t in range(4):
                            rows = slice(64 * h, 64 * h + 64)
                            mm = nc.tensor.matmul(self.bank[2 * h + d][:, t * P:(t + 1) * P],
                                                  self.arena[rows, KD + d * T + t * P:KD + d * T + (t + 1) * P],
                                                  self.arena[rows, QD + d * T + t * P:QD + d * T + (t + 1) * P], start=True, stop=True)
                        mm.then_inc(self.pe_done.up(), 1)

            @block.vector
            def _(dve):
                link = self.linker(dve, self.dve_chain)
                dve.wait_ge(self.pe_done.sem, self.pe_done.at(1))
                for n in range(1, 8):
                    for d in range(2):
                        c = order[d][n - 1]
                        add = self.bank[4 + 2 * d + c % 2][:, (c // 2) * P:(c // 2 + 1) * P]
                        if n == 1:
                            ins = nc.vector.tensor_copy(states(d, order[d][1]), add)
                        else:
                            ins = nc.vector.scalar_tensor_tensor(states(d, order[d][n]), states(d, c),
                                                                 actT[:, at["EB"] + 8 * d + c:at["EB"] + 8 * d + c + 1], add,
                                                                 ALU.mult, ALU.add)
                    link(ins)
                for n in range(4):
                    h, d = n // 2, n % 2
                    dve.wait_ge(self.pe_done.sem, self.pe_done.at(2 + n))
                    link(nc.vector.copy_predicated(dims(actT[:, at["ATT"] + h * P:], [256, 4], [1, P]),
                                                   dims(A(GT + 640 + 256 * d, 1).bitcast(I32), [0, 4], [1, P]),
                                                   dims(self.bank[n][:, 0:], [P, 4], [1, P])))

        with self.stage() as block:
            @block.tensor
            def _(pe):
                for h in range(2):
                    for t in range(4):
                        bank, col = self.bank[2 * h + t // 2], t % 2 * P
                        rows = slice(64 * h, 64 * h + 64)
                        nc.tensor.matmul(bank[:, col:col + P], actT[:, at["ATT"] + t * 256 + h * P:at["ATT"] + t * 256 + (h + 1) * P],
                                         A(at["VB"] + t * 512 + (2 * pair + h) * P, P), start=True, stop=False, skip_group_check=True)
                        rest = [(half, d) for half in range(2) for d in range(2) if 2 * t + half != order[d][0]]
                        for i, (half, d) in enumerate(rest):
                            c = 2 * t + half
                            mm = nc.tensor.matmul(bank[64 * half:64 * half + 64, col:col + P],
                                                  self.arena[rows, QD + d * T + c * 64:QD + d * T + c * 64 + 64],
                                                  states(d, c)[rows, :], start=False, stop=(i == len(rest) - 1), skip_group_check=True)
                        if t % 2:
                            mm.then_inc(self.pe_done.up(), 1)

            @block.scalar
            def _(act):
                for n in range(4):
                    h, t = n // 2, 2 * (n % 2)
                    act.wait_ge(self.pe_done.sem, self.pe_done.at(n + 1))
                    nc.scalar.activation(dims(A(at["O"] + t * D + 512 + (2 * pair + h) * P, 1), [D, 2], [1, P]),
                                         dims(self.bank[n][:, 0:], [P, 2], [1, P]), ACT.Copy)

    def plan_experts(self, layer):
        I = self.I
        self.expert_slots = self.expert_sources(layer, 0)
        for e in range(NE):
            for src, k, n in self.expert_sources(layer, e):
                self.plan(src, k, n)

    def expert_sources(self, layer, e):
        I, H = self.I, DE // 2
        pick = lambda w: w[layer][bass.ds(e, 1), :, :]
        cols = lambda w, c: pick(w)[:, :, c * H:(c + 1) * H].rearrange("o (k p) n -> p (o k) n", p=P)
        rows = lambda w, c: pick(w)[:, c * H:(c + 1) * H, :].rearrange("o (k p) n -> p (o k) n", p=P)
        g, u, d = I["moe_w_gate"], I["moe_w_up"], I["moe_w_down"]
        return [(cols(g, 0), KT, H), (cols(g, 1), KT, H), (cols(u, 0), KT, H), (cols(u, 1), KT, H),
                (rows(d, 0), 2, D), (rows(d, 1), 2, D)]

    def moe(self, layer, nt):
        nc, I, A, misc = self.nc, self.I, self.A, self.misc
        Z, Y, YS, Q, PW, PK, XS, SG, HT = 0, 4096, 8192, 9216, 9728, 10240, 10752, 11776, 12288
        RS, WT, WR, BL, M, W0 = 12800, 12932, 13100, 13400, 13440, 13568
        z_t, y_t = (lambda t: A(Z + t * D, D)), (lambda t: A(Y + t * D, D))

        self.st_transpose(z_t, nt, self.put_pure, self.modulated(z_t, 3))

        def tok(t, k):
            return self.actT[:, k * T + t * P:k * T + (t + 1) * P]

        L, GL, GM, GI, GF, GE, ES, EM, EI, EF = [W0 + 160 * i for i in range(10)]
        TMP, C1, V = W0 + 1600, W0 + 1800, W0 + 1900
        self.OV = W0 + 2000
        X = AX_X
        with self.stage() as block:
            @block.gpsimd
            def _(pool):
                self.load_params(pool, [
                    (A(WR, 288).rearrange("p (k n) -> p k n", k=KT)[:, :, 0:NG], I["moe_w_grp"][layer].rearrange("(k p) n -> p k n", p=P)),
                    (A(WR, 288).rearrange("p (k n) -> p k n", k=KT)[:, :, NG:36], I["moe_w_rexp"][layer].rearrange("(k p) n -> p k n", p=P)),
                    (A(BL, NG), rows_to_all(I["moe_b_grp"][layer], NG)), (A(BL + NG, NE), rows_to_all(I["moe_b_rexp"][layer], NE))])

            @block.scalar
            def _(act):
                act.wait_ge(self.dve_done.sem, self.dve_done.at(1))
                nc.scalar.activation(A(GE, 4 * nt), A(GE, 4 * nt), ACT.Exp).then_inc(self.act_done.up(), 1)
                act.wait_ge(self.dve_done.sem, self.dve_done.at(2))
                nc.scalar.activation(A(V, nt), A(V, nt), ACT.Exp).then_inc(self.act_done.up(), 1)

            @block.tensor
            def _(pe):
                pe.wait_ge(self.params_in.sem, self.params_in.at(64))
                for t in range(nt):
                    for k in range(KT):
                        mm = nc.tensor.matmul(self.bank[t][:, 0:36], tok(t, k), A(WR + 36 * k, 36), start=(k == 0), stop=(k == KT - 1))
                    mm.then_inc(self.pe_done.up(), 1)
                pe.wait_ge(self.dve_done.sem, self.dve_done.at(3))
                for t in range(nt + 1):
                    for u in range(min(t, nt - 1) + 1):
                        mm = nc.tensor.matmul(self.bank[4][:, NE * t:NE * (t + 1)], self.before if u == t else self.ones,
                                              A(M + NE * u, NE), start=(u == 0), stop=(u == min(t, nt - 1)))
                mm.then_inc(self.pe_done.up(), 1)

            @block.vector
            def _(dve):
                link = self.linker(dve, self.dve_chain)
                V_ = nc.vector
                dve.wait_ge(self.params_in.sem, self.params_in.at(64))
                V_.memset(A(GL, 8 * nt), -3.0e38)
                for t in range(nt):
                    dve.wait_ge(self.pe_done.sem, self.pe_done.at(t + 1))
                    ins = V_.tensor_tensor(A(L + 36 * t, 36), self.bank[t][:, 0:36], A(BL, 36), ALU.add)
                link(ins)
                link(V_.tensor_copy(dims(A(GL, 1), [8, nt], [1, NG]), dims(A(L, 1), [36, nt], [1, NG])))
                for t in range(nt):
                    ins = V_.max(A(GM + 8 * t, 8), A(GL + 8 * t, 8))
                link(ins)
                for t in range(nt):
                    ins = V_.max_index(A(GI + 8 * t, 8).bitcast(U32), A(GM + 8 * t, 8), A(GL + 8 * t, 8))
                link(ins)
                V_.tensor_tensor(dims(A(GE, 1), [4, nt], [1, NG]), dims(A(L, 1), [36, nt], [1, NG]),
                                 dims(A(GM, 1), [8, nt], [0, NG]), ALU.subtract).then_inc(self.dve_done.up(), 1)
                link(V_.tensor_copy(A(GF, 8 * nt), A(GI, 8 * nt).bitcast(U32)))
                link(V_.tensor_tensor(dims(A(GI, 1), [4, nt], [1, NG]), dims(self.iota, [0, nt], [1, NG]),
                                      dims(A(GF, 1), [8, nt], [0, NG]), ALU.is_equal))
                for t in range(nt):
                    ins = V_.tensor_tensor(dims(A(TMP + 32 * t, 1), [4, EPG], [1, NG]), dims(A(L + 36 * t + NG, 1), [1, EPG], [EPG, NG]),
                                           dims(A(GI + 4 * t, 1), [0, EPG], [1, NG]), ALU.mult)
                link(ins)
                link(V_.tensor_reduce(A(ES, 8 * nt), dims(A(TMP, 1), [4, 8 * nt], [1, NG]), X, ALU.add))
                for t in range(nt):
                    ins = V_.max(A(EM + 8 * t, 8), A(ES + 8 * t, 8))
                link(ins)
                for t in range(nt):
                    ins = V_.max_index(A(EI + 8 * t, 8).bitcast(U32), A(EM + 8 * t, 8), A(ES + 8 * t, 8))
                link(ins)
                V_.tensor_tensor(A(V, nt), dims(A(EM + 1, 1), [8, nt]), dims(A(EM, 1), [8, nt]), ALU.subtract).then_inc(self.dve_done.up(), 1)
                link(V_.tensor_copy(A(EF, 8 * nt), A(EI, 8 * nt).bitcast(U32)))
                for r in range(2):
                    ins = V_.tensor_tensor(dims(A(ES + 64 * r, 1), [8, nt], [1, EPG]), dims(self.iota, [0, nt], [1, EPG]),
                                           dims(A(EF + r, 1), [8, nt], [0, EPG]), ALU.is_equal)
                link(ins)
                link(V_.tensor_tensor(A(EM, 8 * nt), A(ES, 8 * nt), A(ES + 64, 8 * nt), ALU.add))
                for t in range(nt):
                    ins = V_.tensor_tensor(dims(A(M + NE * t, 1), [EPG, NG], [1, EPG]), dims(A(GI + 4 * t, 1), [1, NG], [0, EPG]),
                                           dims(A(EM + 8 * t, 1), [0, NG], [1, EPG]), ALU.mult)
                ins.then_inc(self.dve_done.up(), 1)
                dve.wait_ge(self.act_done.sem, self.act_done.at(2))
                V_.tensor_reduce(A(C1, nt), dims(A(GE, 1), [4, nt], [1, NG]), X, ALU.add)
                link(V_.tensor_scalar(A(C1 + 8, nt), A(V, nt), 1.0, None, ALU.add))
                link(V_.tensor_tensor(A(C1, nt), A(C1, nt), A(C1 + 8, nt), ALU.mult))
                link(V_.reciprocal(A(C1, nt), A(C1, nt)))
                link(V_.tensor_tensor(A(C1 + 8, nt), A(C1, nt), A(V, nt), ALU.mult))
                for t in range(nt):
                    ins = V_.tensor_scalar(A(EF + 8 * t, 8), A(ES + 8 * t, 8), A(C1 + t, 1), None, ALU.mult)
                link(ins)
                for t in range(nt):
                    ins = V_.scalar_tensor_tensor(A(EF + 8 * t, 8), A(ES + 64 + 8 * t, 8), A(C1 + 8 + t, 1), A(EF + 8 * t, 8), ALU.mult, ALU.add)
                link(ins)
                V_.memset(A(WT, 33 * nt), 0.0)
                link(V_.memset(A(RS, 33 * nt), -1.0))
                for t in range(nt):
                    ins = V_.tensor_tensor(dims(A(WT + t, 1), [EPG * nt, NG], [nt, EPG]), dims(A(GI + 4 * t, 1), [1, NG], [0, EPG]),
                                           dims(A(EF + 8 * t, 1), [0, NG], [1, EPG]), ALU.mult)
                dve.wait_ge(self.pe_done.sem, self.pe_done.at(nt + 1))
                for t in range(nt):
                    ins = V_.scalar_tensor_tensor(dims(A(RS + t, 1), [nt, NE]), self.bank[4][:, NE * t:NE * (t + 1)], 1.0,
                                                  A(M + NE * t, NE), ALU.add, ALU.mult)
                link(ins)
                link(V_.tensor_scalar(A(RS, NE * nt), A(RS, NE * nt), 1.0, None, ALU.subtract))
                self.overflow_tables(link, nt)

        pk = lambda i: A(PK + 256 * i, S * nt)
        xs = lambda i: A(XS + 512 * i, 512)
        xs_k = lambda i, k: A(XS + 512 * i + S * k, S)
        sg, ht = (lambda i: A(SG + 256 * i, 256)), (lambda i: A(HT + 256 * i, 256))
        sm = self.sem
        start = self.used
        base_w = self.weights_used.total
        PAIRS = NE // 2
        bank = self.bank

        def per_turn(name, n):
            sm[name].up(n * PAIRS)
            return sm[name].sem, sm[name].base

        def pick(e, i):
            return nc.vector.tensor_tensor(dims(A(PK + 256 * i, 1), [S, nt], [1, S]), dims(self.iota, [0, nt], [1, S]),
                                           dims(A(RS, 33 * nt)[:, bass.ds(e * nt, nt)], [1, nt], [0, S]), ALU.is_equal)

        def gather(i):
            for k in range(KT):
                for t in range(nt):
                    mm = nc.tensor.matmul(bank[2 + i][:, S * k:S * (k + 1)], z_t(t)[:, k * P:(k + 1) * P],
                                          A(PK + 256 * i + S * t, S), start=(t == 0), stop=(t == nt - 1))
            return mm

        with self.stage() as block:
            @block.vector
            def _(dve):
                nc.vector.memset(A(Y, D * nt), 0.0)
                nc.vector.memset(A(YS, D), 0.0).then_inc(sm["ys_ready"].up(), 1)
                nc.vector.memset(A(Q, 512), 0.0).then_inc(sm["turn_out"].up(), 1)
                pick(0, 0).then_inc(self.dve_done.up(), 1)

            @block.tensor
            def _(pe):
                pe.wait_ge(self.dve_done.sem, self.dve_done.at(1))
                gather(0).then_inc(sm["gather_done"].up(), 1)

            @block.scalar
            def _(act):
                act.wait_ge(sm["gather_done"].sem, sm["gather_done"].at(1))
                nc.scalar.activation(xs(0), bank[2][:, :], ACT.Copy).then_inc(sm["xs_ready"].up(), 1)

        with self.stage() as block:
            gateup_done, b_gu = per_turn("gateup_done", 2)
            down_done, b_dn = per_turn("down_done", 2)
            gather_done, b_ga = per_turn("gather_done", 2)
            turned, b_tu = per_turn("turned", 1)
            sum_done, b_su = per_turn("sum_done", 2 * nt)
            xs_ready, b_xs = per_turn("xs_ready", 2)
            silu_done, b_si = per_turn("silu_done", 2)
            ys_ready, b_ys = per_turn("ys_ready", 2)
            h_ready, b_h = per_turn("h_ready", 2)
            pick_ready, b_pk = per_turn("pick_ready", 2)
            weigh_ready, b_we = per_turn("weigh_ready", 1)
            turn_out, b_to = per_turn("turn_out", 1)
            added, b_ad = per_turn("added", 2 * nt)
            used4 = self.weights_used.up(4 * NE)

            def slot_free(sp, j, e):
                if j == 3:
                    sp.wait_ge(gateup_done, e + b_gu + 1)
                elif j == 5:
                    sp.wait_ge(down_done, e + b_dn + 1)
                else:
                    sp.wait_ge(used4, e * 4 + (base_w + 1 + min(j, 3)))

            @block.sync
            def _(sp):
                assert self.sent == start + R
                with sp.Fori(0, NE - 1) as e:
                    for j, (src, k, n) in enumerate(self.expert_sources(layer, e + 1)):
                        slot_free(sp, j, e)
                        s = (start + j) % R
                        sp.dma_start(self.ring[:, s * SLOT:(s + 1) * SLOT].rearrange("p (k n) -> p k n", k=k),
                                     src).then_inc(self.loaded[s], 16)
                self.sent = start + 6 * NE
                for j in range(6):
                    w = start + 6 * (NE - 1) + j
                    self.freed[w] = (gateup_done, b_gu + NE) if j == 3 else (down_done, b_dn + NE) if j == 5 else \
                        (used4, base_w + 4 * (NE - 1) + 1 + min(j, 3))
                self.used = start + 6 * NE
                self.feed(sp, self.used + R)

            @block.tensor
            def _(pe):
                def piece(j, i, p):
                    w = start + j
                    pe.wait_ge(self.loaded[w % R], p * 32 + (16 * (w // R + 1) + 16 * i))
                    s = w % R
                    _, k, n = self.expert_slots[j]
                    return self.ring[:, s * SLOT:(s + 1) * SLOT].rearrange("p (k n) -> p k n", k=k)

                def gateup(i, p):
                    for j in range(4):
                        w = piece(j, i, p)
                        for f in range(2):
                            col = 256 * (j // 2) + S * (2 * (j % 2) + f)
                            for k in range(KT):
                                mm = nc.tensor.matmul(bank[i][:, col:col + S], w[:, k, f * P:(f + 1) * P], xs_k(i, k),
                                                      start=(k == 0), stop=(k == KT - 1))
                        mm.then_inc(used4 if j < 3 else gateup_done, 1)

                def down(i, p):
                    for j in range(2):
                        w = piece(4 + j, i, p)
                        for half in range(2):
                            for f in range(2):
                                mm = nc.tensor.matmul(bank[4 + half][64 * i:64 * i + 64, :], A(HT + 256 * i + S * (2 * j + f), S),
                                                      w[:, f, half * 512:(half + 1) * 512], start=(j == 0 and f == 0),
                                                      stop=(j == 1 and f == 1))
                        mm.then_inc(down_done if j else used4, 1)

                with pe.Fori(0, PAIRS) as p:
                    pe.wait_ge(xs_ready, p * 2 + b_xs)
                    gateup(0, p)
                    pe.wait_ge(turn_out, p + b_to)
                    pe.wait_ge(ys_ready, p * 2 + b_ys)
                    for n in range(2 * nt):
                        t, half = n // 2, n % 2
                        if n >= 2:
                            pe.wait_ge(added, p * (2 * nt) + (b_ad + n - 1))
                        nc.tensor.matmul(bank[6 + half][:, :], A(Q + t * P, P), A(YS + half * 512, 512),
                                         start=True, stop=True).then_inc(sum_done, 1)
                    pe.wait_ge(pick_ready, p * 2 + (b_pk + 1))
                    gather(1).then_inc(gather_done, 1)
                    pe.wait_ge(h_ready, p * 2 + (b_h + 1))
                    down(0, p)
                    pe.wait_ge(xs_ready, p * 2 + (b_xs + 1))
                    gateup(1, p)
                    pe.wait_ge(weigh_ready, p + (b_we + 1))
                    pe.wait_ge(added, p * (2 * nt) + (b_ad + 2 * nt))
                    for t in range(nt):
                        mm = nc.tensor.transpose(bank[6][:, t * P:(t + 1) * P], A(PW + t * P, P), self.ident)
                    mm.then_inc(turned, 1)
                    pe.wait_ge(pick_ready, p * 2 + (b_pk + 2))
                    gather(0).then_inc(gather_done, 1)
                    pe.wait_ge(h_ready, p * 2 + (b_h + 2))
                    down(1, p)

            @block.scalar
            def _(act):
                def silu(i, p):
                    act.wait_ge(gateup_done, p * 2 + (b_gu + 1 + i))
                    nc.scalar.activation(sg(i), bank[i][:, 0:256], ACT.Silu).then_inc(silu_done, 1)

                def take_xs(i, p, n):
                    act.wait_ge(gather_done, p * 2 + (b_ga + n))
                    nc.scalar.activation(xs(i), bank[2 + i][:, :], ACT.Copy).then_inc(xs_ready, 1)

                def take_ys(i, p):
                    act.wait_ge(down_done, p * 2 + (b_dn + 1 + i))
                    rows = slice(64 * i, 64 * i + 64)
                    for half in range(2):
                        ins = nc.scalar.activation(self.arena[rows, YS + half * 512:YS + half * 512 + 512], bank[4 + half][rows, :], ACT.Copy)
                    ins.then_inc(ys_ready, 1)

                with act.Fori(0, PAIRS) as p:
                    silu(0, p)
                    take_xs(1, p, 1)
                    take_ys(0, p)
                    silu(1, p)
                    take_xs(0, p, 2)
                    take_ys(1, p)

            @block.vector
            def _(dve):
                def h(i, p):
                    dve.wait_ge(silu_done, p * 2 + (b_si + 1 + i))
                    nc.vector.tensor_tensor(ht(i), sg(i), bank[i][:, 256:512], ALU.mult).then_inc(h_ready, 1)

                def weigh(i, e):
                    return nc.vector.tensor_tensor(dims(A(PW + S * i, 1), [P, nt], [1, S]), dims(A(PK + 256 * i, 1), [S, nt], [1, S]),
                                                   dims(A(WT, 33 * nt)[:, bass.ds(e * nt, nt)], [1, nt], [0, S]), ALU.mult)

                with dve.Fori(0, PAIRS) as p:
                    dve.wait_ge(gather_done, p * 2 + b_ga)
                    pick(2 * p + 1, 1).then_inc(pick_ready, 1)
                    h(0, p)
                    dve.wait_ge(pick_ready, p * 2 + (b_pk + 1))
                    weigh(0, 2 * p)
                    weigh(1, 2 * p + 1).then_inc(weigh_ready, 1)
                    for n in range(2 * nt):
                        t, half = n // 2, n % 2
                        dve.wait_ge(sum_done, p * (2 * nt) + (b_su + n + 1))
                        y = A(Y + t * D + half * 512, 512)
                        nc.vector.tensor_tensor(y, y, bank[6 + half][:, :], ALU.add).then_inc(added, 1)
                    dve.wait_ge(weigh_ready, p + (b_we + 1))
                    pick(2 * p + 2, 0).then_inc(pick_ready, 1)
                    h(1, p)
                    dve.wait_ge(turned, p + (b_tu + 1))
                    nc.vector.tensor_copy(A(Q, P * nt), bank[6][:, 0:P * nt]).then_inc(turn_out, 1)

        with self.stage() as block:
            @block.tensor
            def _(pe):
                for n in range(2 * nt):
                    nc.tensor.matmul(bank[n][:, :], A(Q + n // 2 * P, P), A(YS + n % 2 * 512, 512),
                                     start=True, stop=True).then_inc(self.pe_done.up(), 1)

            @block.vector
            def _(dve):
                for n in range(2 * nt):
                    dve.wait_ge(self.pe_done.sem, self.pe_done.at(n + 1))
                    y = A(Y + n * 512, 512)
                    nc.vector.tensor_tensor(y, y, bank[n][:, :], ALU.add)

        self.overflow(layer, nt)
        self.st_add_norm(y_t, nt, 5, I["ln2_g"][layer], I["ln2_b"][layer], A(YS, 2048))

    def overflow_tables(self, link, nt):
        nc, A, V_ = self.nc, self.A, self.nc.vector
        n_ob = self.n_overflow(nt)
        CNT, NB, CUM, EID, OFF, FIN = [self.OV + 32 * i for i in range(6)]
        IND = OVW
        assert FIN + 48 <= OVW
        link(V_.tensor_copy(A(CNT, NE), self.bank[4][:, NE * nt:NE * (nt + 1)]))
        for k in range(1, nt * P // S):
            link(V_.tensor_scalar(A(NB, NE), A(CNT, NE), float(S * k), None, ALU.is_gt) if k == 1 else
                 V_.scalar_tensor_tensor(A(NB, NE), A(CNT, NE), float(S * k), A(NB, NE), ALU.is_gt, ALU.add))
        link(V_.tensor_tensor_scan(A(CUM, NE), self.ones[:, 0:NE], A(NB, NE), 0.0, ALU.mult, ALU.add))
        link(V_.tensor_tensor(dims(A(IND, 1), [NE, n_ob], [1, NE]), dims(A(CUM, 1), [0, n_ob], [1, NE]),
                              dims(self.iota, [1, n_ob], [0, NE]), ALU.is_le))
        link(V_.tensor_reduce(A(EID, n_ob), dims(A(IND, 1), [NE, n_ob], [1, NE]), AX_X, ALU.add))
        link(V_.tensor_tensor(dims(A(IND, 1), [NE, n_ob], [1, NE]), dims(A(IND, 1), [NE, n_ob], [1, NE]),
                              dims(A(NB, 1), [0, n_ob], [1, NE]), ALU.mult))
        link(V_.tensor_reduce(A(OFF, n_ob), dims(A(IND, 1), [NE, n_ob], [1, NE]), AX_X, ALU.add))
        link(V_.tensor_tensor(A(OFF, n_ob), self.iota[:, 0:n_ob], A(OFF, n_ob), ALU.subtract))
        V_.tensor_scalar(A(OFF, n_ob), A(OFF, n_ob), 1.0, float(S), ALU.add, ALU.mult)
        V_.tensor_copy(A(FIN, 1).bitcast(I32), A(CUM + NE - 1, 1))
        V_.tensor_copy(A(FIN + 1, n_ob).bitcast(I32), A(EID, n_ob))
        self.OFF, self.FIN = OFF, FIN

    def n_overflow(self, nt):
        return 2 * nt * P // (S + 1)

    def overflow(self, layer, nt):
        nc, A, bank = self.nc, self.A, self.bank
        Z, Y, YS, Q, PW, PK, XS, SG, HT, RS, WT = 0, 4096, 8192, 9216, 9728, 10240, 10752, 11776, 12288, 12800, 12932
        OFF, FIN, n_ob = self.OFF, self.FIN, self.n_overflow(nt)
        ld, pe_ov, act_ov, dve_ov = self.ov[layer]
        piece = lambda j: self.arena[:, OVW + (j % 4) * SLOT:OVW + (j % 4 + 1) * SLOT]
        rank = lambda e: dims(A(RS, 33 * nt)[:, bass.ds(e * nt, nt)], [1, nt])

        def blocks(eng):
            return eng.value_load(A(FIN, 1)[0:1, :].bitcast(I32), min_val=0, max_val=n_ob)

        def expert(eng, ob):
            return eng.value_load(A(FIN + 1, n_ob)[0:1, bass.ds(ob, 1)].bitcast(I32), min_val=0, max_val=NE - 1)

        with self.stage() as block:
            @block.sync
            def _(sp):
                there = blocks(sp)
                with sp.Fori(0, n_ob) as ob:
                    with sp.If(there > ob):
                        e = expert(sp, ob)
                        for j, (src, k, n) in enumerate(self.expert_sources(layer, e)):
                            if j == 0:
                                sp.wait_ge(dve_ov, ob * 4 + 1)
                            if j == 4:
                                sp.wait_ge(pe_ov, ob * 5 + 2)
                            sp.dma_start(piece(j).rearrange("p (k n) -> p k n", k=k), src).then_inc(ld[j], 16)

            @block.vector
            def _(dve):
                there = blocks(dve)
                with dve.Fori(0, n_ob) as ob:
                    with dve.If(there > ob):
                        e = expert(dve, ob)
                        nc.vector.tensor_tensor(A(SG + 256, nt), rank(e), dims(A(OFF, n_ob)[:, bass.ds(ob, 1)], [0, nt]),
                                                ALU.subtract).then_inc(dve_ov, 1)
                        dve.wait_ge(dve_ov, ob * 4 + 1)
                        nc.vector.tensor_tensor(dims(A(PK, 1), [S, nt], [1, S]), dims(self.iota, [0, nt], [1, S]),
                                                dims(A(SG + 256, nt), [1, nt], [0, S]), ALU.is_equal).then_inc(dve_ov, 1)
                        dve.wait_ge(dve_ov, ob * 4 + 2)
                        nc.vector.tensor_tensor(dims(A(PW, 1), [P, nt], [1, S]), dims(A(PK, 1), [S, nt], [1, S]),
                                                dims(A(WT, 33 * nt)[:, bass.ds(e * nt, nt)], [1, nt], [0, S]), ALU.mult).then_inc(dve_ov, 1)
                        dve.wait_ge(act_ov, ob * 4 + 2)
                        nc.vector.tensor_tensor(A(HT, 256), A(SG, 256), bank[0][:, 256:512], ALU.mult).then_inc(dve_ov, 1)
                        dve.wait_ge(pe_ov, ob * 5 + 5)
                        for n in range(2 * nt):
                            y = A(Y + n * 512, 512)
                            nc.vector.tensor_tensor(y, y, bank[n][:, :], ALU.add)

            @block.scalar
            def _(act):
                there = blocks(act)
                with act.Fori(0, n_ob) as ob:
                    with act.If(there > ob):
                        act.wait_ge(pe_ov, ob * 5 + 1)
                        nc.scalar.activation(A(XS, 512), bank[2][:, :], ACT.Copy).then_inc(act_ov, 1)
                        act.wait_ge(pe_ov, ob * 5 + 2)
                        nc.scalar.activation(A(SG, 256), bank[0][:, 0:256], ACT.Silu).then_inc(act_ov, 1)
                        act.wait_ge(pe_ov, ob * 5 + 3)
                        nc.scalar.activation(self.arena[0:64, Q:Q + P * nt], bank[6][0:64, 0:P * nt], ACT.Copy).then_inc(act_ov, 1)
                        act.wait_ge(pe_ov, ob * 5 + 4)
                        for half in range(2):
                            ins = nc.scalar.activation(self.arena[0:64, YS + half * 512:YS + half * 512 + 512], bank[4 + half][0:64, :], ACT.Copy)
                        ins.then_inc(act_ov, 1)

            @block.tensor
            def _(pe):
                there = blocks(pe)
                with pe.Fori(0, n_ob) as ob:
                    with pe.If(there > ob):
                        pe.wait_ge(dve_ov, ob * 4 + 2)
                        for k in range(KT):
                            for t in range(nt):
                                mm = nc.tensor.matmul(bank[2][:, S * k:S * (k + 1)], A(Z + t * D + k * P, P), A(PK + S * t, S),
                                                      start=(t == 0), stop=(t == nt - 1))
                        mm.then_inc(pe_ov, 1)
                        pe.wait_ge(act_ov, ob * 4 + 1)
                        for j in range(4):
                            pe.wait_ge(ld[j], ob * 16 + 16)
                            w = piece(j).rearrange("p (k n) -> p k n", k=KT)
                            for f in range(2):
                                col = 256 * (j // 2) + S * (2 * (j % 2) + f)
                                for k in range(KT):
                                    mm = nc.tensor.matmul(bank[0][:, col:col + S], w[:, k, f * P:(f + 1) * P], A(XS + S * k, S),
                                                          start=(k == 0), stop=(k == KT - 1))
                        mm.then_inc(pe_ov, 1)
                        pe.wait_ge(dve_ov, ob * 4 + 3)
                        for t in range(nt):
                            mm = nc.tensor.transpose(bank[6][:, t * P:(t + 1) * P], A(PW + t * P, P), self.ident)
                        mm.then_inc(pe_ov, 1)
                        pe.wait_ge(dve_ov, ob * 4 + 4)
                        for j in range(2):
                            pe.wait_ge(ld[4 + j], ob * 16 + 16)
                            w = piece(4 + j).rearrange("p (k n) -> p k n", k=2)
                            for half in range(2):
                                for f in range(2):
                                    mm = nc.tensor.matmul(bank[4 + half][0:64, :], A(HT + S * (2 * j + f), S), w[:, f, half * 512:(half + 1) * 512],
                                                          start=(j == 0 and f == 0), stop=(j == 1 and f == 1))
                        mm.then_inc(pe_ov, 1)
                        pe.wait_ge(act_ov, ob * 4 + 4)
                        for n in range(2 * nt):
                            mm = nc.tensor.matmul(bank[n][:, :], self.arena[0:64, Q + n // 2 * P:Q + n // 2 * P + P],
                                                  self.arena[0:64, YS + n % 2 * 512:YS + n % 2 * 512 + 512], start=True, stop=True)
                        mm.then_inc(pe_ov, 1)

    def st_attention(self, n, ncomp, operands, value, scale, dv, out_at, P0, lam=None):
        nc, A, sm, bank = self.nc, self.A, self.sem, self.bank
        score_done, max_done, exp_done, mix_done, turned, aT_ready, o_done, o_out = (
            sm[k] for k in ("score_done", "max_done", "exp_done", "mix_done", "turned", "aT_ready", "o_done", "o_out"))
        prob = lambda i, c: A(P0 + (i % 2) * 1024 + c * 512, 512)
        mixed = lambda i: A(P0 + 2048 + (i % 2) * 512, 512)
        aT = lambda i: A(P0 + 3072 + (i % 2) * 512, 512)
        small = lambda i, k: self.stat[:, 16 * (i % 2) + k:16 * (i % 2) + k + 1]
        MAX, SUM, REC, LAMREC = 0, 4, 8, 12
        source = (lambda i: mixed(i)) if ncomp == 2 else (lambda i: prob(i, 0))

        with self.stage() as block:
            @block.tensor
            def _(pe):
                def scores(i):
                    if i >= 2:
                        pe.wait_ge(exp_done.sem, exp_done.at(i - 1))
                    for c in range(ncomp):
                        q, k = operands(i, c)
                        mm = nc.tensor.matmul(bank[2 * (i % 2) + c][:, :], q, k, start=True, stop=True)
                    mm.then_inc(score_done.up(), 1)

                def turn(i):
                    pe.wait_ge(mix_done.sem, mix_done.at(i + 1))
                    if i >= 2:
                        pe.wait_ge(aT_ready.sem, aT_ready.at(i - 1))
                    for j in range(4):
                        mm = nc.tensor.transpose(bank[4 + i % 2][:, j * P:(j + 1) * P], source(i)[:, j * P:(j + 1) * P], self.ident)
                    mm.then_inc(turned.up(), 1)

                def values(i):
                    pe.wait_ge(aT_ready.sem, aT_ready.at(i + 1))
                    if i >= 2:
                        pe.wait_ge(o_out.sem, o_out.at(i - 1))
                    for j in range(4):
                        mm = nc.tensor.matmul(bank[6 + i % 2][:, 0:dv], aT(i)[:, j * P:(j + 1) * P], value(i, j),
                                              start=(j == 0), stop=(j == 3))
                    mm.then_inc(o_done.up(), 1)

                scores(0)
                scores(1)
                for i in range(n):
                    turn(i)
                    if i >= 1:
                        values(i - 1)
                    if i + 2 < n:
                        scores(i + 2)
                values(n - 1)

            @block.vector
            def _(dve):
                link = self.linker(dve, self.dve_chain)

                def maxima(i):
                    dve.wait_ge(score_done.sem, score_done.at(i + 1))
                    if i >= 2:
                        dve.wait_ge(exp_done.sem, exp_done.at(i - 1))
                    for c in range(ncomp):
                        ins = nc.vector.tensor_reduce(small(i, MAX + c), bank[2 * (i % 2) + c][:, :], AX_X, ALU.max, negate=True)
                    link(ins)
                    nc.vector.tensor_scalar(dims(small(i, MAX), [1, ncomp]), dims(small(i, MAX), [1, ncomp]), scale, None,
                                            ALU.mult).then_inc(max_done.up(), 1)

                def mix(i):
                    dve.wait_ge(exp_done.sem, exp_done.at(i + 1))
                    if i >= 2:
                        dve.wait_ge(turned.sem, turned.at(i - 1))
                        dve.wait_ge(o_out.sem, o_out.at(i - 1))
                    rec = nc.vector.reciprocal(dims(small(i, REC), [1, ncomp]), dims(small(i, SUM), [1, ncomp]))
                    if ncomp == 1:
                        rec.then_inc(mix_done.up(), 1)
                        return
                    link(rec)
                    link(nc.vector.tensor_tensor(small(i, LAMREC), small(i, REC + 1), lam(i), ALU.mult))
                    link(nc.vector.tensor_scalar(mixed(i), prob(i, 1), small(i, LAMREC), None, ALU.mult))
                    nc.vector.scalar_tensor_tensor(mixed(i), prob(i, 0), small(i, REC), mixed(i), ALU.mult,
                                                   ALU.subtract).then_inc(mix_done.up(), 1)

                maxima(0)
                for i in range(n):
                    if i + 1 < n:
                        maxima(i + 1)
                    mix(i)

            @block.scalar
            def _(act):
                def exps(i):
                    act.wait_ge(max_done.sem, max_done.at(i + 1))
                    if i >= 2:
                        act.wait_ge(mix_done.sem, mix_done.at(i - 1))
                        act.wait_ge(turned.sem, turned.at(i - 1))
                    for c in range(ncomp):
                        ins = nc.scalar.activation(prob(i, c), bank[2 * (i % 2) + c][:, :], ACT.Exp, bias=small(i, MAX + c),
                                                   scale=scale, accum_out=small(i, SUM + c))
                    ins.then_inc(exp_done.up(), 1)

                def take_turned(i):
                    act.wait_ge(turned.sem, turned.at(i + 1))
                    if i >= 2:
                        act.wait_ge(o_done.sem, o_done.at(i - 1))
                    nc.scalar.activation(aT(i), bank[4 + i % 2][:, :], ACT.Copy).then_inc(aT_ready.up(), 1)

                def take_out(i):
                    act.wait_ge(o_done.sem, o_done.at(i + 1))
                    nc.scalar.activation(out_at(i), bank[6 + i % 2][:, 0:dv], ACT.Copy,
                                         scale=1.0 if ncomp == 2 else small(i, REC)).then_inc(o_out.up(), 1)

                exps(0)
                for i in range(n):
                    if i + 1 < n:
                        exps(i + 1)
                    take_turned(i)
                    if i >= 1:
                        take_out(i - 1)
                take_out(n - 1)

    def st_unmix(self, buf):
        nc = self.nc
        with self.stage() as block:
            @block.gpsimd
            def _(pool):
                self.load_params(pool, [(buf[64 * (t % 2):64 * (t % 2) + 64, (t // 2) * D:(t // 2 + 1) * D],
                                         self.xres[0:64, t * D:(t + 1) * D]) for t in range(4)])

            @block.vector
            def _(dve):
                dve.wait_ge(self.params_in.sem, self.params_in.at(64))
                nc.vector.tensor_copy(self.xres[:, 0:2 * D], buf)

    def mixer_c(self):
        nc, I, A = self.nc, self.I, self.A
        QR, K, V, QT, KTT, O, XX = 0, 2048, 6144, 10240, 12288, 16384, 18432
        self.st_transpose(lambda t: A(t * D, D), 4, self.put_mixed, self.modulated(lambda t: A(t * D, D), 0))
        self.st_unmix(A(0, 2048))

        def dest(c, t):
            base = (QR, K, V)[c // 2]
            return A(base + t * D + 512 * (c % 2), 512)
        self.st_linear(lambda m, k: self.actT[:, k * T + m * P:k * T + m * P + P],
                       [(2, [0, 1], 512)] * 2 + [(2, [0, 1, 2, 3], 512)] * 4, dest)
        LQ = XX + 2048 + 256
        LAM = LQ + 2048
        with self.stage() as block:
            @block.gpsimd
            def _(pool):
                self.load_params(pool, [(A(XX, 256).rearrange("p (t n) -> p t n", t=2), I["k_rope_c"].rearrange("(t p) n -> p t n", p=P))] +
                                 [(A(LQ + 512 * i, 512), rows_to_all(I[n][0].rearrange("h d -> (h d)"), 512))
                                  for i, n in enumerate(("c_lq1", "c_lk1", "c_lq2", "c_lk2"))])

            @block.vector
            def _(dve):
                link = self.linker(dve, self.dve_chain)
                dve.wait_ge(self.params_in.sem, self.params_in.at(80))
                for base in (QR, K):
                    for t in range(2):
                        link(self.rope(link, A(base + t * D, D), 16, 64, 64, 16, A(XX + 128 * t, 64), A(XX + 128 * t + 64, 64),
                                       A(XX + 256, 2048)))
                for i in range(2):
                    ins = nc.vector.tensor_tensor(A(LQ + 1024 * i, 512), A(LQ + 1024 * i, 512), A(LQ + 1024 * i + 512, 512), ALU.mult)
                link(ins)
                for i in range(2):
                    ins = nc.vector.tensor_reduce(A(LAM + 8 * i, 8), dims(A(LQ + 1024 * i, 1), [64, 8], [1, 64]), AX_X, ALU.add)
                ins.then_inc(self.dve_done.up(), 1)
                dve.wait_ge(self.act_done.sem, self.act_done.at(1))
                nc.vector.scalar_tensor_tensor(A(LAM, 8), A(LAM, 8), LAM_INIT, A(LAM + 8, 8), ALU.add, ALU.subtract)

            @block.scalar
            def _(act):
                act.wait_ge(self.dve_done.sem, self.dve_done.at(1))
                nc.scalar.activation(A(LAM, 16), A(LAM, 16), ACT.Exp).then_inc(self.act_done.up(), 1)

        self.st_transpose(lambda t: A(QR + t * D, D), 2, lambda t, g: dims(A(QT + 4 * g * SEQ + t * P, 1), [SEQ, 4], [1, P]))
        self.st_transpose(lambda t: A(K + t * D, D), 4, lambda t, g: dims(A(KTT + 4 * g * T + t * P, 1), [T, 4], [1, P]))

        def operands(i, c):
            h, t = i // 2, i % 2
            rows = slice(64 * c, 64 * c + 64)
            return (self.arena[rows, QT + h * SEQ + t * P:QT + h * SEQ + (t + 1) * P], self.arena[rows, KTT + h * T:KTT + (h + 1) * T])
        self.st_attention(16, 2, operands, lambda i, j: A(V + j * D + (i // 2) * P, P), 64 ** -0.5, P,
                          lambda i: A(O + (i % 2) * D + (i // 2) * P, P), 0, lambda i: A(LAM + i // 2, 1))
        GN = XX
        with self.stage() as block:
            @block.gpsimd
            def _(pool):
                self.load_params(pool, [(A(GN, D), rows_to_all(I["c_subln_g"][0], D))])
                self.rstd(pool, 16, self.dve_done.at(1))

            @block.vector
            def _(dve):
                link = self.linker(dve, self.dve_chain)
                self.moments(link, lambda i: [A(O + i * P, P)], 16, LN_EPS, False).then_inc(self.dve_done.up(), 1)
                dve.wait_ge(self.params_in.sem, self.params_in.at(16))
                link(nc.vector.tensor_scalar(A(GN, D), A(GN, D), 1.0 - LAM_INIT, None, ALU.mult))
                dve.wait_ge(self.pool_done.sem, self.pool_done.at(1))
                for i in range(16):
                    nc.vector.scalar_tensor_tensor(A(O + i * P, P), A(O + i * P, P), self.stat[:, i:i + 1],
                                                   A(GN + (i % 8) * P, P), ALU.mult, ALU.mult)

        self.st_transpose(lambda t: A(O + t * D, D), 2, self.put_pure)
        self.st_linear(lambda m, k: self.actT[:, k * T + m * P:k * T + m * P + P], [(2, [0, 1], 512)] * 2,
                       lambda c, t: A(t * D + 512 * c, 512))
        self.st_add_norm(lambda t: A(t * D, D), 2, 2, I["ln1_g"][1], I["ln1_b"][1], A(4096, 2048))

    def st_rms_mod(self, src, z, nt, g_row, i_shift, G):
        nc, A = self.nc, self.A
        with self.stage() as block:
            @block.gpsimd
            def _(pool):
                self.load_params(pool, [(A(G, D), rows_to_all(g_row, D))])
                self.rstd(pool, nt, self.dve_done.at(1))

            @block.vector
            def _(dve):
                link = self.linker(dve, self.dve_chain)
                self.moments(link, lambda t: [src(t)[:, 0:512], src(t)[:, 512:D]], nt, RMS_EPS, False).then_inc(self.dve_done.up(), 1)
                dve.wait_ge(self.params_in.sem, self.params_in.at(16))
                dve.wait_ge(self.pool_done.sem, self.pool_done.at(1))
                for t in range(nt):
                    ins = nc.vector.scalar_tensor_tensor(z(t), src(t), self.stat[:, t:t + 1], A(G, D), ALU.mult, ALU.mult)
                link(ins)
                for t in range(nt):
                    ins = nc.vector.scalar_tensor_tensor(z(t), self.mod_row(i_shift + 1), 1.0, z(t), ALU.add, ALU.mult)
                link(ins)
                for t in range(nt):
                    nc.vector.tensor_tensor(z(t), z(t), self.mod_row(i_shift), ALU.add)

    def st_add(self, y, nt, i_gate):
        nc = self.nc
        with self.stage() as block:
            @block.vector
            def _(dve):
                link = self.linker(dve, self.dve_chain)
                for t in range(nt):
                    ins = nc.vector.tensor_tensor(y(t), y(t), self.mod_row(i_gate), ALU.mult)
                link(ins)
                for t in range(nt):
                    nc.vector.tensor_tensor(self.x_tile(t), self.x_tile(t), y(t), ALU.add)

    def st_group_rms(self, rows, G, g_row, width, more=None):
        nc, A = self.nc, self.A
        n = len(rows)
        with self.stage() as block:
            @block.gpsimd
            def _(pool):
                self.load_params(pool, [(A(G, width), rows_to_all(g_row, width))])
                self.rstd(pool, n, self.dve_done.at(1))

            @block.vector
            def _(dve):
                link = self.linker(dve, self.dve_chain)
                self.moments(link, lambda i: [rows[i]], n, RMS_EPS, False).then_inc(self.dve_done.up(), 1)
                dve.wait_ge(self.params_in.sem, self.params_in.at(16))
                dve.wait_ge(self.pool_done.sem, self.pool_done.at(1))
                for i in range(n):
                    nc.vector.scalar_tensor_tensor(rows[i], rows[i], self.stat[:, i:i + 1], A(G, width), ALU.mult, ALU.mult)

    def mixer_mla(self):
        nc, I, A = self.nc, self.I, self.A
        CQ, KV, UF, CQT, CKT, QM, KM, VM = 0, 768, 1920, 2944, 3712, 4736, 6272, 9344
        QT, KTT, FT, O, XX = 11392, 13440, 17536, 19584, 20608
        Z = 0
        with self.stage() as block:
            @block.gpsimd
            def _(pool):
                self.load_params(pool, [(self.arena[0:64, Z + t * D:Z + (t + 1) * D],
                                         self.xres[64 * (t % 2):64 * (t % 2) + 64, (t // 2) * D:(t // 2 + 1) * D]) for t in range(4)] +
                    [(self.arena[64:128, Z:Z + 4 * D].rearrange("p (t d) -> p t d", t=4), I["ctx_2"][0].rearrange("(t p) d -> p t d", p=64))])
                pool.wait_ge(self.params_in.sem, self.params_in.at(80))

        z = lambda t: A(Z + t * D, D)
        self.st_rms_mod(z, z, 4, I["norm1_g_2"][0], 0, 4096)
        self.st_transpose(z, 4, self.put_mixed)
        self.st_linear(lambda m, k: self.actT[:, k * T + m * P:k * T + m * P + P],
                       [(2, [0, 1], 384), (2, [0, 1, 2, 3], 288), (2, [0, 1], 512)],
                       lambda c, t: A((CQ + 384 * t, KV + 288 * t, UF + 512 * t)[c], (384, 288, 512)[c]))
        self.st_group_rms([A(CQ + 384 * t, 384) for t in range(2)], XX, I["a_q_ln_g_2"][0], 384)
        self.st_group_rms([A(KV + 288 * t, 256) for t in range(4)], XX, I["a_kv_ln_g_2"][0], 256)
        self.st_transpose(lambda t: A(CQ + 384 * t, 384), 2, lambda t, g: dims(A(CQT + t * P, 1), [SEQ, 3], [1, P]), nb=3)
        self.st_transpose(lambda t: A(KV + 288 * t, 288), 4, lambda t, g: dims(A(CKT + t * P, 1), [T, 2], [1, P]), nb=2)
        self.st_linear(lambda m, k: A(CQT + k * SEQ + m * P, P), [(1, [0, 1], 384)] * 2, lambda c, t: A(QM + 768 * t + 384 * c, 384))
        self.st_linear(lambda m, k: A(CKT + k * T + m * P, P), [(1, [0, 1, 2, 3], 512)] * 2,
                       lambda c, t: A(XX + 512 * t, 512) if c == 0 else A(VM + 512 * t, 512))
        with self.stage() as block:
            @block.vector
            def _(dve):
                for t in range(4):
                    nc.vector.tensor_copy(dims(A(KM + 768 * t, 1), [96, 8], [1, 64]), dims(A(XX + 512 * t, 1), [64, 8], [1, 64]))
                    nc.vector.tensor_copy(dims(A(KM + 768 * t + 64, 1), [96, 8], [1, 32]), dims(A(KV + 288 * t + 256, 1), [0, 8], [1, 32]))
        self.st_group_rms([A(QM + 96 * i, 96) for i in range(16)], XX, I["a_q_norm_g_2"][0], 96)
        self.st_group_rms([A(KM + 96 * i, 96) for i in range(32)], XX, I["a_k_norm_g_2"][0], 96)
        DT, DC = XX + 1024, XX + 2048
        with self.stage() as block:
            @block.gpsimd
            def _(pool):
                self.load_params(pool, [(A(XX, 128).rearrange("p (t n) -> p t n", t=2), I["k_rope_m"].rearrange("(t p) n -> p t n", p=P)),
                                        (A(DT, 1024), I["k_dft_tok"]), (A(DC, 256), I["k_dft_ch"])])

            @block.vector
            def _(dve):
                link = self.linker(dve, self.dve_chain)
                dve.wait_ge(self.params_in.sem, self.params_in.at(48))
                for base in (QM, KM):
                    for t in range(2):
                        link(self.rope(link, A(base + 768 * t + 64, 704), 8, 96, 32, 16, A(XX + 64 * t, 32), A(XX + 64 * t + 32, 32),
                                       A(XX + 128, 512)))

            @block.tensor
            def _(pe):
                pe.wait_ge(self.params_in.sem, self.params_in.at(48))
                for g in range(4):
                    for t in range(2):
                        mm = nc.tensor.matmul(self.bank[g][:, :], A(UF + 512 * t + g * P, P), A(DT + 512 * t, 512), start=(t == 0), stop=(t == 1))
                    mm.then_inc(self.pe_done.up(), 1)
                for g in range(4):
                    pe.wait_ge(self.act_done.sem, self.act_done.at(g + 1))
                    for n in range(2):
                        mm = nc.tensor.matmul(self.bank[4 + g][:, 0:SEQ], A(DC + n * P, P), A(FT + 512 * g + n * SEQ, SEQ),
                                              start=(n == 0), stop=(n == 1))
                    mm.then_inc(self.pe_done.up(), 1)

            @block.scalar
            def _(act):
                for g in range(4):
                    act.wait_ge(self.pe_done.sem, self.pe_done.at(g + 1))
                    nc.scalar.activation(A(FT + 512 * g, 512), self.bank[g][:, :], ACT.Copy).then_inc(self.act_done.up(), 1)
                for g in range(4):
                    act.wait_ge(self.pe_done.sem, self.pe_done.at(5 + g))
                    nc.scalar.activation(self.actT[:, (4 + g) * T:(4 + g) * T + SEQ], self.bank[4 + g][:, 0:SEQ], ACT.Copy)

        self.st_transpose(lambda t: A(QM + 768 * t, 768), 2, lambda t, g: dims(self.arena[0:96, QT + 4 * g * SEQ + t * P:], [SEQ, 4], [1, P]), bw=96)
        self.st_transpose(lambda t: A(KM + 768 * t, 768), 4, lambda t, g: dims(self.arena[0:96, KTT + 4 * g * T + t * P:], [T, 4], [1, P]), bw=96)

        def operands(i, c):
            h, t = i // 2, i % 2
            return self.arena[0:96, QT + h * SEQ + t * P:QT + h * SEQ + (t + 1) * P], self.arena[0:96, KTT + h * T:KTT + (h + 1) * T]
        self.st_attention(16, 1, operands, lambda i, j: A(VM + 512 * j + 64 * (i // 2), 64), 96 ** -0.5, 64,
                          lambda i: A(O + (i % 2) * 512 + (i // 2) * 64, 64), 0)
        self.st_transpose(lambda t: A(O + t * 512, 512), 2, self.put_pure, nb=4)
        self.st_linear(lambda m, k: self.actT[:, k * T + m * P:k * T + m * P + P], [(2, [0, 1], 512)] * 2,
                       lambda c, t: A(t * D + 512 * c, 512))
        self.st_add(lambda t: A(t * D, D), 2, 2)

    def plan_ffn(self, l):
        I, H = self.I, 256
        n = D_FF // H
        for j in range(n + 1):
            if j < n:
                self.plan_linear(I["ffn_w1_2"][l], j * H, (j + 1) * H, width=H, ks=8)
                self.plan_linear(I["ffn_w3_2"][l], j * H, (j + 1) * H, width=H, ks=8)
            if j >= 1:
                self.plan(I["ffn_w2_2"][l][(j - 1) * H:j * H, :].rearrange("(k p) n -> p k n", p=P), 2, D)

    def ffn(self, l):
        nc, I, A, bank, sm = self.nc, self.I, self.A, self.bank, self.sem
        Z, SG, H, TMP = 0, 2048, 3072, 4096
        z = lambda t: A(Z + t * D, D)
        self.st_rms_mod(self.x_tile, z, 2, I["norm2_g_2"][l], 3, 4096)
        self.st_transpose(z, 2, self.put_pure)
        n = D_FF // 256
        gateup_done, silu_done, h_ready, down_done = (sm[k] for k in ("gateup_done", "silu_done", "h_ready", "down_done"))
        with self.stage() as block:
            @block.tensor
            def _(pe):
                def gateup(j):
                    if j >= 2:
                        pe.wait_ge(h_ready.sem, h_ready.at(j - 1))
                    for which in range(2):
                        self.arrived(pe, self.used)
                        w = self.slot(self.used)
                        for f in range(2):
                            for k in range(KT):
                                mm = nc.tensor.matmul(bank[2 * (j % 2) + which][:, f * SEQ:(f + 1) * SEQ], w[:, k, f * P:(f + 1) * P],
                                                      self.actT[:, k * T:k * T + SEQ], start=(k == 0), stop=(k == KT - 1))
                        c = gateup_done if which else self.weights_used
                        mm.then_inc(c.up(), 1)
                        self.frees(self.used, c)
                        self.used += 1

                def down(j):
                    pe.wait_ge(h_ready.sem, h_ready.at(j + 1))
                    self.arrived(pe, self.used)
                    w = self.slot(self.used)
                    for f in range(2):
                        for t in range(2):
                            for half in range(2):
                                mm = nc.tensor.matmul(bank[4 + 2 * t + half][:, :], A(H + 512 * (j % 2) + f * SEQ + t * P, P),
                                                      w[:, f, half * 512:(half + 1) * 512], start=(j == 0 and f == 0),
                                                      stop=(j == n - 1 and f == 1))
                    mm.then_inc(down_done.up(), 1)
                    self.frees(self.used, down_done)
                    self.used += 1

                gateup(0)
                for j in range(n):
                    if j + 1 < n:
                        gateup(j + 1)
                    down(j)

            @block.sync
            def _(sp):
                self.feed(sp, self.used + R)

            @block.scalar
            def _(act):
                for j in range(n):
                    act.wait_ge(gateup_done.sem, gateup_done.at(j + 1))
                    if j >= 2:
                        act.wait_ge(h_ready.sem, h_ready.at(j - 1))
                    nc.scalar.activation(A(SG + 512 * (j % 2), 512), bank[2 * (j % 2)][:, :], ACT.Silu).then_inc(silu_done.up(), 1)

            @block.vector
            def _(dve):
                link = self.linker(dve, self.dve_chain)
                for j in range(n):
                    dve.wait_ge(silu_done.sem, silu_done.at(j + 1))
                    if j >= 2:
                        dve.wait_ge(down_done.sem, down_done.at(j - 1))
                    nc.vector.tensor_tensor(A(H + 512 * (j % 2), 512), A(SG + 512 * (j % 2), 512), bank[2 * (j % 2) + 1][:, :],
                                            ALU.mult).then_inc(h_ready.up(), 1)
                dve.wait_ge(down_done.sem, down_done.at(n))
                for q in range(4):
                    ins = nc.vector.tensor_tensor(A(TMP + 512 * q, 512), bank[4 + q][:, :], self.mod_row(5)[:, (q % 2) * 512:(q % 2) * 512 + 512], ALU.mult)
                link(ins)
                nc.vector.tensor_tensor(self.xres[:, 0:2 * D], self.xres[:, 0:2 * D], A(TMP, 2048), ALU.add)

    def mixer_conv(self):
        nc, I, A, bank, actT = self.nc, self.I, self.A, self.bank, self.actT
        U, CB, SB_, CV, XC, SQ, RW, PC = 2048, 7168, 8400, 9600, 10624, 11648, 12672, 13200
        z = lambda t: A(t * D, D)
        CW, SW = 288, 260
        self.st_rms_mod(self.x_tile, z, 2, I["norm1_g_2"][1], 0, 4096)
        self.st_transpose(z, 2, self.put_pure)
        rows = [("b_conf_dw_2", 31), ("b_sc_dw_2", 3), ("b_conf_dw_b_2", 1), ("b_conf_ln_g_2", 1), ("b_conf_ln_b_2", 1)]
        with self.stage() as block:
            @block.tensor
            def _(pe):
                for j in range(10):
                    if j >= 6:
                        on_act = (j - 6) % 2 == 0
                        c = self.act_done if on_act else self.dve_done
                        pe.wait_ge(c.sem, c.at((j - 6) // 2 + 1))
                    self.arrived(pe, self.used)
                    w = self.slot(self.used)
                    for f in range(2):
                        for k in range(KT):
                            mm = nc.tensor.matmul(bank[j % 6][:, f * SEQ:(f + 1) * SEQ], w[:, k, f * P:(f + 1) * P],
                                                  actT[:, k * T:k * T + SEQ], start=(k == 0), stop=(k == KT - 1))
                    mm.then_inc(self.pe_done.up(), 1)
                    self.frees(self.used, self.pe_done)
                    self.used += 1
                pe.wait_ge(self.params_in.sem, self.params_in.at(80))
                for c in range(4):
                    mm = nc.tensor.transpose(bank[6][:, 64 * c:64 * c + 37], self.arena[0:37, RW + c * P:RW + (c + 1) * P], self.ident[0:37, 0:37])
                mm.then_inc(self.pe_done.up(), 1)

            @block.sync
            def _(sp):
                self.feed(sp, self.used + R)

            @block.gpsimd
            def _(pool):
                at, pairs = 0, []
                for name, k in rows:
                    src = I[name][0] if k > 1 else I[name]
                    pairs.append((self.arena[at:at + k, RW:RW + 512], src))
                    at += k
                self.load_params(pool, pairs)

            @block.scalar
            def _(act):
                for j in range(0, 10, 2):
                    act.wait_ge(self.pe_done.sem, self.pe_done.at(j + 1))
                    nc.scalar.activation(A(U + 512 * j, 512), bank[j % 6][:, :], ACT.Sigmoid if j == 2 else ACT.Copy).then_inc(self.act_done.up(), 1)
                act.wait_ge(self.dve_done.sem, self.dve_done.at(2))
                nc.scalar.activation(A(U + 512 * 3, 512), A(U + 512 * 3, 512), ACT.Sigmoid)

            @block.vector
            def _(dve):
                for j in range(1, 10, 2):
                    dve.wait_ge(self.pe_done.sem, self.pe_done.at(j + 1))
                    nc.vector.tensor_copy(A(U + 512 * j, 512), bank[j % 6][:, :]).then_inc(self.dve_done.up(), 1)
                dve.wait_ge(self.pe_done.sem, self.pe_done.at(11))
                nc.vector.tensor_copy(dims(A(PC, 1), [40, 4], [1, 37]), dims(bank[6][:, 0:], [64, 4], [1, 37]))

        par = lambda c, i: A(PC + 40 * c + i, 1)
        with self.stage() as block:
            @block.vector
            def _(dve):
                link = self.linker(dve, self.dve_chain)
                V_ = nc.vector
                V_.memset(A(CB, 4 * CW), 0.0)
                link(V_.memset(A(SB_, 4 * SW), 0.0))
                V_.tensor_tensor(dims(A(CB + 15, 1), [CW, 4], [1, SEQ]), dims(A(U, 1), [SEQ, 4], [1, SEQ]),
                                 dims(A(U + 1024, 1), [SEQ, 4], [1, SEQ]), ALU.mult)
                link(V_.tensor_tensor(dims(A(SB_ + 1, 1), [SW, 4], [1, SEQ]), dims(A(U + 3072, 1), [SEQ, 4], [1, SEQ]),
                                      dims(A(U + 4096, 1), [SEQ, 4], [1, SEQ]), ALU.mult))
                for tap in range(31):
                    for c in range(4):
                        acc, x = A(CV + SEQ * c, SEQ), A(CB + CW * c + tap, SEQ)
                        ins = V_.tensor_scalar(acc, x, par(c, 0), par(c, 34), ALU.mult, ALU.add) if tap == 0 else \
                            V_.scalar_tensor_tensor(acc, x, par(c, tap), acc, ALU.mult, ALU.add)
                    link(ins)
                V_.engine_nop
                V_.tensor_copy(self.stat[:, 0:1], self.stat[:, 0:1]) if False else None
                V_.memset(self.stat[:, 0:1], 0.0).then_inc(self.dve_done.up(), 1)
                for tap in range(3):
                    for c in range(4):
                        acc, x = A(SQ + SEQ * c, SEQ), A(SB_ + SW * c + tap, SEQ)
                        ins = V_.tensor_scalar(acc, x, par(c, 31), None, ALU.mult) if tap == 0 else \
                            V_.scalar_tensor_tensor(acc, x, par(c, 31 + tap), acc, ALU.mult, ALU.add)
                    link(ins)
                link(V_.tensor_tensor(dims(actT[:, 4 * T:], [T, 4], [1, SEQ]), dims(A(SQ, 1), [SEQ, 4], [1, SEQ]),
                                      dims(A(U + 2048, 1), [SEQ, 4], [1, SEQ]), ALU.mult))
                dve.wait_ge(self.pe_done.sem, self.pe_done.at(1))
                for b in range(2):
                    ins = V_.tensor_tensor(A(XC + 512 * b, 512), A(CV + 512 * b, 512), bank[b][:, :], ALU.subtract)
                link(ins)
                V_.tensor_tensor(A(SQ, 1024), A(XC, 1024), A(XC, 1024), ALU.mult).then_inc(self.dve_done.up(), 1)
                dve.wait_ge(self.pe_done.sem, self.pe_done.at(2))
                for b in range(2):
                    ins = V_.tensor_scalar(A(CV + 512 * b, 512), bank[2 + b][:, :], RMS_EPS, None, ALU.add)
                ins.then_inc(self.dve_done.up(), 1)
                dve.wait_ge(self.pool_done.sem, self.pool_done.at(1))
                V_.tensor_tensor(A(XC, 1024), A(XC, 1024), A(CV, 1024), ALU.mult).then_inc(self.dve_done.up(), 1)

            @block.tensor
            def _(pe):
                for n, src in enumerate((CV, SQ)):
                    pe.wait_ge(self.dve_done.sem, self.dve_done.at(n + 1))
                    for b in range(2):
                        mm = nc.tensor.matmul(bank[2 * n + b][:, :], self.mean_of, A(src + 512 * b, 512), start=True, stop=True)
                    mm.then_inc(self.pe_done.up(), 1)

            @block.gpsimd
            def _(pool):
                pool.wait_ge(self.dve_done.sem, self.dve_done.at(3))
                nc.gpsimd.tensor_tensor(A(CV, 1024), A(CV, 1024), dims(self.pw[:, 0:], [0, 1024]), ALU.pow).then_inc(self.pool_done.up(), 1)

            @block.scalar
            def _(act):
                act.wait_ge(self.dve_done.sem, self.dve_done.at(4))
                for c in range(4):
                    nc.scalar.activation(actT[:, c * T:c * T + SEQ], A(XC + SEQ * c, SEQ), ACT.Silu, bias=par(c, 36), scale=par(c, 35))

        self.st_linear(lambda m, k: actT[:, k * T + m * P:k * T + m * P + P], [(2, [0, 1], 512)] * 2,
                       lambda c, t: A(t * D + 512 * c, 512))
        self.st_add(lambda t: A(t * D, D), 2, 2)

    def run(self):
        I = self.I
        for l in range(2):
            self.plan_linear(I["ada_w"][l], 0, 6 * D)
            if l == 0:
                self.plan_linear(I["ab_w_in"][0], 0, 3584)
                self.plan_linear(I["ab_w_in"][0], 3584, 3616, ks=8)
                self.plan_linear(I["ab_w_out"][0], 0, D)
            else:
                self.plan_linear(I["c_w_qkv"][0], 0, 3 * D)
                self.plan_linear(I["c_w_out"][0], 0, D)
            self.plan_experts(l)
        self.plan_linear(I["ada_w_2"][0], 0, 6 * D)
        w = I["a_w_in_2"][0]
        for lo, hi in ((0, 384), (384, 672), (672, 1184)):
            self.plan_linear(w, lo, hi)
        self.plan_linear(I["a_w_uq_2"][0].rearrange("r h d -> r (h d)"), 0, 768, width=384)
        self.plan_linear(I["a_w_uk_2"][0].rearrange("r h d -> r (h d)"), 0, 512)
        self.plan_linear(I["a_w_uv_2"][0].rearrange("r h d -> r (h d)"), 0, 512)
        self.plan_linear(I["a_w_out_2"][0], 0, D)
        self.plan_ffn(0)
        self.plan_linear(I["ada_w_2"][1], 0, 6 * D)
        self.plan_linear(I["b_w_in_2"][0], 0, 2560, width=256, ks=8)
        self.plan_linear(I["b_w_out_2"][0], 0, D)
        self.plan_ffn(1)

        self.st_setup()
        self.st_ada(12, (0, 1), I["ada_b"][0])
        self.mixer_ab()
        if self.stop("l0mix", 4): return
        self.moe(0, 4)
        if self.stop("l0", 4): return
        self.st_ada(4, (0, 1), I["ada_b"][1])
        self.st_ada(8, (0, 0), I["ada_b"][1], first=4)
        self.mixer_c()
        if self.stop("l1mix", 2): return
        self.moe(1, 2)
        if self.stop("l1", 2): return
        self.st_ada(4, (2, 3), I["ada_b_2"][0])
        self.st_ada(8, (2, 2), I["ada_b_2"][0], first=4)
        self.mixer_mla()
        if self.stop("b2mix", 2): return
        self.ffn(0)
        self.st_ada(12, (2, 2), I["ada_b_2"][1])
        self.mixer_conv()
        if self.stop("b2conv", 2): return
        self.ffn(1)
        self.store(2)
        assert self.used == len(self.W)

    def stop(self, name, nt):
        if self.debug == name:
            self.W = self.W[:self.sent]
            self.store(nt)
            return True

    def store(self, nt):
        nc = self.nc
        with self.stage() as block:
            @block.sync
            def _(sp):
                rows = self.out[0] if not self.debug else self.out
                sp.dma_start(rows.rearrange("(t p) d -> p t d", p=P), self.xres[:, 0:nt * D].rearrange("p (t d) -> p t d", t=nt)).then_inc(self.sem["stored"].up(16), 16)
                sp.wait_ge(self.sem["stored"].sem, self.sem["stored"].at(16))


def kernel(**inputs):
    import concourse.bacc as bacc
    from concourse.bass_utils import run_bass_kernel_spmd

    nc = bacc.Bacc("TRN2", target_bir_lowering=False, num_devices=1)
    arrays = {n: np.ascontiguousarray(a) for n, a in inputs.items()} | constants()
    I = {n: nc.dram_tensor(n, a.shape, mybir.dt.from_np(a.dtype), kind="ExternalInput").ap() for n, a in arrays.items()}
    out = nc.dram_tensor("out", (1, SEQ, D), F32, kind="ExternalOutput").ap()
    build_program(nc, I, out)
    result = run_bass_kernel_spmd(nc, [arrays], core_ids=[0])
    return result.results[0]["out"]
```

```python
from contextlib import ExitStack
import math

import numpy as np

import concourse.bass as bass
from concourse import mybir
from concourse.alu_op_type import AluOpType as ALU

F32 = mybir.dt.float32
BF16 = mybir.dt.bfloat16
I32 = mybir.dt.int32
U32 = mybir.dt.uint32
ACT = mybir.ActivationFunctionType
AX_X = mybir.AxisListType.X

P = 128
D = 1024
KT = D // P
SEQ = 256
T = 2 * SEQ
R = 6
SLOT = 2048
ARENA = 24192
OVW = 18176
ALPHA = 4.0 ** 0.25
LN_EPS = 1e-5
RMS_EPS = 1e-6
NG, EPG = 4, 8
NE = NG * EPG
DE = 512
S = 64
ZP = 4096
MOE_BUFFERS = (10240, 11264, 11776, 12288, 12544, 13568, 14080, 14592, 15104, 15240)
D_FF = 2816
LAM_INIT = 0.8 - 0.6 * math.exp(-0.3)


def rope_tables(head, quarter):
    tok = np.arange(SEQ)
    inv = 10000.0 ** (-np.arange(quarter, dtype=np.float64) / quarter)
    row, col = (tok // 64)[:, None] * inv, (tok % 64)[:, None] * inv
    ang = np.concatenate([row, row, col, col], 1)
    sign = np.tile(np.repeat([-1.0, 1.0], quarter), 2)
    return np.concatenate([np.cos(ang), np.sin(ang) * sign], 1).astype(np.float32)


def mla_rope_tables():
    tok = np.arange(SEQ)
    inv = 10000.0 ** (-np.arange(8, dtype=np.float64) / 8)
    ang = np.concatenate([(tok // 64)[:, None] * inv, (tok % 64)[:, None] * inv], 1)
    c, s = np.cos(ang), np.sin(ang)
    return np.concatenate([c, c, -s, s], 1).astype(np.float32)


def retention_tables():
    i, j = np.arange(SEQ)[None, :], np.arange(SEQ)[:, None]
    out = np.zeros((P, 4, 2, 2, SEQ), np.float64)
    for h in range(4):
        gf, gb = np.log1p(-2.0 ** -(5.0 + h)), np.log1p(-2.0 ** -(5.5 + h))
        within = np.where(i >= j, np.exp(gf * (i - j)), np.exp(gb * (j - i - 1)))
        across = np.exp(gf * (SEQ + i - j)) + np.exp(gb * (SEQ - 1 - i + j))
        for n, m in enumerate((within, across)):
            out[:, h, n] = m.reshape(2, P, SEQ).transpose(1, 0, 2)
    return (out * P ** -0.5).astype(np.float32).reshape(P, -1)


def gla_tables():
    j, i = np.arange(P)[:, None], np.arange(P)[None, :]
    same = (j // 64) == (i // 64)
    sums = [(same & m) / 16.0 for m in (j <= i, j > i, j >= i, j > i, j < i)]
    masks = [same & m for m in (j <= i, j <= i, j > i, j > i)]
    return np.concatenate(sums + masks, 1).astype(np.float32)


def fourier_tables():
    n = np.arange(SEQ)
    a = 2 * np.pi * np.outer(n, n) / SEQ
    tokens = np.concatenate([np.cos(a), np.sin(a)], 1)
    c = np.arange(P)
    b = 2 * np.pi * np.outer(c, c) / P
    chans = np.concatenate([np.cos(b), -np.sin(b)], 1) / math.sqrt(SEQ * P)
    return (tokens.astype(np.float32).reshape(2, P, T).transpose(1, 0, 2).reshape(P, -1).copy(),
            chans.astype(np.float32))


def misc_tables():
    j, i = np.arange(P)[:, None], np.arange(P)[None, :]
    return np.concatenate([np.eye(P), (j < i) * 1.0, np.ones((P, P)), np.tile(np.arange(P), (P, 1)),
                           np.full((P, P), 1.0 / P)], 1).astype(np.float32)


def constants():
    dft_tok, dft_ch = fourier_tables()
    return {"k_misc": misc_tables(), "k_rope_a": rope_tables(128, 32), "k_rope_c": rope_tables(64, 16),
            "k_rope_m": mla_rope_tables(), "k_ret": retention_tables(), "k_gla": gla_tables(),
            "k_dft_tok": dft_tok, "k_dft_ch": dft_ch}


class Count:

    def __init__(self, sem):
        self.sem, self.base, self.total = sem, 0, 0

    def up(self, times=1):
        self.total += times
        return self.sem

    def at(self, k):
        return self.base + k


def dims(ap, *free):
    return bass.AP(tensor=ap.tensor, offset=ap.offset, ap=[list(ap.ap[0])] + [list(f) for f in free])


def rows_to_all(ap_row, n):
    return bass.AP(tensor=ap_row.tensor, offset=ap_row.offset, ap=[[0, P], [1, n]])


def build_program(nc, I, out, debug=None):
    ctx = ExitStack()
    with ctx:
        Program(nc, ctx, I, out, debug).run()


class Program:
    def __init__(self, nc, ctx, I, out, debug):
        self.nc, self.I, self.out, self.debug = nc, I, out, debug

        def sb(name, n, dt=F32, p=P):
            return ctx.enter_context(nc.sbuf_tensor(name, [p, n], dt))

        self.counts = []

        def count(name):
            c = Count(ctx.enter_context(nc.semaphore(name)))
            self.counts.append(c)
            return c

        self.bank = [ctx.enter_context(nc.psum_tensor(f"bank{i}", [P, 512], F32)) for i in range(8)]
        self.ring = sb("ring", R * SLOT)
        self.xres = sb("xres", 4 * D)
        self.mod = sb("mod", 6 * D)
        self.actT = sb("actT", KT * T)
        self.misc = sb("misc", 5 * P)
        self.scx = sb("scx", KT * P)
        self.cols = sb("cols", 64)
        self.stat = sb("stat", 512)
        self.pw = sb("pw", 64)
        self.arena = sb("arena", ARENA)
        self.ident = self.misc[:, 0:P]
        self.before = self.misc[:, P:2 * P]
        self.ones = self.misc[:, 2 * P:3 * P]
        self.iota = self.misc[:, 3 * P:4 * P]
        self.mean_of = self.misc[:, 4 * P:5 * P]

        self.loaded = [ctx.enter_context(nc.semaphore(f"loaded{i}")) for i in range(R)]
        self.freed = {}
        self.weights_used = count("weights_used")
        self.pe_done = count("pe_done")
        self.act_done = count("act_done")
        self.dve_done = count("dve_done")
        self.pool_done = count("pool_done")
        self.params_in = count("params_in")
        self.dve_chain = count("dve_chain")
        self.act_chain = count("act_chain")
        self.pool_chain = count("pool_chain")
        self.sem = {n: count(n) for n in (
            "silu_done", "h_ready", "gather_done", "xs_ready", "pick_ready",
            "weigh_ready", "turned", "turn_out", "ys_ready", "sum_done", "added", "exp_done", "max_done",
            "score_done", "h_turned", "hT_ready", "pieces_used", "gateup_done", "down_done", "mix_done", "aT_ready", "o_out", "o_done", "stored")}
        self.ov = [([ctx.enter_context(nc.semaphore(f"ov{l}_weights{j}")) for j in range(6)],
                    *(ctx.enter_context(nc.semaphore(f"ov{l}_{n}")) for n in ("pe", "act", "dve", "slots_free"))) for l in range(2)]
        self.W = []
        self.sent = 0
        self.used = 0

    def stage(self):
        for c in self.counts:
            c.base = c.total
        return self.nc.Block(no_gpsimd_drain=True)

    def linker(self, eng, chain):
        def link(ins):
            ins.then_inc(chain.up(), 1)
            eng.wait_ge(chain.sem, chain.total)
        return link

    def plan(self, src, k, n):
        self.W.append((src, k, n))

    def plan_linear(self, w, n0, n1, width=512, ks=4):
        kt = w.shape[0] // P
        for c in range(n0, n1, width):
            e = min(c + width, n1)
            for k in range(0, kt, ks):
                kk = min(ks, kt - k)
                self.plan(w[k * P:(k + kk) * P, c:e].rearrange("(k p) n -> p k n", p=P), kk, e - c)

    def slot(self, i):
        _, k, n = self.W[i]
        s = i % R
        return self.ring[:, s * SLOT:s * SLOT + k * n].rearrange("p (k n) -> p k n", k=k)

    def feed(self, sp, upto):
        while self.sent < min(upto, len(self.W)):
            i = self.sent
            if i >= R:
                sem, value = self.freed[i - R]
                sp.wait_ge(sem, value)
            sp.dma_start(self.slot(i), self.W[i][0]).then_inc(self.loaded[i % R], 16)
            self.sent += 1

    def arrived(self, pe, i):
        pe.wait_ge(self.loaded[i % R], 16 * (i // R + 1))

    def frees(self, w, c):
        self.freed[w] = (c.sem, c.total)

    def load_params(self, pool, pairs):
        for dst, src in pairs:
            pool.dma_start(dst, src, allow_slow_non_contiguous=True).then_inc(self.params_in.up(16), 16)

    def A(self, off, n):
        assert off + n <= ARENA, (off, n)
        return self.arena[:, off:off + n]

    def st_linear(self, lhsT, chunks, dest, add=None, params=None):
        nc = self.nc
        first = self.used
        groups = []
        for ci, (ns, tiles, _) in enumerate(chunks):
            for n, m in enumerate(tiles):
                groups.append((ci, m, 4 * (ci % 2) + n, add is None and len(groups) % 2 == 0))

        def out_of(g):
            c = self.act_done if groups[g][3] else self.dve_done
            return c.sem, c.at(sum(x[3] == groups[g][3] for x in groups[:g + 1]))

        with self.stage() as block:
            @block.tensor
            def _(pe):
                g0 = 0
                for ci, (ns, tiles, ncols) in enumerate(chunks):
                    kts = sum(self.W[self.used + j][1] for j in range(ns))
                    kt = 0
                    for j in range(ns):
                        self.arrived(pe, self.used)
                        sl, kk = self.slot(self.used), self.W[self.used][1]
                        for n, m in enumerate(tiles):
                            bank = groups[g0 + n][2]
                            earlier = [q for q in range(g0) if groups[q][2] == bank]
                            if j == 0 and earlier:
                                pe.wait_ge(*out_of(earlier[-1]))
                            for k in range(kk):
                                mm = nc.tensor.matmul(self.bank[bank][:, 0:ncols], lhsT(m, kt + k), sl[:, k, 0:ncols],
                                                      start=(kt + k == 0), stop=(kt + k == kts - 1))
                            if j == ns - 1:
                                mm.then_inc(self.pe_done.up(), 1)
                        if j == ns - 1:
                            self.frees(self.used, self.pe_done)
                        else:
                            mm.then_inc(self.weights_used.up(), 1)
                            self.frees(self.used, self.weights_used)
                        kt += kk
                        self.used += 1
                    g0 += len(tiles)

            @block.sync
            def _(sp):
                self.feed(sp, self.used + R)

            if params:
                @block.gpsimd
                def _(pool):
                    self.load_params(pool, params)

            @block.scalar
            def _(act):
                for g, (ci, m, bank, on_act) in enumerate(groups):
                    if on_act:
                        act.wait_ge(self.pe_done.sem, self.pe_done.at(g + 1))
                        nc.scalar.activation(dest(ci, m), self.bank[bank][:, 0:chunks[ci][2]],
                                             ACT.Copy).then_inc(self.act_done.up(), 1)

            @block.vector
            def _(dve):
                if params:
                    dve.wait_ge(self.params_in.sem, self.params_in.at(16 * len(params)))
                for g, (ci, m, bank, on_act) in enumerate(groups):
                    if not on_act:
                        dve.wait_ge(self.pe_done.sem, self.pe_done.at(g + 1))
                        src = self.bank[bank][:, 0:chunks[ci][2]]
                        if add is None:
                            nc.vector.tensor_copy(dest(ci, m), src).then_inc(self.dve_done.up(), 1)
                        else:
                            nc.vector.tensor_tensor(dest(ci, m), src, add(ci, m), ALU.add).then_inc(self.dve_done.up(), 1)

    def st_transpose(self, src, nt, put, prep=None, nb=KT, bw=P, scale=1.0):
        nc = self.nc
        G = -(-nb // 4)
        groups = [(t, g, 4 if 4 * g + 4 <= nb else nb - 4 * g) for t in range(nt) for g in range(G)]
        assert len(groups) <= 8
        with self.stage() as block:
            def taken(eng, n):
                eng.wait_ge(self.pe_done.sem, self.pe_done.at(n + 1))
                t, g, k = groups[n]
                return put(t, g), dims(self.bank[n][0:bw, :], [P, k], [1, P])

            @block.vector
            def _(dve):
                link = self.linker(dve, self.dve_chain)
                if prep:
                    for t in range(nt):
                        prep(link, t).then_inc(self.dve_done.up(), 1)
                for n in range(1, len(groups), 2):
                    dst, bank = taken(dve, n)
                    nc.vector.tensor_scalar(dst, bank, scale, None, ALU.mult)

            @block.scalar
            def _(act):
                for n in range(0, len(groups), 2):
                    dst, bank = taken(act, n)
                    nc.scalar.activation(dst, bank, ACT.Copy, scale=scale)

            @block.tensor
            def _(pe):
                for n, (t, g, blocks) in enumerate(groups):
                    if prep and g == 0:
                        pe.wait_ge(self.dve_done.sem, self.dve_done.at(t + 1))
                    for q in range(blocks):
                        k = 4 * g + q
                        mm = nc.tensor.transpose(self.bank[n][0:bw, q * P:(q + 1) * P],
                                                 src(t)[:, k * bw:(k + 1) * bw], self.ident)
                    mm.then_inc(self.pe_done.up(), 1)

    def put_mixed(self, t, half):
        return dims(self.actT[:, 4 * half * T + 64 * t:], [T, 4], [SEQ, 2], [1, 64])

    def put_pure(self, t, half):
        return dims(self.actT[:, 4 * half * T + P * t:], [T, 4], [1, P])

    def put_for_mixed(self, t, half):
        return dims(self.actT[:, 4 * half * T + (t % 2) * SEQ + 64 * (t // 2):], [T, 4], [P, 2], [1, 64])

    def x_tile(self, t):
        return self.xres[:, t * D:(t + 1) * D]

    def mod_row(self, i):
        return self.mod[:, i * D:(i + 1) * D]

    def modulated(self, dst, i_shift):
        nc = self.nc

        def prep(link, t):
            link(nc.vector.scalar_tensor_tensor(dst(t), self.mod_row(i_shift + 1), 1.0, self.x_tile(t), ALU.add, ALU.mult))
            return nc.vector.tensor_tensor(dst(t), dst(t), self.mod_row(i_shift), ALU.add)
        return prep

    def rstd(self, pool, n, waits):
        pool.wait_ge(self.dve_done.sem, waits)
        self.nc.gpsimd.tensor_tensor(self.stat[:, 0:n], self.stat[:, 0:n], self.pw[:, 0:n],
                                     ALU.pow).then_inc(self.pool_done.up(), 1)

    def moments(self, link, views, n, eps, centred):
        nc = self.nc
        k = len(views(0))
        for i in range(n):
            for j, v in enumerate(views(i)):
                ins = nc.vector.bn_stats(self.stat[:, 192 + 6 * (k * i + j):198 + 6 * (k * i + j)], v)
        link(ins)
        for i in range(n):
            ins = nc.vector.bn_aggr(self.stat[:, 64 + 2 * i:66 + 2 * i],
                                    self.stat[:, 192 + 6 * k * i:192 + 6 * k * (i + 1)])
        link(ins)
        mean, var = dims(self.stat[:, 64:], [2, n]), dims(self.stat[:, 65:], [2, n])
        if centred:
            return nc.vector.tensor_scalar(self.stat[:, 0:n], var, 1.0, eps, ALU.mult, ALU.add)
        link(nc.vector.tensor_tensor(self.stat[:, 0:n], mean, mean, ALU.mult))
        return nc.vector.scalar_tensor_tensor(self.stat[:, 0:n], self.stat[:, 0:n], eps, var, ALU.add, ALU.add)

    def mean_at(self, i):
        return self.stat[:, 64 + 2 * i:65 + 2 * i]

    def st_add_norm(self, y, nt, i_gate, g_row, b_row, buf):
        nc = self.nc
        with self.stage() as block:
            @block.gpsimd
            def _(pool):
                self.load_params(pool, [(buf[:, 0:D], rows_to_all(g_row, D)), (buf[:, D:2 * D], rows_to_all(b_row, D))])
                self.rstd(pool, nt, self.dve_done.at(1))

            @block.vector
            def _(dve):
                link = self.linker(dve, self.dve_chain)
                for t in range(nt):
                    ins = nc.vector.tensor_tensor(y(t), y(t), self.mod_row(i_gate), ALU.mult)
                link(ins)
                for t in range(nt):
                    ins = nc.vector.scalar_tensor_tensor(self.x_tile(t), self.x_tile(t), ALPHA, y(t), ALU.mult, ALU.add)
                link(ins)
                self.moments(link, lambda t: [self.x_tile(t)[:, 0:512], self.x_tile(t)[:, 512:D]], nt, LN_EPS,
                             True).then_inc(self.dve_done.up(), 1)
                dve.wait_ge(self.pool_done.sem, self.pool_done.at(1))
                for t in range(nt):
                    ins = nc.vector.tensor_scalar(self.x_tile(t), self.x_tile(t), self.mean_at(t), self.stat[:, t:t + 1],
                                                  ALU.subtract, ALU.mult)
                link(ins)
                dve.wait_ge(self.params_in.sem, self.params_in.at(32))
                for t in range(nt):
                    ins = nc.vector.tensor_tensor(self.x_tile(t), self.x_tile(t), buf[:, 0:D], ALU.mult)
                link(ins)
                for t in range(nt):
                    nc.vector.tensor_tensor(self.x_tile(t), self.x_tile(t), buf[:, D:2 * D], ALU.add)

    def st_ada(self, n_chunks, cvecs, bias_row, first=0):
        nc = self.nc
        with self.stage() as block:
            @block.vector
            def _(dve):
                for half, v in enumerate(cvecs):
                    ins = nc.vector.tensor_copy(dims(self.scx[:, 64 * half:], [P, KT], [1, 64]),
                                                dims(self.cols[:, 8 * v:], [1, KT], [0, 64]))
                ins.then_inc(self.dve_done.up(), 1)
        lo, n = first * 512, n_chunks * 512
        self.st_linear(lambda m, k: self.scx[:, k * P:(k + 1) * P], [(2, [0], 512)] * n_chunks,
                       lambda c, m: self.mod[:, lo + c * 512:lo + (c + 1) * 512],
                       lambda c, m: self.mod[:, lo + c * 512:lo + (c + 1) * 512],
                       [(self.mod[:, lo:lo + n], rows_to_all(bias_row[lo:lo + n], n))])

    def st_setup(self):
        nc, I = self.nc, self.I
        vecs = [I["c"], I["c_ctx"], I["c_2"], I["c_ctx_2"]]
        with self.stage() as block:
            @block.sync
            def _(sp):
                self.feed(sp, R)

            @block.gpsimd
            def _(pool):
                nc.gpsimd.memset(self.pw[:, :], -0.5)
                for v, src in enumerate(vecs):
                    flat = bass.AP(tensor=src.tensor, offset=src.offset, ap=[[1, P], [P, KT]])
                    self.load_params(pool, [(self.cols[:, 8 * v:8 * v + 8], flat)])
                pool.wait_ge(self.params_in.sem, self.params_in.at(64))
                self.load_params(pool, [(self.misc[:, :], I["k_misc"])] +
                    [(self.xres[64 * s:64 * s + 64, :].rearrange("p (t d) -> p t d", t=4),
                      I[n][0].rearrange("(t p) d -> p t d", p=64)) for s, n in enumerate(("x", "ctx"))])
                pool.wait_ge(self.params_in.sem, self.params_in.at(112))

            @block.scalar
            def _(act):
                act.wait_ge(self.params_in.sem, self.params_in.at(64))
                nc.scalar.activation(self.stat[:, 0:32], self.cols[:, 0:32], ACT.Silu).then_inc(self.act_done.up(), 1)
                act.wait_ge(self.act_done.sem, self.act_done.at(1))
                nc.scalar.activation(self.cols[:, 0:32], self.stat[:, 0:32], ACT.Copy)

    def rope(self, link, view, n, step, width, quarter, cos, sin, tmp):
        nc, m = self.nc, width // quarter // 2
        t1, t2 = tmp[:, 0:n * width], tmp[:, n * width:2 * n * width]
        nc.vector.tensor_tensor(dims(t1, [width, n], [1, width]), dims(view, [step, n], [1, width]),
                                dims(cos, [0, n], [1, width]), ALU.mult)
        for k in range(2):
            part = lambda ap, s, off: dims(ap[:, off * quarter:], [s, n], [2 * quarter, m], [1, quarter])
            ins = nc.vector.tensor_tensor(part(t2, width, k), part(view, step, 1 - k), part(sin, 0, k), ALU.mult)
        link(ins)
        return nc.vector.tensor_tensor(dims(view, [step, n], [1, width]), dims(t1, [width, n], [1, width]),
                                       dims(t2, [width, n], [1, width]), ALU.add)

    def mixer_ab(self):
        nc, I = self.nc, self.I
        O, VA, G, QKB, VB, LRT, QBT, XX = 0, 4096, 6144, 10240, 12288, 14336, 14848, 16896
        A = self.A
        w_in, w_out = I["ab_w_in"][0], I["ab_w_out"][0]

        def O_t(t):
            return A(O + t * D, D)

        self.st_transpose(O_t, 4, self.put_mixed, self.modulated(O_t, 0))

        def dest(c, t):
            off = [O + t * D, O + t * D + 512, VA + t * 512, G + t * D, QKB + t * 512, VB + t * 512,
                   G + t * D + 512][c]
            return A(off, 512)
        self.st_linear(lambda m, k: self.actT[:, k * T + m * P:k * T + m * P + P],
                       [(2, [0, 1, 2, 3], 512)] * 7, dest)

        rope_at = XX + 4096
        with self.stage() as block:
            @block.gpsimd
            def _(pool):
                self.load_params(pool, [(A(rope_at, 512).rearrange("p (t n) -> p t n", t=2),
                                         I["k_rope_a"].rearrange("(t p) n -> p t n", p=P))])

            @block.tensor
            def _(pe):
                self.arrived(pe, self.used)
                sl = self.slot(self.used)
                for k in range(KT):
                    mm = nc.tensor.matmul(self.bank[0][0:32, :], sl[:, k, :], self.actT[:, k * T:(k + 1) * T],
                                          start=(k == 0), stop=(k == KT - 1))
                mm.then_inc(self.pe_done.up(), 1)
                self.frees(self.used, self.pe_done)
                self.used += 1
                for t in range(4):
                    for q in range(4):
                        mm = nc.tensor.transpose(self.bank[1 + t][:, q * P:(q + 1) * P],
                                                 A(QKB + t * 512 + q * P, P), self.ident)
                    mm.then_inc(self.pe_done.up(), 1)

            @block.sync
            def _(sp):
                self.feed(sp, self.used + R)

            @block.scalar
            def _(act):
                act.wait_ge(self.pe_done.sem, self.pe_done.at(1))
                nc.scalar.activation(self.arena[0:32, LRT:LRT + 512], self.bank[0][0:32, :], ACT.Copy)
                for t in range(4):
                    act.wait_ge(self.pe_done.sem, self.pe_done.at(2 + t))
                    nc.scalar.activation(dims(A(QBT + t * P, 1), [T, 4], [1, P]), self.bank[1 + t][:, :], ACT.Copy)

            @block.vector
            def _(dve):
                link = self.linker(dve, self.dve_chain)
                dve.wait_ge(self.params_in.sem, self.params_in.at(16))
                for t in range(2):
                    link(self.rope(link, O_t(t), 8, P, P, 32, A(rope_at + 256 * t, P), A(rope_at + 256 * t + P, P),
                                   A(rope_at + 512, 2048)))

        QAT = XX
        TAB = [QKB, QKB + 1024, XX + 4096, XX + 5120]
        self.st_transpose(O_t, 4, lambda t, half: dims(A(QAT + half * 2048 + t * P, 1), [T, 4], [1, P]))

        with self.stage() as block:
            @block.gpsimd
            def _(pool):
                self.load_params(pool, [(A(TAB[2 * i], 2048), I["k_ret"][:, 2048 * i:2048 * (i + 1)]) for i in range(2)])

            def score(h):
                b = 3 * (h % 2)
                for n, (k0, q0) in enumerate(((0, 0), (SEQ, SEQ), (SEQ, 0))):
                    for j in range(2):
                        mm = nc.tensor.matmul(self.bank[b + n][:, j * SEQ:(j + 1) * SEQ],
                                              A(QAT + 2048 + h * T + k0 + j * P, P), A(QAT + h * T + q0, SEQ),
                                              start=True, stop=True)
                mm.then_inc(self.pe_done.up(), 1)

            def att(h, n, j, t):
                off = 1536 * (h % 2) + 512 * n + SEQ * j + P * t
                return self.actT[:, off:off + P]

            @block.tensor
            def _(pe):
                score(0)
                for h in range(4):
                    if h < 3:
                        if h >= 1:
                            pe.wait_ge(self.dve_done.sem, self.dve_done.at(h))
                        score(h + 1)
                    pe.wait_ge(self.dve_done.sem, self.dve_done.at(h + 1))
                    if h >= 2:
                        pe.wait_ge(self.act_done.sem, self.act_done.at(h - 1))
                    for t in range(4):
                        parts = [(0, 0, t, 0), (0, 1, t, 1), (2, 0, t, 2), (2, 1, t, 3)] if t < 2 else \
                                [(1, 0, t - 2, 2), (1, 1, t - 2, 3)]
                        for i, (n, j, tq, v) in enumerate(parts):
                            mm = nc.tensor.matmul(self.bank[6 + h % 2][:, t * P:(t + 1) * P], att(h, n, j, tq),
                                                  A(VA + v * 512 + h * P, P), start=(i == 0), stop=(i == len(parts) - 1))
                    mm.then_inc(self.sem["mix_done"].up(), 1)

            @block.vector
            def _(dve):
                dve.wait_ge(self.params_in.sem, self.params_in.at(32))
                for h in range(4):
                    dve.wait_ge(self.pe_done.sem, self.pe_done.at(h + 1))
                    if h >= 2:
                        dve.wait_ge(self.sem["mix_done"].sem, self.sem["mix_done"].at(h - 1))
                    for n in range(3):
                        off = 1536 * (h % 2) + 512 * n
                        ins = nc.vector.tensor_tensor(self.actT[:, off:off + 512], self.bank[3 * (h % 2) + n][:, :],
                                                      A(TAB[h] + (512 if n == 2 else 0), 512), ALU.mult)
                    ins.then_inc(self.dve_done.up(), 1)

            @block.scalar
            def _(act):
                for h in range(4):
                    act.wait_ge(self.sem["mix_done"].sem, self.sem["mix_done"].at(h + 1))
                    nc.scalar.activation(dims(A(O + h * P, 1), [D, 4], [1, P]), self.bank[6 + h % 2][:, :],
                                         ACT.Copy).then_inc(self.act_done.up(), 1)

        LA, GT = XX, XX + 2048
        QD, KD, KTT, KTOK = XX + 3200, XX + 4224, XX + 5248, XX + 6272
        wlr, blr = (lambda r, c0, c1: self.actT[r, 2048 + c0:2048 + c1]), self.actT[:, 2560:3072]
        with self.stage() as block:
            @block.gpsimd
            def _(pool):
                nc.gpsimd.memset(wlr(slice(0, 32), 0, 512), 0.0).then_inc(self.pool_done.up(), 1)
                pool.wait_ge(self.pool_done.sem, self.pool_done.at(1))
                self.load_params(pool, [
                    (wlr(slice(0, 16), 0, 256), I["ab_w_lr_f"][0]), (wlr(slice(16, 32), 256, 512), I["ab_w_lr_b"][0]),
                    (blr[:, 0:256], rows_to_all(I["ab_b_lr_f"][0], 256)), (blr[:, 256:512], rows_to_all(I["ab_b_lr_b"][0], 256)),
                    (A(GT, 1152), I["k_gla"])])

            @block.tensor
            def _(pe):
                pe.wait_ge(self.params_in.sem, self.params_in.at(80))
                for t in range(4):
                    nc.tensor.matmul(self.bank[t][:, :], self.arena[0:32, LRT + t * P:LRT + (t + 1) * P],
                                     wlr(slice(0, 32), 0, 512), start=True, stop=True).then_inc(self.pe_done.up(), 1)

            @block.vector
            def _(dve):
                link = self.linker(dve, self.dve_chain)
                dve.wait_ge(self.params_in.sem, self.params_in.at(80))
                for t in range(4):
                    dve.wait_ge(self.pe_done.sem, self.pe_done.at(t + 1))
                    ins = nc.vector.tensor_tensor(A(LA + 512 * t, 512), self.bank[t][:, :], blr, ALU.add)
                link(ins)
                nc.vector.scalar_tensor_tensor(self.actT[:, 0:2048], A(LA, 2048), -1.0, A(LA, 2048), ALU.mult,
                                               ALU.max).then_inc(self.dve_done.up(), 1)
                dve.wait_ge(self.act_done.sem, self.act_done.at(2))
                nc.vector.scalar_tensor_tensor(A(LA, 2048), A(LA, 2048), 0.0, self.actT[:, 0:2048], ALU.min, ALU.subtract)

            @block.scalar
            def _(act):
                act.wait_ge(self.dve_done.sem, self.dve_done.at(1))
                nc.scalar.activation(self.actT[:, 0:2048], self.actT[:, 0:2048], ACT.Exp, scale=-1.0).then_inc(self.act_done.up(), 1)
                act.wait_ge(self.act_done.sem, self.act_done.at(1))
                nc.scalar.activation(self.actT[:, 0:2048], self.actT[:, 0:2048], ACT.Ln, bias=1.0).then_inc(self.act_done.up(), 1)

        ST, ATT, EB = 0, 2048, 3072
        for pair in range(2):
            self.gla_pair(pair, dict(O=O, VB=VB, QBT=QBT, LA=LA, GT=GT, QD=QD, KD=KD, KTT=KTT, KTOK=KTOK,
                                     ST=ST, ATT=ATT, EB=EB))

        GN = XX
        with self.stage() as block:
            @block.gpsimd
            def _(pool):
                self.load_params(pool, [(A(GN, 512), rows_to_all(I["ab_gn_a"][0], 512)), (A(GN + 512, 512), rows_to_all(I["ab_gn_b"][0], 512))])
                self.rstd(pool, 32, self.dve_done.at(1))

            @block.scalar
            def _(act):
                nc.scalar.activation(A(XX + 1024, 4096), A(G, 4096), ACT.Silu).then_inc(self.act_done.up(), 1)

            @block.vector
            def _(dve):
                link = self.linker(dve, self.dve_chain)
                link(self.moments(link, lambda i: [A(O + i * P, P)], 32, LN_EPS, True))
                mean_b = dims(self.stat[:, 64 + 8:], [16, 4], [2, 4])
                sq, var_b = dims(self.stat[:, 160:], [4, 4], [1, 4]), dims(self.stat[:, 4:], [8, 4], [1, 4])
                link(nc.vector.tensor_tensor(sq, mean_b, mean_b, ALU.mult))
                nc.vector.tensor_tensor(var_b, var_b, sq, ALU.add)
                link(nc.vector.memset(mean_b, 0.0))
                nc.vector.memset(self.stat[:, 180:181], 0.0).then_inc(self.dve_done.up(), 1)
                dve.wait_ge(self.pool_done.sem, self.pool_done.at(1))
                for i in range(32):
                    ins = nc.vector.tensor_scalar(A(O + i * P, P), A(O + i * P, P), self.mean_at(i), self.stat[:, i:i + 1],
                                                  ALU.subtract, ALU.mult)
                link(ins)
                dve.wait_ge(self.params_in.sem, self.params_in.at(32))
                for t in range(4):
                    ins = nc.vector.tensor_tensor(O_t(t), O_t(t), A(GN, D), ALU.mult)
                link(ins)
                dve.wait_ge(self.act_done.sem, self.act_done.at(1))
                nc.vector.tensor_tensor(A(O, 4096), A(O, 4096), A(XX + 1024, 4096), ALU.mult)

        self.st_transpose(O_t, 4, self.put_for_mixed)
        self.st_linear(lambda m, k: self.actT[:, k * T + m * P:k * T + m * P + P],
                       [(2, [0, 1, 2, 3], 512)] * 2, lambda c, t: A(O + t * D + 512 * c, 512))
        self.st_add_norm(O_t, 4, 2, I["ln1_g"][0], I["ln1_b"][0], A(4096, 2048))

    def gla_pair(self, pair, at):
        nc, A = self.nc, self.A
        QT, KTb = at["QBT"] + pair * T, at["QBT"] + 2 * T + pair * T
        LA, GT, QD, KD, KTT, KTOK = at["LA"], at["GT"], at["QD"], at["KD"], at["KTT"], at["KTOK"]
        actT = self.actT
        states = lambda d, c: actT[:, at["ST"] + (d * 8 + c) * P:at["ST"] + (d * 8 + c + 1) * P]
        order = [[4, 5, 6, 7, 0, 1, 2, 3], [7, 6, 5, 4, 3, 2, 1, 0]]
        E = KTOK
        with self.stage() as block:
            @block.tensor
            def _(pe):
                for b in range(5):
                    d = 0 if b < 2 else 1
                    for t in range(4):
                        mm = nc.tensor.matmul(self.bank[b][:, t * P:(t + 1) * P],
                                              A(LA + t * 512 + d * 256 + pair * P, P), A(GT + b * P, P), start=True, stop=True)
                    mm.then_inc(self.pe_done.up(), 1)
                for d in range(2):
                    pe.wait_ge(self.dve_done.sem, self.dve_done.at(3 * d + 3))
                    for t in range(4):
                        mm = nc.tensor.transpose(self.bank[5 + d][:, t * P:(t + 1) * P], A(KTT + d * T + t * P, P), self.ident)
                    mm.then_inc(self.pe_done.up(), 1)

            jobs = [(0, 1.0), (0, -1.0), (1, 1.0), (3, 1.0), (2, -1.0), (4, 1.0)]

            @block.scalar
            def _(act):
                for n, (b, sign) in enumerate(jobs):
                    act.wait_ge(self.pe_done.sem, self.pe_done.at(b + 1))
                    if n >= 2:
                        act.wait_ge(self.dve_done.sem, self.dve_done.at(n - 1))
                    nc.scalar.activation(A(E + 512 * (n % 2), 512), self.bank[b][:, :], ACT.Exp, scale=sign).then_inc(self.act_done.up(), 1)
                nc.scalar.activation(actT[:, at["EB"]:at["EB"] + 8], dims(self.bank[0][:, 63:], [64, 8]), ACT.Exp)
                nc.scalar.activation(actT[:, at["EB"] + 8:at["EB"] + 16], dims(self.bank[2][:, 0:], [64, 8]), ACT.Exp)
                for d in range(2):
                    act.wait_ge(self.pe_done.sem, self.pe_done.at(6 + d))
                    act.wait_ge(self.dve_done.sem, self.dve_done.at(6))
                    nc.scalar.activation(A(KTOK + d * T, T), self.bank[5 + d][:, :], ACT.Copy)

            @block.vector
            def _(dve):
                for n in range(6):
                    dve.wait_ge(self.act_done.sem, self.act_done.at(n + 1))
                    d, what = n // 3, n % 3
                    dst, src = ((QD, QT), (KD, KTb), (KTT, KTb))[what]
                    nc.vector.scalar_tensor_tensor(A(dst + d * T, T), A(E + 512 * (n % 2), 512), 0.125 if what == 0 else 1.0,
                                                   A(src, T), ALU.mult, ALU.mult).then_inc(self.dve_done.up(), 1)
                if pair == 0:
                    nc.vector.memset(actT[:, at["ATT"]:at["ATT"] + 1024], 0.0)

        with self.stage() as block:
            @block.tensor
            def _(pe):
                for d in range(2):
                    for n in range(7):
                        c = order[d][n]
                        t, half = c // 2, c % 2
                        for h in range(2):
                            rows = slice(64 * half, 64 * half + 64)
                            mm = nc.tensor.matmul(
                                self.bank[4 + 2 * d + half][64 * h:64 * h + 64, t * P:(t + 1) * P],
                                self.arena[rows, KTOK + d * T + t * P + 64 * h:KTOK + d * T + t * P + 64 * h + 64],
                                self.arena[rows, at["VB"] + t * 512 + (2 * pair + h) * P:at["VB"] + t * 512 + (2 * pair + h + 1) * P],
                                start=True, stop=True)
                mm.then_inc(self.pe_done.up(), 1)
                for h in range(2):
                    for d in range(2):
                        for t in range(4):
                            rows = slice(64 * h, 64 * h + 64)
                            mm = nc.tensor.matmul(self.bank[2 * h + d][:, t * P:(t + 1) * P],
                                                  self.arena[rows, KD + d * T + t * P:KD + d * T + (t + 1) * P],
                                                  self.arena[rows, QD + d * T + t * P:QD + d * T + (t + 1) * P], start=True, stop=True)
                        mm.then_inc(self.pe_done.up(), 1)

            @block.vector
            def _(dve):
                link = self.linker(dve, self.dve_chain)
                dve.wait_ge(self.pe_done.sem, self.pe_done.at(1))
                for n in range(1, 8):
                    for d in range(2):
                        c = order[d][n - 1]
                        add = self.bank[4 + 2 * d + c % 2][:, (c // 2) * P:(c // 2 + 1) * P]
                        if n == 1:
                            ins = nc.vector.tensor_copy(states(d, order[d][1]), add)
                        else:
                            ins = nc.vector.scalar_tensor_tensor(states(d, order[d][n]), states(d, c),
                                                                 actT[:, at["EB"] + 8 * d + c:at["EB"] + 8 * d + c + 1], add,
                                                                 ALU.mult, ALU.add)
                    link(ins)
                for n in range(4):
                    h, d = n // 2, n % 2
                    dve.wait_ge(self.pe_done.sem, self.pe_done.at(2 + n))
                    link(nc.vector.copy_predicated(dims(actT[:, at["ATT"] + h * P:], [256, 4], [1, P]),
                                                   dims(A(GT + 640 + 256 * d, 1).bitcast(I32), [0, 4], [1, P]),
                                                   dims(self.bank[n][:, 0:], [P, 4], [1, P])))

        with self.stage() as block:
            @block.tensor
            def _(pe):
                for h in range(2):
                    for t in range(4):
                        bank, col = self.bank[2 * h + t // 2], t % 2 * P
                        rows = slice(64 * h, 64 * h + 64)
                        nc.tensor.matmul(bank[:, col:col + P], actT[:, at["ATT"] + t * 256 + h * P:at["ATT"] + t * 256 + (h + 1) * P],
                                         A(at["VB"] + t * 512 + (2 * pair + h) * P, P), start=True, stop=False, skip_group_check=True)
                        rest = [(half, d) for half in range(2) for d in range(2) if 2 * t + half != order[d][0]]
                        for i, (half, d) in enumerate(rest):
                            c = 2 * t + half
                            mm = nc.tensor.matmul(bank[64 * half:64 * half + 64, col:col + P],
                                                  self.arena[rows, QD + d * T + c * 64:QD + d * T + c * 64 + 64],
                                                  states(d, c)[rows, :], start=False, stop=(i == len(rest) - 1), skip_group_check=True)
                        if t % 2:
                            mm.then_inc(self.pe_done.up(), 1)

            @block.scalar
            def _(act):
                for n in range(4):
                    h, t = n // 2, 2 * (n % 2)
                    act.wait_ge(self.pe_done.sem, self.pe_done.at(n + 1))
                    nc.scalar.activation(dims(A(at["O"] + t * D + 512 + (2 * pair + h) * P, 1), [D, 2], [1, P]),
                                         dims(self.bank[n][:, 0:], [P, 2], [1, P]), ACT.Copy)

    def plan_experts(self, layer):
        for p in range(NE // 2):
            for src, k, n in self.pair_sources(layer, p):
                self.plan(src, k, n)

    def pair_sources(self, layer, p):
        a, b = [self.pieces_of(lambda w: w[layer].rearrange("(h two) r c -> h two r c", two=2)[bass.ds(p, 1), i, :, :])
                for i in range(2)]
        return [piece for both in zip(b, a) for piece in both]

    def expert_sources(self, layer, e):
        return self.pieces_of(lambda w: w[layer][bass.ds(e, 1), :, :])

    def pieces_of(self, expert):
        pieces = []
        for name, k, n in (("moe_w_gate", 4, DE), ("moe_w_up", 4, DE), ("moe_w_down", 2, D)):
            w = expert(self.I[name])
            for c in range(2):
                pieces.append((w[:, c * k * P:(c + 1) * k * P, :].rearrange("o (k p) n -> p (o k) n", p=P), k, n))
        return pieces

    def moe(self, layer, nt):
        nc, I, A, misc = self.nc, self.I, self.A, self.misc
        Z, Y = 0, 0
        YS, Q, PW, PK, XS, SG, HH, HT, RS, WT = MOE_BUFFERS
        WR, BL, M, W0 = WT + 168, WT + 468, WT + 508, WT + 636
        z_t, y_t = (lambda t: A(Z + t * D, D)), (lambda t: A(Y + t * D, D))
        part = lambda i: A(ZP + 2048 * i, nt * 512).bitcast(BF16)

        self.st_transpose(z_t, nt, self.put_pure, self.modulated(z_t, 3))

        def tok(t, k):
            return self.actT[:, k * T + t * P:k * T + (t + 1) * P]

        L, GL, GM, GI, GF, GE, ES, EM, EI, EF = [W0 + 160 * i for i in range(10)]
        TMP, C1, V = W0 + 1600, W0 + 1800, W0 + 1900
        self.OV = W0 + 2000
        X = AX_X
        with self.stage() as block:
            @block.gpsimd
            def _(pool):
                self.load_params(pool, [
                    (A(WR, 288).rearrange("p (k n) -> p k n", k=KT)[:, :, 0:NG], I["moe_w_grp"][layer].rearrange("(k p) n -> p k n", p=P)),
                    (A(WR, 288).rearrange("p (k n) -> p k n", k=KT)[:, :, NG:36], I["moe_w_rexp"][layer].rearrange("(k p) n -> p k n", p=P)),
                    (A(BL, NG), rows_to_all(I["moe_b_grp"][layer], NG)), (A(BL + NG, NE), rows_to_all(I["moe_b_rexp"][layer], NE))])

                pool.wait_ge(self.act_done.sem, self.act_done.at(1))
                nc.gpsimd.tensor_tensor(A(Z, D * nt), A(Z, D * nt), part(0), ALU.subtract).then_inc(self.pool_done.up(), 1)
                pool.wait_ge(self.act_done.sem, self.act_done.at(4))
                nc.gpsimd.tensor_tensor(part(2), A(Z, D * nt), part(1), ALU.subtract).then_inc(self.pool_done.up(), 1)

            @block.scalar
            def _(act):
                nc.scalar.activation(part(0), A(Z, D * nt), ACT.Copy).then_inc(self.act_done.up(), 1)
                act.wait_ge(self.dve_done.sem, self.dve_done.at(1))
                nc.scalar.activation(A(GE, 4 * nt), A(GE, 4 * nt), ACT.Exp).then_inc(self.act_done.up(), 1)
                act.wait_ge(self.dve_done.sem, self.dve_done.at(2))
                nc.scalar.activation(A(V, nt), A(V, nt), ACT.Exp).then_inc(self.act_done.up(), 1)
                act.wait_ge(self.pool_done.sem, self.pool_done.at(1))
                nc.scalar.activation(part(1), A(Z, D * nt), ACT.Copy).then_inc(self.act_done.up(), 1)

            @block.tensor
            def _(pe):
                pe.wait_ge(self.params_in.sem, self.params_in.at(64))
                for t in range(nt):
                    for k in range(KT):
                        mm = nc.tensor.matmul(self.bank[t][:, 0:36], tok(t, k), A(WR + 36 * k, 36), start=(k == 0), stop=(k == KT - 1))
                    mm.then_inc(self.pe_done.up(), 1)
                pe.wait_ge(self.dve_done.sem, self.dve_done.at(3))
                for t in range(nt + 1):
                    for u in range(min(t, nt - 1) + 1):
                        mm = nc.tensor.matmul(self.bank[4][:, NE * t:NE * (t + 1)], self.before if u == t else self.ones,
                                              A(M + NE * u, NE), start=(u == 0), stop=(u == min(t, nt - 1)))
                mm.then_inc(self.pe_done.up(), 1)

            @block.vector
            def _(dve):
                link = self.linker(dve, self.dve_chain)
                V_ = nc.vector
                dve.wait_ge(self.params_in.sem, self.params_in.at(64))
                V_.memset(A(GL, 8 * nt), -3.0e38)
                for t in range(nt):
                    dve.wait_ge(self.pe_done.sem, self.pe_done.at(t + 1))
                    ins = V_.tensor_tensor(A(L + 36 * t, 36), self.bank[t][:, 0:36], A(BL, 36), ALU.add)
                link(ins)
                link(V_.tensor_copy(dims(A(GL, 1), [8, nt], [1, NG]), dims(A(L, 1), [36, nt], [1, NG])))
                for t in range(nt):
                    ins = V_.max(A(GM + 8 * t, 8), A(GL + 8 * t, 8))
                link(ins)
                for t in range(nt):
                    ins = V_.max_index(A(GI + 8 * t, 8).bitcast(U32), A(GM + 8 * t, 8), A(GL + 8 * t, 8))
                link(ins)
                V_.tensor_tensor(dims(A(GE, 1), [4, nt], [1, NG]), dims(A(L, 1), [36, nt], [1, NG]),
                                 dims(A(GM, 1), [8, nt], [0, NG]), ALU.subtract).then_inc(self.dve_done.up(), 1)
                link(V_.tensor_copy(A(GF, 8 * nt), A(GI, 8 * nt).bitcast(U32)))
                link(V_.tensor_tensor(dims(A(GI, 1), [4, nt], [1, NG]), dims(self.iota, [0, nt], [1, NG]),
                                      dims(A(GF, 1), [8, nt], [0, NG]), ALU.is_equal))
                for t in range(nt):
                    ins = V_.tensor_tensor(dims(A(TMP + 32 * t, 1), [4, EPG], [1, NG]), dims(A(L + 36 * t + NG, 1), [1, EPG], [EPG, NG]),
                                           dims(A(GI + 4 * t, 1), [0, EPG], [1, NG]), ALU.mult)
                link(ins)
                link(V_.tensor_reduce(A(ES, 8 * nt), dims(A(TMP, 1), [4, 8 * nt], [1, NG]), X, ALU.add))
                for t in range(nt):
                    ins = V_.max(A(EM + 8 * t, 8), A(ES + 8 * t, 8))
                link(ins)
                for t in range(nt):
                    ins = V_.max_index(A(EI + 8 * t, 8).bitcast(U32), A(EM + 8 * t, 8), A(ES + 8 * t, 8))
                link(ins)
                V_.tensor_tensor(A(V, nt), dims(A(EM + 1, 1), [8, nt]), dims(A(EM, 1), [8, nt]), ALU.subtract).then_inc(self.dve_done.up(), 1)
                link(V_.tensor_copy(A(EF, 8 * nt), A(EI, 8 * nt).bitcast(U32)))
                for r in range(2):
                    ins = V_.tensor_tensor(dims(A(ES + 64 * r, 1), [8, nt], [1, EPG]), dims(self.iota, [0, nt], [1, EPG]),
                                           dims(A(EF + r, 1), [8, nt], [0, EPG]), ALU.is_equal)
                link(ins)
                link(V_.tensor_tensor(A(EM, 8 * nt), A(ES, 8 * nt), A(ES + 64, 8 * nt), ALU.add))
                for t in range(nt):
                    ins = V_.tensor_tensor(dims(A(M + NE * t, 1), [EPG, NG], [1, EPG]), dims(A(GI + 4 * t, 1), [1, NG], [0, EPG]),
                                           dims(A(EM + 8 * t, 1), [0, NG], [1, EPG]), ALU.mult)
                ins.then_inc(self.dve_done.up(), 1)
                dve.wait_ge(self.act_done.sem, self.act_done.at(3))
                V_.tensor_reduce(A(C1, nt), dims(A(GE, 1), [4, nt], [1, NG]), X, ALU.add)
                link(V_.tensor_scalar(A(C1 + 8, nt), A(V, nt), 1.0, None, ALU.add))
                link(V_.tensor_tensor(A(C1, nt), A(C1, nt), A(C1 + 8, nt), ALU.mult))
                link(V_.reciprocal(A(C1, nt), A(C1, nt)))
                link(V_.tensor_tensor(A(C1 + 8, nt), A(C1, nt), A(V, nt), ALU.mult))
                for t in range(nt):
                    ins = V_.tensor_scalar(A(EF + 8 * t, 8), A(ES + 8 * t, 8), A(C1 + t, 1), None, ALU.mult)
                link(ins)
                for t in range(nt):
                    ins = V_.scalar_tensor_tensor(A(EF + 8 * t, 8), A(ES + 64 + 8 * t, 8), A(C1 + 8 + t, 1), A(EF + 8 * t, 8), ALU.mult, ALU.add)
                link(ins)
                V_.memset(A(WT, 34 * nt), 0.0)
                link(V_.memset(A(RS, 34 * nt), -1.0))
                for t in range(nt):
                    ins = V_.tensor_tensor(dims(A(WT + t, 1), [EPG * nt, NG], [nt, EPG]), dims(A(GI + 4 * t, 1), [1, NG], [0, EPG]),
                                           dims(A(EF + 8 * t, 1), [0, NG], [1, EPG]), ALU.mult)
                dve.wait_ge(self.pe_done.sem, self.pe_done.at(nt + 1))
                for t in range(nt):
                    ins = V_.scalar_tensor_tensor(dims(A(RS + t, 1), [nt, NE]), self.bank[4][:, NE * t:NE * (t + 1)], 1.0,
                                                  A(M + NE * t, NE), ALU.add, ALU.mult)
                link(ins)
                link(V_.tensor_scalar(A(RS, NE * nt), A(RS, NE * nt), 1.0, None, ALU.subtract))
                self.overflow_tables(link, nt)

        self.experts(layer, nt, part)
        self.overflow(layer, nt)
        self.st_add_norm(y_t, nt, 5, I["ln2_g"][layer], I["ln2_b"][layer], A(YS, 2048))

    def experts(self, layer, nt, part):
        nc, A, bank, sm = self.nc, self.A, self.bank, self.sem
        YS, Q, PW, PK, XS, SG, HH, HT, RS, WT = MOE_BUFFERS
        Y = 0
        PAIRS = NE // 2
        start = self.used
        pk = lambda i: A(PK + 128 * i, 128).bitcast(BF16)[:, 0:S * nt]
        by_tile = lambda ap: ap.rearrange("p (t s) -> p t s", t=nt)

        def per_turn(name, n):
            sm[name].up(n * PAIRS)
            return sm[name].sem, sm[name].base

        def pick(e, i):
            return nc.vector.tensor_tensor(by_tile(pk(i)), dims(self.iota, [0, nt], [1, S]),
                                           dims(A(RS, 34 * nt)[:, bass.ds(e * nt, nt)], [1, nt], [0, S]), ALU.is_equal)

        def gather_pair():
            for i in range(2):
                mm = self.gather_slots(nt, part, pk(i), bank[2 + i])
            return mm

        def take_tokens():
            for i in range(2):
                ins = nc.scalar.activation(A(XS + 512 * i, 512), bank[2 + i][:, :], ACT.Copy)
            return ins

        with self.stage() as block:
            @block.vector
            def _(dve):
                dve.wait_ge(self.pool_done.sem, self.pool_done.total)
                nc.vector.memset(A(Y, D * nt), 0.0)
                nc.vector.memset(A(YS, D), 0.0).then_inc(sm["ys_ready"].up(), 1)
                nc.vector.memset(A(Q, 512), 0.0).then_inc(sm["turn_out"].up(), 1)
                pick(0, 0)
                pick(1, 1).then_inc(sm["pick_ready"].up(), 1)

            @block.tensor
            def _(pe):
                pe.wait_ge(sm["pick_ready"].sem, sm["pick_ready"].at(1))
                gather_pair().then_inc(sm["gather_done"].up(), 1)

            @block.scalar
            def _(act):
                act.wait_ge(sm["gather_done"].sem, sm["gather_done"].at(1))
                take_tokens().then_inc(sm["xs_ready"].up(), 1)

        with self.stage() as block:
            pieces_used, b_pu = per_turn("pieces_used", 6)
            gather_done, b_ga = per_turn("gather_done", 1)
            h_turned, b_ht = per_turn("h_turned", 1)
            hT_ready, b_hT = per_turn("hT_ready", 1)
            turned, b_tu = per_turn("turned", 1)
            sum_done, b_su = per_turn("sum_done", 2 * nt)
            xs_ready, b_xs = per_turn("xs_ready", 1)
            silu_done, b_si = per_turn("silu_done", 1)
            ys_ready, b_ys = per_turn("ys_ready", 1)
            h_ready, b_h = per_turn("h_ready", 1)
            pick_ready, b_pk = per_turn("pick_ready", 1)
            weigh_ready, b_we = per_turn("weigh_ready", 1)
            turn_out, b_to = per_turn("turn_out", 1)
            added, b_ad = per_turn("added", 2 * nt)
            slot_of = lambda m: self.ring[:, (start + m) % R * SLOT:((start + m) % R + 1) * SLOT]

            @block.sync
            def _(sp):
                def load(p, m, sources):
                    src, k, n = sources[m % 12]
                    if m % 2 == 0:
                        sp.wait_ge(pieces_used, p * 6 + (b_pu + (m - R) // 2 + 1))
                    sp.dma_start(slot_of(m).rearrange("p (k n) -> p k n", k=k), src).then_inc(self.loaded[(start + m) % R], 16)

                assert self.sent == start + R and R == 6
                with sp.Fori(0, PAIRS - 1) as p:
                    now, later = self.pair_sources(layer, p), self.pair_sources(layer, p + 1)
                    for m in range(6, 12):
                        load(p, m, now)
                    for m in range(12, 18):
                        load(p, m, later)
                last = self.pair_sources(layer, PAIRS - 1)
                for m in range(6, 12):
                    src, k, n = last[m]
                    sp.wait_ge(pieces_used, 6 * (PAIRS - 1) + b_pu + (m - R) // 2 + 1)
                    sp.dma_start(slot_of(m).rearrange("p (k n) -> p k n", k=k), src).then_inc(self.loaded[(start + m) % R], 16)
                    self.freed[start + 12 * (PAIRS - 1) + m] = (pieces_used, 6 * (PAIRS - 1) + b_pu + m // 2 + 1)
                self.sent = self.used = start + 12 * PAIRS
                self.feed(sp, self.used + R)

            @block.tensor
            def _(pe):
                def arrived(p, m):
                    w = start + m
                    pe.wait_ge(self.loaded[w % R], p * 32 + 16 * (w // R + 1))

                with pe.Fori(0, PAIRS) as p:
                    pe.wait_ge(xs_ready, p + b_xs)
                    for j in range(4):
                        if j == 2:
                            pe.wait_ge(turn_out, p + b_to)
                            pe.wait_ge(ys_ready, p + b_ys)
                            for n in range(2 * nt):
                                if n >= 2:
                                    pe.wait_ge(added, p * (2 * nt) + (b_ad + n - 1))
                                nc.tensor.matmul(bank[6 + n % 2][:, :], A(Q + n // 2 * P, P), A(YS + n % 2 * 512, 512),
                                                 start=True, stop=True).then_inc(sum_done, 1)
                        arrived(p, 2 * j)
                        arrived(p, 2 * j + 1)
                        for k in range(4):
                            for i in range(2):
                                mm = self.gateup_tile(i, j, k, slot_of(2 * j + 1 - i), A(XS + 512 * i, 512))
                        mm.then_inc(pieces_used, 1)
                    pe.wait_ge(weigh_ready, p + (b_we + 1))
                    pe.wait_ge(added, p * (2 * nt) + (b_ad + 2 * nt))
                    for t in range(nt):
                        mm = nc.tensor.transpose(bank[6][:, t * P:(t + 1) * P], A(PW + t * P, P), self.ident)
                    mm.then_inc(turned, 1)
                    pe.wait_ge(pick_ready, p + (b_pk + 1))
                    gather_pair().then_inc(gather_done, 1)
                    pe.wait_ge(h_ready, p + (b_h + 1))
                    for f in range(4):
                        mm = nc.tensor.transpose(bank[0][:, f * P:(f + 1) * P], A(HH + f * P, P), self.ident)
                    mm.then_inc(h_turned, 1)
                    pe.wait_ge(hT_ready, p + (b_hT + 1))
                    for j in range(2):
                        arrived(p, 8 + 2 * j)
                        arrived(p, 9 + 2 * j)
                        for half in range(2):
                            for f in range(2):
                                for i in range(2):
                                    w = slot_of(9 + 2 * j - i).rearrange("p (k n) -> p k n", k=2)
                                    mm = nc.tensor.matmul(bank[4 + half][64 * i:64 * i + 64, :], A(HT + P * (2 * j + f) + S * i, S),
                                                          w[:, f, half * 512:(half + 1) * 512], start=(j == 0 and f == 0),
                                                          stop=(j == 1 and f == 1))
                        mm.then_inc(pieces_used, 1)

            @block.scalar
            def _(act):
                with act.Fori(0, PAIRS) as p:
                    act.wait_ge(pieces_used, p * 6 + (b_pu + 4))
                    nc.scalar.activation(A(SG, 512), bank[0][:, :], ACT.Silu).then_inc(silu_done, 1)
                    act.wait_ge(h_turned, p + (b_ht + 1))
                    nc.scalar.activation(A(HT, 512), bank[0][:, :], ACT.Copy).then_inc(hT_ready, 1)
                    act.wait_ge(gather_done, p + (b_ga + 1))
                    take_tokens().then_inc(xs_ready, 1)
                    act.wait_ge(pieces_used, p * 6 + (b_pu + 6))
                    for half in range(2):
                        ins = nc.scalar.activation(A(YS + half * 512, 512), bank[4 + half][:, :], ACT.Copy)
                    ins.then_inc(ys_ready, 1)

            @block.vector
            def _(dve):
                with dve.Fori(0, PAIRS) as p:
                    dve.wait_ge(pick_ready, p + b_pk)
                    for i in range(2):
                        ins = nc.vector.tensor_tensor(dims(A(PW + S * i, 1), [P, nt], [1, S]), by_tile(pk(i)),
                                                      dims(A(WT, 34 * nt)[:, bass.ds((2 * p + i) * nt, nt)], [1, nt], [0, S]), ALU.mult)
                    ins.then_inc(weigh_ready, 1)
                    dve.wait_ge(gather_done, p + b_ga)
                    dve.wait_ge(weigh_ready, p + (b_we + 1))
                    pick(2 * p + 2, 0)
                    pick(2 * p + 3, 1).then_inc(pick_ready, 1)
                    for n in range(2 * nt):
                        dve.wait_ge(sum_done, p * (2 * nt) + (b_su + n + 1))
                        y = A(Y + n * 512, 512)
                        nc.vector.tensor_tensor(y, y, bank[6 + n % 2][:, :], ALU.add).then_inc(added, 1)
                    dve.wait_ge(turned, p + (b_tu + 1))
                    nc.vector.tensor_copy(A(Q, P * nt), bank[6][:, 0:P * nt]).then_inc(turn_out, 1)
                    dve.wait_ge(silu_done, p + (b_si + 1))
                    nc.vector.tensor_tensor(A(HH, 512), A(SG, 512), bank[1][:, :], ALU.mult).then_inc(h_ready, 1)

        with self.stage() as block:
            @block.tensor
            def _(pe):
                for n in range(2 * nt):
                    nc.tensor.matmul(bank[n][:, :], A(Q + n // 2 * P, P), A(YS + n % 2 * 512, 512),
                                     start=True, stop=True).then_inc(self.pe_done.up(), 1)

            @block.vector
            def _(dve):
                for n in range(2 * nt):
                    dve.wait_ge(self.pe_done.sem, self.pe_done.at(n + 1))
                    y = A(Y + n * 512, 512)
                    nc.vector.tensor_tensor(y, y, bank[n][:, :], ALU.add)

    def overflow_tables(self, link, nt):
        nc, A, V_ = self.nc, self.A, self.nc.vector
        n_ob = self.n_overflow(nt)
        CNT, NB, CUM, EID, OFF, FIN = [self.OV + 32 * i for i in range(6)]
        IND = OVW
        assert FIN + 48 <= OVW
        link(V_.tensor_copy(A(CNT, NE), self.bank[4][:, NE * nt:NE * (nt + 1)]))
        for k in range(1, nt * P // S):
            link(V_.tensor_scalar(A(NB, NE), A(CNT, NE), float(S * k), None, ALU.is_gt) if k == 1 else
                 V_.scalar_tensor_tensor(A(NB, NE), A(CNT, NE), float(S * k), A(NB, NE), ALU.is_gt, ALU.add))
        link(V_.tensor_tensor_scan(A(CUM, NE), self.ones[:, 0:NE], A(NB, NE), 0.0, ALU.mult, ALU.add))
        link(V_.tensor_tensor(dims(A(IND, 1), [NE, n_ob], [1, NE]), dims(A(CUM, 1), [0, n_ob], [1, NE]),
                              dims(self.iota, [1, n_ob], [0, NE]), ALU.is_le))
        link(V_.tensor_reduce(A(EID, n_ob), dims(A(IND, 1), [NE, n_ob], [1, NE]), AX_X, ALU.add))
        link(V_.tensor_tensor(dims(A(IND, 1), [NE, n_ob], [1, NE]), dims(A(IND, 1), [NE, n_ob], [1, NE]),
                              dims(A(NB, 1), [0, n_ob], [1, NE]), ALU.mult))
        link(V_.tensor_reduce(A(OFF, n_ob), dims(A(IND, 1), [NE, n_ob], [1, NE]), AX_X, ALU.add))
        link(V_.tensor_tensor(A(OFF, n_ob), self.iota[:, 0:n_ob], A(OFF, n_ob), ALU.subtract))
        V_.tensor_scalar(A(OFF, n_ob), A(OFF, n_ob), 1.0, float(S), ALU.add, ALU.mult)
        V_.tensor_copy(A(FIN, 1).bitcast(I32), A(CUM + NE - 1, 1))
        V_.tensor_copy(A(FIN + 1, n_ob).bitcast(I32), A(EID, n_ob))
        self.OFF, self.FIN = OFF, FIN

    def n_overflow(self, nt):
        return 2 * nt * P // (S + 1)

    def overflow(self, layer, nt):
        nc, A, bank = self.nc, self.A, self.bank
        YS, Q, PW, PK, XS, SG, HH, HT, RS, WT = MOE_BUFFERS
        Y, pick = 0, A(PK, 128).bitcast(BF16)[:, 0:S * nt]
        part = lambda i: A(ZP + 2048 * i, nt * 512).bitcast(BF16)
        OFF, FIN, n_ob = self.OFF, self.FIN, self.n_overflow(nt)
        PE_COUNTS = 6 + 2 * nt
        ld, pe_ov, act_ov, dve_ov, slots_free = self.ov[layer]
        piece = lambda j: A(OVW + j % 4 * SLOT, SLOT) if j % 4 < 2 else self.actT[:, (j % 4 - 2) * SLOT:(j % 4 - 1) * SLOT]
        rank = lambda e: dims(A(RS, 34 * nt)[:, bass.ds(e * nt, nt)], [1, nt])

        def blocks(eng):
            return eng.value_load(A(FIN, 1)[0:1, :].bitcast(I32), min_val=0, max_val=n_ob)

        def expert(eng, ob):
            return eng.value_load(A(FIN + 1, n_ob)[0:1, bass.ds(ob, 1)].bitcast(I32), min_val=0, max_val=NE - 1)

        with self.stage() as block:
            @block.sync
            def _(sp):
                there = blocks(sp)
                with sp.Fori(0, n_ob) as ob:
                    with sp.If(there > ob):
                        e = expert(sp, ob)
                        for j, (src, k, n) in enumerate(self.expert_sources(layer, e)):
                            if j == 0:
                                sp.wait_ge(slots_free, ob + 1)
                            if j == 4:
                                sp.wait_ge(pe_ov, ob * PE_COUNTS + 2)
                            sp.dma_start(piece(j).rearrange("p (k n) -> p k n", k=k), src).then_inc(ld[j], 16)

            @block.vector
            def _(dve):
                there = blocks(dve)
                nc.vector.memset(A(PW, P * nt), 0.0).then_inc(slots_free, 1)
                with dve.Fori(0, n_ob) as ob:
                    with dve.If(there > ob):
                        e = expert(dve, ob)
                        nc.vector.tensor_tensor(A(PK + 128, nt), rank(e), dims(A(OFF, n_ob)[:, bass.ds(ob, 1)], [0, nt]),
                                                ALU.subtract).then_inc(dve_ov, 1)
                        dve.wait_ge(dve_ov, ob * 4 + 1)
                        nc.vector.tensor_tensor(pick.rearrange("p (t s) -> p t s", t=nt), dims(self.iota, [0, nt], [1, S]),
                                                dims(A(PK + 128, nt), [1, nt], [0, S]), ALU.is_equal).then_inc(dve_ov, 1)
                        dve.wait_ge(dve_ov, ob * 4 + 2)
                        nc.vector.tensor_tensor(dims(A(PW, 1), [P, nt], [1, S]), pick.rearrange("p (t s) -> p t s", t=nt),
                                                dims(A(WT, 34 * nt)[:, bass.ds(e * nt, nt)], [1, nt], [0, S]), ALU.mult).then_inc(dve_ov, 1)
                        dve.wait_ge(act_ov, ob * 4 + 2)
                        nc.vector.tensor_tensor(self.arena[0:64, HH:HH + 512], self.arena[0:64, SG:SG + 512], bank[1][0:64, :], ALU.mult).then_inc(dve_ov, 1)
                        for n in range(2 * nt):
                            dve.wait_ge(pe_ov, ob * PE_COUNTS + (7 + n))
                            y = A(Y + n * 512, 512)
                            nc.vector.tensor_tensor(y, y, bank[n][:, :], ALU.add)

            @block.scalar
            def _(act):
                there = blocks(act)
                with act.Fori(0, n_ob) as ob:
                    with act.If(there > ob):
                        act.wait_ge(pe_ov, ob * PE_COUNTS + 1)
                        nc.scalar.activation(A(XS, 512), bank[2][:, :], ACT.Copy).then_inc(act_ov, 1)
                        act.wait_ge(pe_ov, ob * PE_COUNTS + 3)
                        nc.scalar.activation(self.arena[0:64, SG:SG + 512], bank[0][0:64, :], ACT.Silu).then_inc(act_ov, 1)
                        act.wait_ge(pe_ov, ob * PE_COUNTS + 4)
                        nc.scalar.activation(A(Q, P * nt), bank[6][:, 0:P * nt], ACT.Copy)
                        act.wait_ge(pe_ov, ob * PE_COUNTS + 5)
                        nc.scalar.activation(A(HT, 256).rearrange("p (f s) -> p f s", f=4), dims(bank[3][:, 0:], [P, 4], [1, S]),
                                             ACT.Copy).then_inc(act_ov, 1)
                        act.wait_ge(pe_ov, ob * PE_COUNTS + 6)
                        for half, sem in enumerate((slots_free, act_ov)):
                            nc.scalar.activation(self.arena[0:64, YS + half * 512:YS + half * 512 + 512], bank[4 + half][0:64, :],
                                                 ACT.Copy).then_inc(sem, 1)

            @block.tensor
            def _(pe):
                there = blocks(pe)
                with pe.Fori(0, n_ob) as ob:
                    with pe.If(there > ob):
                        pe.wait_ge(dve_ov, ob * 4 + 2)
                        self.gather_slots(nt, part, pick, bank[2]).then_inc(pe_ov, 1)
                        pe.wait_ge(act_ov, ob * 4 + 1)
                        for j in range(4):
                            pe.wait_ge(ld[j], ob * 16 + 16)
                            for k in range(4):
                                mm = self.gateup_tile(0, j, k, piece(j), A(XS, 512))
                            if j % 2 == 1:
                                mm.then_inc(pe_ov, 1)
                        pe.wait_ge(dve_ov, ob * 4 + 3)
                        for t in range(nt):
                            mm = nc.tensor.transpose(bank[6][:, t * P:(t + 1) * P], A(PW + t * P, P), self.ident)
                        mm.then_inc(pe_ov, 1)
                        pe.wait_ge(dve_ov, ob * 4 + 4)
                        for f in range(4):
                            mm = nc.tensor.transpose(bank[3][:, f * P:(f + 1) * P], A(HH + f * P, P), self.ident)
                        mm.then_inc(pe_ov, 1)
                        pe.wait_ge(act_ov, ob * 4 + 3)
                        for j in range(2):
                            pe.wait_ge(ld[4 + j], ob * 16 + 16)
                            w = piece(4 + j).rearrange("p (k n) -> p k n", k=2)
                            for half in range(2):
                                for f in range(2):
                                    mm = nc.tensor.matmul(bank[4 + half][0:64, :], A(HT + S * (2 * j + f), S), w[:, f, half * 512:(half + 1) * 512],
                                                          start=(j == 0 and f == 0), stop=(j == 1 and f == 1))
                        mm.then_inc(pe_ov, 1)
                        pe.wait_ge(act_ov, ob * 4 + 4)
                        for n in range(2 * nt):
                            nc.tensor.matmul(bank[n][:, :], A(Q + n // 2 * P, P), A(YS + n % 2 * 512, 512),
                                             start=True, stop=True).then_inc(pe_ov, 1)

    def gather_slots(self, nt, part, pick, bank):
        for k in range(KT):
            for n in range(3 * nt):
                i, t = n % 3, n // 3
                mm = self.nc.tensor.matmul(bank[:, S * k:S * (k + 1)], part(i)[:, t * D + k * P:t * D + (k + 1) * P],
                                           pick[:, S * t:S * (t + 1)], start=(n == 0), stop=(n == 3 * nt - 1))
        return mm

    def gateup_tile(self, i, j, k, piece, xs):
        kt = 4 * (j % 2) + k
        return self.nc.tensor.matmul(self.bank[j // 2][64 * i:64 * i + 64, :], xs[:, S * kt:S * kt + S],
                                     piece[:, k * DE:(k + 1) * DE], start=(kt == 0), stop=(kt == KT - 1))

    def st_attention(self, n, ncomp, operands, value, scale, dv, out_at, P0, lam=None):
        nc, A, sm, bank = self.nc, self.A, self.sem, self.bank
        score_done, max_done, exp_done, mix_done, turned, aT_ready, o_done, o_out = (
            sm[k] for k in ("score_done", "max_done", "exp_done", "mix_done", "turned", "aT_ready", "o_done", "o_out"))
        prob = lambda i, c: A(P0 + (i % 2) * 1024 + c * 512, 512)
        mixed = lambda i: A(P0 + 2048 + (i % 2) * 512, 512)
        aT = lambda i: A(P0 + 3072 + (i % 2) * 512, 512)
        small = lambda i, k: self.stat[:, 16 * (i % 2) + k:16 * (i % 2) + k + 1]
        MAX, SUM, REC, LAMREC = 0, 4, 8, 12
        source = (lambda i: mixed(i)) if ncomp == 2 else (lambda i: prob(i, 0))

        with self.stage() as block:
            @block.tensor
            def _(pe):
                def scores(i):
                    if i >= 2:
                        pe.wait_ge(exp_done.sem, exp_done.at(i - 1))
                    for c in range(ncomp):
                        q, k = operands(i, c)
                        mm = nc.tensor.matmul(bank[2 * (i % 2) + c][:, :], q, k, start=True, stop=True)
                    mm.then_inc(score_done.up(), 1)

                def turn(i):
                    pe.wait_ge(mix_done.sem, mix_done.at(i + 1))
                    if i >= 2:
                        pe.wait_ge(aT_ready.sem, aT_ready.at(i - 1))
                    for j in range(4):
                        mm = nc.tensor.transpose(bank[4 + i % 2][:, j * P:(j + 1) * P], source(i)[:, j * P:(j + 1) * P], self.ident)
                    mm.then_inc(turned.up(), 1)

                def values(i):
                    pe.wait_ge(aT_ready.sem, aT_ready.at(i + 1))
                    if i >= 2:
                        pe.wait_ge(o_out.sem, o_out.at(i - 1))
                    for j in range(4):
                        mm = nc.tensor.matmul(bank[6 + i % 2][:, 0:dv], aT(i)[:, j * P:(j + 1) * P], value(i, j),
                                              start=(j == 0), stop=(j == 3))
                    mm.then_inc(o_done.up(), 1)

                scores(0)
                scores(1)
                for i in range(n):
                    turn(i)
                    if i >= 1:
                        values(i - 1)
                    if i + 2 < n:
                        scores(i + 2)
                values(n - 1)

            @block.vector
            def _(dve):
                link = self.linker(dve, self.dve_chain)

                def maxima(i):
                    dve.wait_ge(score_done.sem, score_done.at(i + 1))
                    if i >= 2:
                        dve.wait_ge(exp_done.sem, exp_done.at(i - 1))
                    for c in range(ncomp):
                        ins = nc.vector.tensor_reduce(small(i, MAX + c), bank[2 * (i % 2) + c][:, :], AX_X, ALU.max, negate=True)
                    link(ins)
                    nc.vector.tensor_scalar(dims(small(i, MAX), [1, ncomp]), dims(small(i, MAX), [1, ncomp]), scale, None,
                                            ALU.mult).then_inc(max_done.up(), 1)

                def mix(i):
                    dve.wait_ge(exp_done.sem, exp_done.at(i + 1))
                    if i >= 2:
                        dve.wait_ge(turned.sem, turned.at(i - 1))
                        dve.wait_ge(o_out.sem, o_out.at(i - 1))
                    rec = nc.vector.reciprocal(dims(small(i, REC), [1, ncomp]), dims(small(i, SUM), [1, ncomp]))
                    if ncomp == 1:
                        rec.then_inc(mix_done.up(), 1)
                        return
                    link(rec)
                    link(nc.vector.tensor_tensor(small(i, LAMREC), small(i, REC + 1), lam(i), ALU.mult))
                    link(nc.vector.tensor_scalar(mixed(i), prob(i, 1), small(i, LAMREC), None, ALU.mult))
                    nc.vector.scalar_tensor_tensor(mixed(i), prob(i, 0), small(i, REC), mixed(i), ALU.mult,
                                                   ALU.subtract).then_inc(mix_done.up(), 1)

                maxima(0)
                for i in range(n):
                    if i + 1 < n:
                        maxima(i + 1)
                    mix(i)

            @block.scalar
            def _(act):
                def exps(i):
                    act.wait_ge(max_done.sem, max_done.at(i + 1))
                    if i >= 2:
                        act.wait_ge(mix_done.sem, mix_done.at(i - 1))
                        act.wait_ge(turned.sem, turned.at(i - 1))
                    for c in range(ncomp):
                        ins = nc.scalar.activation(prob(i, c), bank[2 * (i % 2) + c][:, :], ACT.Exp, bias=small(i, MAX + c),
                                                   scale=scale, accum_out=small(i, SUM + c))
                    ins.then_inc(exp_done.up(), 1)

                def take_turned(i):
                    act.wait_ge(turned.sem, turned.at(i + 1))
                    if i >= 2:
                        act.wait_ge(o_done.sem, o_done.at(i - 1))
                    nc.scalar.activation(aT(i), bank[4 + i % 2][:, :], ACT.Copy).then_inc(aT_ready.up(), 1)

                def take_out(i):
                    act.wait_ge(o_done.sem, o_done.at(i + 1))
                    nc.scalar.activation(out_at(i), bank[6 + i % 2][:, 0:dv], ACT.Copy,
                                         scale=1.0 if ncomp == 2 else small(i, REC)).then_inc(o_out.up(), 1)

                exps(0)
                for i in range(n):
                    if i + 1 < n:
                        exps(i + 1)
                    take_turned(i)
                    if i >= 1:
                        take_out(i - 1)
                take_out(n - 1)

    def st_unmix(self, buf):
        nc = self.nc
        with self.stage() as block:
            @block.gpsimd
            def _(pool):
                self.load_params(pool, [(buf[64 * (t % 2):64 * (t % 2) + 64, (t // 2) * D:(t // 2 + 1) * D],
                                         self.xres[0:64, t * D:(t + 1) * D]) for t in range(4)])

            @block.vector
            def _(dve):
                dve.wait_ge(self.params_in.sem, self.params_in.at(64))
                nc.vector.tensor_copy(self.xres[:, 0:2 * D], buf)

    def mixer_c(self):
        nc, I, A = self.nc, self.I, self.A
        QR, K, V, QT, KTT, O, XX = 0, 2048, 6144, 10240, 12288, 16384, 18432
        self.st_transpose(lambda t: A(t * D, D), 4, self.put_mixed, self.modulated(lambda t: A(t * D, D), 0))
        self.st_unmix(A(0, 2048))

        def dest(c, t):
            base = (QR, K, V)[c // 2]
            return A(base + t * D + 512 * (c % 2), 512)
        self.st_linear(lambda m, k: self.actT[:, k * T + m * P:k * T + m * P + P],
                       [(2, [0, 1], 512)] * 2 + [(2, [0, 1, 2, 3], 512)] * 4, dest)
        LQ = XX + 2048 + 256
        LAM = LQ + 2048
        with self.stage() as block:
            @block.gpsimd
            def _(pool):
                self.load_params(pool, [(A(XX, 256).rearrange("p (t n) -> p t n", t=2), I["k_rope_c"].rearrange("(t p) n -> p t n", p=P))] +
                                 [(A(LQ + 512 * i, 512), rows_to_all(I[n][0].rearrange("h d -> (h d)"), 512))
                                  for i, n in enumerate(("c_lq1", "c_lk1", "c_lq2", "c_lk2"))])

            @block.vector
            def _(dve):
                link = self.linker(dve, self.dve_chain)
                dve.wait_ge(self.params_in.sem, self.params_in.at(80))
                for base in (QR, K):
                    for t in range(2):
                        link(self.rope(link, A(base + t * D, D), 16, 64, 64, 16, A(XX + 128 * t, 64), A(XX + 128 * t + 64, 64),
                                       A(XX + 256, 2048)))
                for i in range(2):
                    ins = nc.vector.tensor_tensor(A(LQ + 1024 * i, 512), A(LQ + 1024 * i, 512), A(LQ + 1024 * i + 512, 512), ALU.mult)
                link(ins)
                for i in range(2):
                    ins = nc.vector.tensor_reduce(A(LAM + 8 * i, 8), dims(A(LQ + 1024 * i, 1), [64, 8], [1, 64]), AX_X, ALU.add)
                ins.then_inc(self.dve_done.up(), 1)
                dve.wait_ge(self.act_done.sem, self.act_done.at(1))
                nc.vector.scalar_tensor_tensor(A(LAM, 8), A(LAM, 8), LAM_INIT, A(LAM + 8, 8), ALU.add, ALU.subtract)

            @block.scalar
            def _(act):
                act.wait_ge(self.dve_done.sem, self.dve_done.at(1))
                nc.scalar.activation(A(LAM, 16), A(LAM, 16), ACT.Exp).then_inc(self.act_done.up(), 1)

        self.st_transpose(lambda t: A(QR + t * D, D), 2, lambda t, g: dims(A(QT + 4 * g * SEQ + t * P, 1), [SEQ, 4], [1, P]))
        self.st_transpose(lambda t: A(K + t * D, D), 4, lambda t, g: dims(A(KTT + 4 * g * T + t * P, 1), [T, 4], [1, P]))

        def operands(i, c):
            h, t = i // 2, i % 2
            rows = slice(64 * c, 64 * c + 64)
            return (self.arena[rows, QT + h * SEQ + t * P:QT + h * SEQ + (t + 1) * P], self.arena[rows, KTT + h * T:KTT + (h + 1) * T])
        self.st_attention(16, 2, operands, lambda i, j: A(V + j * D + (i // 2) * P, P), 64 ** -0.5, P,
                          lambda i: A(O + (i % 2) * D + (i // 2) * P, P), 0, lambda i: A(LAM + i // 2, 1))
        GN = XX
        with self.stage() as block:
            @block.gpsimd
            def _(pool):
                self.load_params(pool, [(A(GN, D), rows_to_all(I["c_subln_g"][0], D))])
                self.rstd(pool, 16, self.dve_done.at(1))

            @block.vector
            def _(dve):
                link = self.linker(dve, self.dve_chain)
                self.moments(link, lambda i: [A(O + i * P, P)], 16, LN_EPS, False).then_inc(self.dve_done.up(), 1)
                dve.wait_ge(self.params_in.sem, self.params_in.at(16))
                link(nc.vector.tensor_scalar(A(GN, D), A(GN, D), 1.0 - LAM_INIT, None, ALU.mult))
                dve.wait_ge(self.pool_done.sem, self.pool_done.at(1))
                for i in range(16):
                    nc.vector.scalar_tensor_tensor(A(O + i * P, P), A(O + i * P, P), self.stat[:, i:i + 1],
                                                   A(GN + (i % 8) * P, P), ALU.mult, ALU.mult)

        self.st_transpose(lambda t: A(O + t * D, D), 2, self.put_pure)
        self.st_linear(lambda m, k: self.actT[:, k * T + m * P:k * T + m * P + P], [(2, [0, 1], 512)] * 2,
                       lambda c, t: A(t * D + 512 * c, 512))
        self.st_add_norm(lambda t: A(t * D, D), 2, 2, I["ln1_g"][1], I["ln1_b"][1], A(4096, 2048))

    def st_rms_mod(self, src, z, nt, g_row, i_shift, G):
        nc, A = self.nc, self.A
        with self.stage() as block:
            @block.gpsimd
            def _(pool):
                self.load_params(pool, [(A(G, D), rows_to_all(g_row, D))])
                self.rstd(pool, nt, self.dve_done.at(1))

            @block.vector
            def _(dve):
                link = self.linker(dve, self.dve_chain)
                self.moments(link, lambda t: [src(t)[:, 0:512], src(t)[:, 512:D]], nt, RMS_EPS, False).then_inc(self.dve_done.up(), 1)
                dve.wait_ge(self.params_in.sem, self.params_in.at(16))
                dve.wait_ge(self.pool_done.sem, self.pool_done.at(1))
                for t in range(nt):
                    ins = nc.vector.scalar_tensor_tensor(z(t), src(t), self.stat[:, t:t + 1], A(G, D), ALU.mult, ALU.mult)
                link(ins)
                for t in range(nt):
                    ins = nc.vector.scalar_tensor_tensor(z(t), self.mod_row(i_shift + 1), 1.0, z(t), ALU.add, ALU.mult)
                link(ins)
                for t in range(nt):
                    nc.vector.tensor_tensor(z(t), z(t), self.mod_row(i_shift), ALU.add)

    def st_add(self, y, nt, i_gate):
        nc = self.nc
        with self.stage() as block:
            @block.vector
            def _(dve):
                link = self.linker(dve, self.dve_chain)
                for t in range(nt):
                    ins = nc.vector.tensor_tensor(y(t), y(t), self.mod_row(i_gate), ALU.mult)
                link(ins)
                for t in range(nt):
                    nc.vector.tensor_tensor(self.x_tile(t), self.x_tile(t), y(t), ALU.add)

    def st_group_rms(self, rows, G, g_row, width, more=None):
        nc, A = self.nc, self.A
        n = len(rows)
        with self.stage() as block:
            @block.gpsimd
            def _(pool):
                self.load_params(pool, [(A(G, width), rows_to_all(g_row, width))])
                self.rstd(pool, n, self.dve_done.at(1))

            @block.vector
            def _(dve):
                link = self.linker(dve, self.dve_chain)
                self.moments(link, lambda i: [rows[i]], n, RMS_EPS, False).then_inc(self.dve_done.up(), 1)
                dve.wait_ge(self.params_in.sem, self.params_in.at(16))
                dve.wait_ge(self.pool_done.sem, self.pool_done.at(1))
                for i in range(n):
                    nc.vector.scalar_tensor_tensor(rows[i], rows[i], self.stat[:, i:i + 1], A(G, width), ALU.mult, ALU.mult)

    def mixer_mla(self):
        nc, I, A = self.nc, self.I, self.A
        CQ, KV, UF, CQT, CKT, QM, KM, VM = 0, 768, 1920, 2944, 3712, 4736, 6272, 9344
        QT, KTT, FT, O, XX = 11392, 13440, 17536, 19584, 20608
        Z = 0
        with self.stage() as block:
            @block.gpsimd
            def _(pool):
                self.load_params(pool, [(self.arena[0:64, Z + t * D:Z + (t + 1) * D],
                                         self.xres[64 * (t % 2):64 * (t % 2) + 64, (t // 2) * D:(t // 2 + 1) * D]) for t in range(4)] +
                    [(self.arena[64:128, Z:Z + 4 * D].rearrange("p (t d) -> p t d", t=4), I["ctx_2"][0].rearrange("(t p) d -> p t d", p=64))])
                pool.wait_ge(self.params_in.sem, self.params_in.at(80))

        z = lambda t: A(Z + t * D, D)
        self.st_rms_mod(z, z, 4, I["norm1_g_2"][0], 0, 4096)
        self.st_transpose(z, 4, self.put_mixed)
        self.st_linear(lambda m, k: self.actT[:, k * T + m * P:k * T + m * P + P],
                       [(2, [0, 1], 384), (2, [0, 1, 2, 3], 288), (2, [0, 1], 512)],
                       lambda c, t: A((CQ + 384 * t, KV + 288 * t, UF + 512 * t)[c], (384, 288, 512)[c]))
        self.st_group_rms([A(CQ + 384 * t, 384) for t in range(2)], XX, I["a_q_ln_g_2"][0], 384)
        self.st_group_rms([A(KV + 288 * t, 256) for t in range(4)], XX, I["a_kv_ln_g_2"][0], 256)
        self.st_transpose(lambda t: A(CQ + 384 * t, 384), 2, lambda t, g: dims(A(CQT + t * P, 1), [SEQ, 3], [1, P]), nb=3)
        self.st_transpose(lambda t: A(KV + 288 * t, 288), 4, lambda t, g: dims(A(CKT + t * P, 1), [T, 2], [1, P]), nb=2)
        self.st_linear(lambda m, k: A(CQT + k * SEQ + m * P, P), [(1, [0, 1], 384)] * 2, lambda c, t: A(QM + 768 * t + 384 * c, 384))
        self.st_linear(lambda m, k: A(CKT + k * T + m * P, P), [(1, [0, 1, 2, 3], 512)] * 2,
                       lambda c, t: A(XX + 512 * t, 512) if c == 0 else A(VM + 512 * t, 512))
        with self.stage() as block:
            @block.vector
            def _(dve):
                for t in range(4):
                    nc.vector.tensor_copy(dims(A(KM + 768 * t, 1), [96, 8], [1, 64]), dims(A(XX + 512 * t, 1), [64, 8], [1, 64]))
                    nc.vector.tensor_copy(dims(A(KM + 768 * t + 64, 1), [96, 8], [1, 32]), dims(A(KV + 288 * t + 256, 1), [0, 8], [1, 32]))
        self.st_group_rms([A(QM + 96 * i, 96) for i in range(16)], XX, I["a_q_norm_g_2"][0], 96)
        self.st_group_rms([A(KM + 96 * i, 96) for i in range(32)], XX, I["a_k_norm_g_2"][0], 96)
        DT, DC = XX + 1024, XX + 2048
        with self.stage() as block:
            @block.gpsimd
            def _(pool):
                self.load_params(pool, [(A(XX, 128).rearrange("p (t n) -> p t n", t=2), I["k_rope_m"].rearrange("(t p) n -> p t n", p=P)),
                                        (A(DT, 1024), I["k_dft_tok"]), (A(DC, 256), I["k_dft_ch"])])

            @block.vector
            def _(dve):
                link = self.linker(dve, self.dve_chain)
                dve.wait_ge(self.params_in.sem, self.params_in.at(48))
                for base in (QM, KM):
                    for t in range(2):
                        link(self.rope(link, A(base + 768 * t + 64, 704), 8, 96, 32, 16, A(XX + 64 * t, 32), A(XX + 64 * t + 32, 32),
                                       A(XX + 128, 512)))

            @block.tensor
            def _(pe):
                pe.wait_ge(self.params_in.sem, self.params_in.at(48))
                for g in range(4):
                    for t in range(2):
                        mm = nc.tensor.matmul(self.bank[g][:, :], A(UF + 512 * t + g * P, P), A(DT + 512 * t, 512), start=(t == 0), stop=(t == 1))
                    mm.then_inc(self.pe_done.up(), 1)
                for g in range(4):
                    pe.wait_ge(self.act_done.sem, self.act_done.at(g + 1))
                    for n in range(2):
                        mm = nc.tensor.matmul(self.bank[4 + g][:, 0:SEQ], A(DC + n * P, P), A(FT + 512 * g + n * SEQ, SEQ),
                                              start=(n == 0), stop=(n == 1))
                    mm.then_inc(self.pe_done.up(), 1)

            @block.scalar
            def _(act):
                for g in range(4):
                    act.wait_ge(self.pe_done.sem, self.pe_done.at(g + 1))
                    nc.scalar.activation(A(FT + 512 * g, 512), self.bank[g][:, :], ACT.Copy).then_inc(self.act_done.up(), 1)
                for g in range(4):
                    act.wait_ge(self.pe_done.sem, self.pe_done.at(5 + g))
                    nc.scalar.activation(self.actT[:, (4 + g) * T:(4 + g) * T + SEQ], self.bank[4 + g][:, 0:SEQ], ACT.Copy)

        self.st_transpose(lambda t: A(QM + 768 * t, 768), 2, lambda t, g: dims(self.arena[0:96, QT + 4 * g * SEQ + t * P:], [SEQ, 4], [1, P]), bw=96)
        self.st_transpose(lambda t: A(KM + 768 * t, 768), 4, lambda t, g: dims(self.arena[0:96, KTT + 4 * g * T + t * P:], [T, 4], [1, P]), bw=96)

        def operands(i, c):
            h, t = i // 2, i % 2
            return self.arena[0:96, QT + h * SEQ + t * P:QT + h * SEQ + (t + 1) * P], self.arena[0:96, KTT + h * T:KTT + (h + 1) * T]
        self.st_attention(16, 1, operands, lambda i, j: A(VM + 512 * j + 64 * (i // 2), 64), 96 ** -0.5, 64,
                          lambda i: A(O + (i % 2) * 512 + (i // 2) * 64, 64), 0)
        self.st_transpose(lambda t: A(O + t * 512, 512), 2, self.put_pure, nb=4)
        self.st_linear(lambda m, k: self.actT[:, k * T + m * P:k * T + m * P + P], [(2, [0, 1], 512)] * 2,
                       lambda c, t: A(t * D + 512 * c, 512))
        self.st_add(lambda t: A(t * D, D), 2, 2)

    def plan_ffn(self, l):
        I, H = self.I, 256
        n = D_FF // H
        for j in range(n + 1):
            if j < n:
                self.plan_linear(I["ffn_w1_2"][l], j * H, (j + 1) * H, width=H, ks=8)
                self.plan_linear(I["ffn_w3_2"][l], j * H, (j + 1) * H, width=H, ks=8)
            if j >= 1:
                self.plan(I["ffn_w2_2"][l][(j - 1) * H:j * H, :].rearrange("(k p) n -> p k n", p=P), 2, D)

    def ffn(self, l):
        nc, I, A, bank, sm = self.nc, self.I, self.A, self.bank, self.sem
        Z, SG, H, TMP = 0, 2048, 3072, 4096
        z = lambda t: A(Z + t * D, D)
        self.st_rms_mod(self.x_tile, z, 2, I["norm2_g_2"][l], 3, 4096)
        self.st_transpose(z, 2, self.put_pure)
        n = D_FF // 256
        gateup_done, silu_done, h_ready, down_done = (sm[k] for k in ("gateup_done", "silu_done", "h_ready", "down_done"))
        with self.stage() as block:
            @block.tensor
            def _(pe):
                def gateup(j):
                    if j >= 2:
                        pe.wait_ge(h_ready.sem, h_ready.at(j - 1))
                    for which in range(2):
                        self.arrived(pe, self.used)
                        w = self.slot(self.used)
                        for f in range(2):
                            for k in range(KT):
                                mm = nc.tensor.matmul(bank[2 * (j % 2) + which][:, f * SEQ:(f + 1) * SEQ], w[:, k, f * P:(f + 1) * P],
                                                      self.actT[:, k * T:k * T + SEQ], start=(k == 0), stop=(k == KT - 1))
                        c = gateup_done if which else self.weights_used
                        mm.then_inc(c.up(), 1)
                        self.frees(self.used, c)
                        self.used += 1

                def down(j):
                    pe.wait_ge(h_ready.sem, h_ready.at(j + 1))
                    self.arrived(pe, self.used)
                    w = self.slot(self.used)
                    for f in range(2):
                        for t in range(2):
                            for half in range(2):
                                mm = nc.tensor.matmul(bank[4 + 2 * t + half][:, :], A(H + 512 * (j % 2) + f * SEQ + t * P, P),
                                                      w[:, f, half * 512:(half + 1) * 512], start=(j == 0 and f == 0),
                                                      stop=(j == n - 1 and f == 1))
                    mm.then_inc(down_done.up(), 1)
                    self.frees(self.used, down_done)
                    self.used += 1

                gateup(0)
                for j in range(n):
                    if j + 1 < n:
                        gateup(j + 1)
                    down(j)

            @block.sync
            def _(sp):
                self.feed(sp, self.used + R)

            @block.scalar
            def _(act):
                for j in range(n):
                    act.wait_ge(gateup_done.sem, gateup_done.at(j + 1))
                    if j >= 2:
                        act.wait_ge(h_ready.sem, h_ready.at(j - 1))
                    nc.scalar.activation(A(SG + 512 * (j % 2), 512), bank[2 * (j % 2)][:, :], ACT.Silu).then_inc(silu_done.up(), 1)

            @block.vector
            def _(dve):
                link = self.linker(dve, self.dve_chain)
                for j in range(n):
                    dve.wait_ge(silu_done.sem, silu_done.at(j + 1))
                    if j >= 2:
                        dve.wait_ge(down_done.sem, down_done.at(j - 1))
                    nc.vector.tensor_tensor(A(H + 512 * (j % 2), 512), A(SG + 512 * (j % 2), 512), bank[2 * (j % 2) + 1][:, :],
                                            ALU.mult).then_inc(h_ready.up(), 1)
                dve.wait_ge(down_done.sem, down_done.at(n))
                for q in range(4):
                    ins = nc.vector.tensor_tensor(A(TMP + 512 * q, 512), bank[4 + q][:, :], self.mod_row(5)[:, (q % 2) * 512:(q % 2) * 512 + 512], ALU.mult)
                link(ins)
                nc.vector.tensor_tensor(self.xres[:, 0:2 * D], self.xres[:, 0:2 * D], A(TMP, 2048), ALU.add)

    def mixer_conv(self):
        nc, I, A, bank, actT = self.nc, self.I, self.A, self.bank, self.actT
        U, CB, SB_, CV, XC, SQ, RW, PC = 2048, 7168, 8400, 9600, 10624, 11648, 12672, 13200
        z = lambda t: A(t * D, D)
        CW, SW = 288, 260
        self.st_rms_mod(self.x_tile, z, 2, I["norm1_g_2"][1], 0, 4096)
        self.st_transpose(z, 2, self.put_pure)
        rows = [("b_conf_dw_2", 31), ("b_sc_dw_2", 3), ("b_conf_dw_b_2", 1), ("b_conf_ln_g_2", 1), ("b_conf_ln_b_2", 1)]
        with self.stage() as block:
            @block.tensor
            def _(pe):
                for j in range(10):
                    if j >= 6:
                        on_act = (j - 6) % 2 == 0
                        c = self.act_done if on_act else self.dve_done
                        pe.wait_ge(c.sem, c.at((j - 6) // 2 + 1))
                    self.arrived(pe, self.used)
                    w = self.slot(self.used)
                    for f in range(2):
                        for k in range(KT):
                            mm = nc.tensor.matmul(bank[j % 6][:, f * SEQ:(f + 1) * SEQ], w[:, k, f * P:(f + 1) * P],
                                                  actT[:, k * T:k * T + SEQ], start=(k == 0), stop=(k == KT - 1))
                    mm.then_inc(self.pe_done.up(), 1)
                    self.frees(self.used, self.pe_done)
                    self.used += 1
                pe.wait_ge(self.params_in.sem, self.params_in.at(80))
                for c in range(4):
                    mm = nc.tensor.transpose(bank[6][:, 64 * c:64 * c + 37], self.arena[0:37, RW + c * P:RW + (c + 1) * P], self.ident[0:37, 0:37])
                mm.then_inc(self.pe_done.up(), 1)

            @block.sync
            def _(sp):
                self.feed(sp, self.used + R)

            @block.gpsimd
            def _(pool):
                at, pairs = 0, []
                for name, k in rows:
                    src = I[name][0] if k > 1 else I[name]
                    pairs.append((self.arena[at:at + k, RW:RW + 512], src))
                    at += k
                self.load_params(pool, pairs)

            @block.scalar
            def _(act):
                for j in range(0, 10, 2):
                    act.wait_ge(self.pe_done.sem, self.pe_done.at(j + 1))
                    nc.scalar.activation(A(U + 512 * j, 512), bank[j % 6][:, :], ACT.Sigmoid if j == 2 else ACT.Copy).then_inc(self.act_done.up(), 1)
                act.wait_ge(self.dve_done.sem, self.dve_done.at(2))
                nc.scalar.activation(A(U + 512 * 3, 512), A(U + 512 * 3, 512), ACT.Sigmoid)

            @block.vector
            def _(dve):
                for j in range(1, 10, 2):
                    dve.wait_ge(self.pe_done.sem, self.pe_done.at(j + 1))
                    nc.vector.tensor_copy(A(U + 512 * j, 512), bank[j % 6][:, :]).then_inc(self.dve_done.up(), 1)
                dve.wait_ge(self.pe_done.sem, self.pe_done.at(11))
                nc.vector.tensor_copy(dims(A(PC, 1), [40, 4], [1, 37]), dims(bank[6][:, 0:], [64, 4], [1, 37]))

        par = lambda c, i: A(PC + 40 * c + i, 1)
        with self.stage() as block:
            @block.vector
            def _(dve):
                link = self.linker(dve, self.dve_chain)
                V_ = nc.vector
                V_.memset(A(CB, 4 * CW), 0.0)
                link(V_.memset(A(SB_, 4 * SW), 0.0))
                V_.tensor_tensor(dims(A(CB + 15, 1), [CW, 4], [1, SEQ]), dims(A(U, 1), [SEQ, 4], [1, SEQ]),
                                 dims(A(U + 1024, 1), [SEQ, 4], [1, SEQ]), ALU.mult)
                link(V_.tensor_tensor(dims(A(SB_ + 1, 1), [SW, 4], [1, SEQ]), dims(A(U + 3072, 1), [SEQ, 4], [1, SEQ]),
                                      dims(A(U + 4096, 1), [SEQ, 4], [1, SEQ]), ALU.mult))
                for tap in range(31):
                    for c in range(4):
                        acc, x = A(CV + SEQ * c, SEQ), A(CB + CW * c + tap, SEQ)
                        ins = V_.tensor_scalar(acc, x, par(c, 0), par(c, 34), ALU.mult, ALU.add) if tap == 0 else \
                            V_.scalar_tensor_tensor(acc, x, par(c, tap), acc, ALU.mult, ALU.add)
                    link(ins)
                V_.memset(self.stat[:, 0:1], 0.0).then_inc(self.dve_done.up(), 1)
                for tap in range(3):
                    for c in range(4):
                        acc, x = A(SQ + SEQ * c, SEQ), A(SB_ + SW * c + tap, SEQ)
                        ins = V_.tensor_scalar(acc, x, par(c, 31), None, ALU.mult) if tap == 0 else \
                            V_.scalar_tensor_tensor(acc, x, par(c, 31 + tap), acc, ALU.mult, ALU.add)
                    link(ins)
                link(V_.tensor_tensor(dims(actT[:, 4 * T:], [T, 4], [1, SEQ]), dims(A(SQ, 1), [SEQ, 4], [1, SEQ]),
                                      dims(A(U + 2048, 1), [SEQ, 4], [1, SEQ]), ALU.mult))
                dve.wait_ge(self.pe_done.sem, self.pe_done.at(1))
                for b in range(2):
                    ins = V_.tensor_tensor(A(XC + 512 * b, 512), A(CV + 512 * b, 512), bank[b][:, :], ALU.subtract)
                link(ins)
                V_.tensor_tensor(A(SQ, 1024), A(XC, 1024), A(XC, 1024), ALU.mult).then_inc(self.dve_done.up(), 1)
                dve.wait_ge(self.pe_done.sem, self.pe_done.at(2))
                for b in range(2):
                    ins = V_.tensor_scalar(A(CV + 512 * b, 512), bank[2 + b][:, :], RMS_EPS, None, ALU.add)
                ins.then_inc(self.dve_done.up(), 1)
                dve.wait_ge(self.act_done.sem, self.act_done.at(1))
                link(V_.reciprocal(A(CV, 1024), A(CV, 1024)))
                V_.tensor_tensor(A(XC, 1024), A(XC, 1024), A(CV, 1024), ALU.mult).then_inc(self.dve_done.up(), 1)

            @block.tensor
            def _(pe):
                for n, src in enumerate((CV, SQ)):
                    pe.wait_ge(self.dve_done.sem, self.dve_done.at(n + 1))
                    for b in range(2):
                        mm = nc.tensor.matmul(bank[2 * n + b][:, :], self.mean_of, A(src + 512 * b, 512), start=True, stop=True)
                    mm.then_inc(self.pe_done.up(), 1)

            @block.scalar
            def _(act):
                act.wait_ge(self.dve_done.sem, self.dve_done.at(3))
                nc.scalar.activation(A(CV, 1024), A(CV, 1024), ACT.Sqrt).then_inc(self.act_done.up(), 1)
                act.wait_ge(self.dve_done.sem, self.dve_done.at(4))
                for c in range(4):
                    nc.scalar.activation(actT[:, c * T:c * T + SEQ], A(XC + SEQ * c, SEQ), ACT.Silu, bias=par(c, 36), scale=par(c, 35))

        self.st_linear(lambda m, k: actT[:, k * T + m * P:k * T + m * P + P], [(2, [0, 1], 512)] * 2,
                       lambda c, t: A(t * D + 512 * c, 512))
        self.st_add(lambda t: A(t * D, D), 2, 2)

    def run(self):
        I = self.I
        for l in range(2):
            self.plan_linear(I["ada_w"][l], 0, 6 * D)
            if l == 0:
                self.plan_linear(I["ab_w_in"][0], 0, 3584)
                self.plan_linear(I["ab_w_in"][0], 3584, 3616, ks=8)
                self.plan_linear(I["ab_w_out"][0], 0, D)
            else:
                self.plan_linear(I["c_w_qkv"][0], 0, 3 * D)
                self.plan_linear(I["c_w_out"][0], 0, D)
            self.plan_experts(l)
        self.plan_linear(I["ada_w_2"][0], 0, 6 * D)
        w = I["a_w_in_2"][0]
        for lo, hi in ((0, 384), (384, 672), (672, 1184)):
            self.plan_linear(w, lo, hi)
        self.plan_linear(I["a_w_uq_2"][0].rearrange("r h d -> r (h d)"), 0, 768, width=384)
        self.plan_linear(I["a_w_uk_2"][0].rearrange("r h d -> r (h d)"), 0, 512)
        self.plan_linear(I["a_w_uv_2"][0].rearrange("r h d -> r (h d)"), 0, 512)
        self.plan_linear(I["a_w_out_2"][0], 0, D)
        self.plan_ffn(0)
        self.plan_linear(I["ada_w_2"][1], 0, 6 * D)
        self.plan_linear(I["b_w_in_2"][0], 0, 2560, width=256, ks=8)
        self.plan_linear(I["b_w_out_2"][0], 0, D)
        self.plan_ffn(1)

        self.st_setup()
        self.st_ada(12, (0, 1), I["ada_b"][0])
        self.mixer_ab()
        if self.stop("l0mix", 4): return
        self.moe(0, 4)
        if self.stop("l0", 4): return
        self.st_ada(4, (0, 1), I["ada_b"][1])
        self.st_ada(8, (0, 0), I["ada_b"][1], first=4)
        self.mixer_c()
        if self.stop("l1mix", 2): return
        self.moe(1, 2)
        if self.stop("l1", 2): return
        self.st_ada(4, (2, 3), I["ada_b_2"][0])
        self.st_ada(8, (2, 2), I["ada_b_2"][0], first=4)
        self.mixer_mla()
        if self.stop("b2mix", 2): return
        self.ffn(0)
        self.st_ada(12, (2, 2), I["ada_b_2"][1])
        self.mixer_conv()
        if self.stop("b2conv", 2): return
        self.ffn(1)
        self.store(2)
        assert self.used == len(self.W)

    def stop(self, name, nt):
        if self.debug == name:
            self.W = self.W[:self.sent]
            self.store(nt)
            return True

    def store(self, nt):
        nc = self.nc
        with self.stage() as block:
            @block.sync
            def _(sp):
                rows = self.out[0] if not self.debug else self.out
                sp.dma_start(rows.rearrange("(t p) d -> p t d", p=P), self.xres[:, 0:nt * D].rearrange("p (t d) -> p t d", t=nt)).then_inc(self.sem["stored"].up(16), 16)
                sp.wait_ge(self.sem["stored"].sem, self.sem["stored"].at(16))


def kernel(**inputs):
    import concourse.bacc as bacc
    from concourse.bass_utils import run_bass_kernel_spmd

    nc = bacc.Bacc("TRN2", target_bir_lowering=False, num_devices=1)
    arrays = {n: np.ascontiguousarray(a) for n, a in inputs.items()} | constants()
    I = {n: nc.dram_tensor(n, a.shape, mybir.dt.from_np(a.dtype), kind="ExternalInput").ap() for n, a in arrays.items()}
    out = nc.dram_tensor("out", (1, SEQ, D), F32, kind="ExternalOutput").ap()
    build_program(nc, I, out)
    result = run_bass_kernel_spmd(nc, [arrays], core_ids=[0])
    return result.results[0]["out"]
```
